# Optimizing a Trainium2 kernel written in Bass

```python
import math
import jax, jax.numpy as jnp
from jax import lax
import numpy as np

D_MODEL = 2048
BATCH = 1
SEQ = 256
DEPTH = 1

MIX_WIDTH = D_MODEL
SSM_WIDTH = MIX_WIDTH // 2
SSM_GROUP = 16
SSM_GROUPS = SSM_WIDTH // SSM_GROUP
SSM_STATE = 64
DT_MIN = 1e-3
DT_MAX = 1e-1
QK_NOPE_DIM = 128
QK_ROPE_DIM = 64
V_HEAD_DIM = 128
MLA_WIDTH = MIX_WIDTH - SSM_WIDTH
MLA_HEADS = MLA_WIDTH // V_HEAD_DIM
Q_LORA_RANK = D_MODEL // 4
KV_LORA_RANK = D_MODEL // 8
ROPE_THETA = 10000.0
Q_BLOCK = 128
IN_WIDTH = SSM_WIDTH + Q_LORA_RANK + KV_LORA_RANK + QK_ROPE_DIM
D_FF = ((8 * D_MODEL // 3 + 255) // 256) * 256
CONV_WIDTH = 3
RMS_EPS = 1e-6


def _rmsnorm(x, w):
    xf = x.astype(jnp.float32)
    y = xf * lax.rsqrt(jnp.mean(xf * xf, axis=-1, keepdims=True) + RMS_EPS)
    return (y * w.astype(jnp.float32)).astype(x.dtype)

def _rope_tables(positions, dtype):
    inv_freq = ROPE_THETA ** (-jnp.arange(0, QK_ROPE_DIM, 2, dtype=jnp.float32) / QK_ROPE_DIM)
    ang = positions.astype(jnp.float32)[..., None] * inv_freq
    return jnp.cos(ang).astype(dtype), jnp.sin(ang).astype(dtype)

def _rope(x, cos, sin):
    x1, x2 = jnp.split(x, 2, axis=-1)
    return jnp.concatenate([x1 * cos - x2 * sin, x1 * sin + x2 * cos], axis=-1)

def _ssm_combine(left, right):
    ar1, ai1, br1, bi1 = left
    ar2, ai2, br2, bi2 = right
    ar = ar2 * ar1 - ai2 * ai1
    ai = ar2 * ai1 + ai2 * ar1
    br = ar2 * br1 - ai2 * bi1 + br2
    bi = ar2 * bi1 + ai2 * br1 + bi2
    return ar, ai, br, bi

def _s5_group(u, lam_re, lam_im, log_dt, b_re, b_im, c_re, c_im, d_skip, w_glu, b_glu):
    bsz, seq, _ = u.shape
    ug = u.astype(jnp.float32).reshape(bsz, seq, SSM_GROUPS, SSM_GROUP)
    lr = lam_re.astype(jnp.float32)
    li = lam_im.astype(jnp.float32)
    dt = jnp.exp(log_dt.astype(jnp.float32))[:, None]
    mag = jnp.exp(lr * dt)
    abar_re = mag * jnp.cos(li * dt)
    abar_im = mag * jnp.sin(li * dt)
    nr, ni = abar_re - 1.0, abar_im
    den = lr * lr + li * li
    zr = (nr * lr + ni * li) / den
    zi = (ni * lr - nr * li) / den
    bre = b_re.astype(jnp.float32)
    bim = b_im.astype(jnp.float32)
    bbar_re = zr[..., None] * bre - zi[..., None] * bim
    bbar_im = zr[..., None] * bim + zi[..., None] * bre
    bu_re = jnp.einsum('blgh,gph->lbgp', ug, bbar_re)
    bu_im = jnp.einsum('blgh,gph->lbgp', ug, bbar_im)
    a_re = jnp.broadcast_to(abar_re, (seq, 1, SSM_GROUPS, SSM_STATE))
    a_im = jnp.broadcast_to(abar_im, (seq, 1, SSM_GROUPS, SSM_STATE))
    _, _, s_re, s_im = lax.associative_scan(_ssm_combine, (a_re, a_im, bu_re, bu_im), axis=0)
    y = (jnp.einsum('lbgp,ghp->blgh', s_re, c_re.astype(jnp.float32))
         - jnp.einsum('lbgp,ghp->blgh', s_im, c_im.astype(jnp.float32))
         + d_skip.astype(jnp.float32).reshape(SSM_GROUPS, SSM_GROUP) * ug)
    y = jax.nn.gelu(y.reshape(bsz, seq, SSM_WIDTH)).astype(u.dtype)
    return y * jax.nn.sigmoid(y @ w_glu + b_glu)

def _mla_group(c_q, c_kv, k_pe, positions, q_norm_w, w_uq, kv_norm_w, w_ukv):
    bsz, seq, _ = c_q.shape
    q = (_rmsnorm(c_q, q_norm_w) @ w_uq).reshape(bsz, seq, MLA_HEADS, QK_NOPE_DIM + QK_ROPE_DIM)
    q_nope, q_pe = q[..., :QK_NOPE_DIM], q[..., QK_NOPE_DIM:]
    kv = (_rmsnorm(c_kv, kv_norm_w) @ w_ukv).reshape(bsz, seq, MLA_HEADS, QK_NOPE_DIM + V_HEAD_DIM)
    k_nope, v = kv[..., :QK_NOPE_DIM], kv[..., QK_NOPE_DIM:]
    cos, sin = _rope_tables(positions, q.dtype)
    q_pe = _rope(q_pe, cos[:, :, None, :], sin[:, :, None, :])
    k_pe = _rope(k_pe, cos, sin)
    scale = (QK_NOPE_DIM + QK_ROPE_DIM) ** -0.5
    neg = jnp.finfo(jnp.float32).min
    outs = []
    for blk in range(seq // Q_BLOCK):
        q0 = blk * Q_BLOCK
        kend = q0 + Q_BLOCK
        s = (jnp.einsum('bqhd,bkhd->bhqk', q_nope[:, q0:kend], k_nope[:, :kend])
             + jnp.einsum('bqhr,bkr->bhqk', q_pe[:, q0:kend], k_pe[:, :kend]))
        s = s.astype(jnp.float32) * scale
        causal = jnp.arange(kend)[None, :] <= (q0 + jnp.arange(Q_BLOCK))[:, None]
        s = jnp.where(causal, s, neg)
        p = jax.nn.softmax(s, axis=-1).astype(v.dtype)
        outs.append(jnp.einsum('bhqk,bkhd->bqhd', p, v[:, :kend]))
    o = jnp.concatenate(outs, axis=1)
    return o.reshape(bsz, seq, MLA_WIDTH)

def _conv_ffn(h, w_up, conv_w, conv_b, w_down):
    a = h @ w_up
    a = lax.conv_general_dilated(a, conv_w[:, None, :], window_strides=(1,),
                                 padding=[(CONV_WIDTH - 1, 0)],
                                 dimension_numbers=('NWC', 'WIO', 'NWC'),
                                 feature_group_count=2 * D_FF) + conv_b
    gate, val = jnp.split(a, 2, axis=-1)
    return (jax.nn.silu(gate) * val) @ w_down

def first_inputs(seed: int = 0) -> dict:
    key = jax.random.key(seed)
    ks = jax.random.split(key, 32)
    f32 = jnp.float32

    def nrm(k, shape, scale):
        return jax.random.normal(k, (DEPTH,) + shape, f32) * scale

    def gain(k, n):
        return 1.0 + 0.02 * jax.random.normal(k, (DEPTH, n), f32)

    x = jax.random.normal(ks[0], (BATCH, SEQ, D_MODEL), f32)
    offs = jax.random.randint(ks[1], (BATCH, 1), 0, 1024, dtype=jnp.int32)
    positions = offs + jnp.arange(SEQ, dtype=jnp.int32)[None, :]
    lam_re = -0.5 + 0.01 * jax.random.normal(ks[4], (DEPTH, SSM_GROUPS, SSM_STATE), f32)
    lam_im = (math.pi * jnp.arange(SSM_STATE, dtype=f32))[None, None, :] + 0.01 * jax.random.normal(ks[5], (DEPTH, SSM_GROUPS, SSM_STATE), f32)
    log_dt = jax.random.uniform(ks[6], (DEPTH, SSM_GROUPS), f32, math.log(DT_MIN), math.log(DT_MAX))
    return {
        'x': x,
        'positions': positions,
        'attn_norm_w': gain(ks[2], D_MODEL),
        'w_in': nrm(ks[3], (D_MODEL, IN_WIDTH), D_MODEL ** -0.5),
        'ssm_lambda_re': lam_re,
        'ssm_lambda_im': lam_im,
        'ssm_log_dt': log_dt,
        'ssm_b_re': nrm(ks[7], (SSM_GROUPS, SSM_STATE, SSM_GROUP), (2 * SSM_GROUP) ** -0.5),
        'ssm_b_im': nrm(ks[8], (SSM_GROUPS, SSM_STATE, SSM_GROUP), (2 * SSM_GROUP) ** -0.5),
        'ssm_c_re': nrm(ks[9], (SSM_GROUPS, SSM_GROUP, SSM_STATE), (2 * SSM_STATE) ** -0.5),
        'ssm_c_im': nrm(ks[10], (SSM_GROUPS, SSM_GROUP, SSM_STATE), (2 * SSM_STATE) ** -0.5),
        'ssm_d': nrm(ks[11], (SSM_WIDTH,), 1.0),
        'ssm_w_glu': nrm(ks[12], (SSM_WIDTH, SSM_WIDTH), SSM_WIDTH ** -0.5),
        'ssm_b_glu': nrm(ks[13], (SSM_WIDTH,), 0.01),
        'mla_q_norm_w': gain(ks[14], Q_LORA_RANK),
        'mla_w_uq': nrm(ks[15], (Q_LORA_RANK, MLA_HEADS * (QK_NOPE_DIM + QK_ROPE_DIM)), Q_LORA_RANK ** -0.5),
        'mla_kv_norm_w': gain(ks[16], KV_LORA_RANK),
        'mla_w_ukv': nrm(ks[17], (KV_LORA_RANK, MLA_HEADS * (QK_NOPE_DIM + V_HEAD_DIM)), KV_LORA_RANK ** -0.5),
        'ssm_out_norm_w': gain(ks[18], SSM_WIDTH),
        'mla_out_norm_w': gain(ks[19], MLA_WIDTH),
        'w_out': nrm(ks[20], (MIX_WIDTH, D_MODEL), MIX_WIDTH ** -0.5),
        'ffn_norm_w': gain(ks[21], D_MODEL),
        'ffn_w_up': nrm(ks[22], (D_MODEL, 2 * D_FF), D_MODEL ** -0.5),
        'ffn_conv_w': nrm(ks[23], (CONV_WIDTH, 2 * D_FF), CONV_WIDTH ** -0.5),
        'ffn_conv_b': nrm(ks[24], (2 * D_FF,), 0.01),
        'ffn_w_down': nrm(ks[25], (D_FF, D_MODEL), D_FF ** -0.5),
        'final_norm_w': 1.0 + 0.02 * jax.random.normal(ks[26], (D_MODEL,), f32),
    }

def first_block(x, positions, attn_norm_w, w_in, ssm_lambda_re, ssm_lambda_im, ssm_log_dt,
              ssm_b_re, ssm_b_im, ssm_c_re, ssm_c_im, ssm_d, ssm_w_glu, ssm_b_glu,
              mla_q_norm_w, mla_w_uq, mla_kv_norm_w, mla_w_ukv, ssm_out_norm_w,
              mla_out_norm_w, w_out, ffn_norm_w, ffn_w_up, ffn_conv_w, ffn_conv_b,
              ffn_w_down, final_norm_w):
    split_at = [SSM_WIDTH, SSM_WIDTH + Q_LORA_RANK, SSM_WIDTH + Q_LORA_RANK + KV_LORA_RANK]
    h = x
    for l in range(DEPTH):
        hn = _rmsnorm(h, attn_norm_w[l])
        proj = hn @ w_in[l]
        u, c_q, c_kv, k_pe = jnp.split(proj, split_at, axis=-1)
        y_ssm = _s5_group(u, ssm_lambda_re[l], ssm_lambda_im[l], ssm_log_dt[l],
                          ssm_b_re[l], ssm_b_im[l], ssm_c_re[l], ssm_c_im[l],
                          ssm_d[l], ssm_w_glu[l], ssm_b_glu[l])
        y_mla = _mla_group(c_q, c_kv, k_pe, positions, mla_q_norm_w[l], mla_w_uq[l],
                           mla_kv_norm_w[l], mla_w_ukv[l])
        y = jnp.concatenate([_rmsnorm(y_ssm, ssm_out_norm_w[l]),
                             _rmsnorm(y_mla, mla_out_norm_w[l])], axis=-1)
        h = h + y @ w_out[l]
        h = h + _conv_ffn(_rmsnorm(h, ffn_norm_w[l]), ffn_w_up[l], ffn_conv_w[l],
                          ffn_conv_b[l], ffn_w_down[l])
    return _rmsnorm(h, final_norm_w)


_first_inputs = first_inputs


def first_inputs(seed=0):
    import zlib

    import numpy as np

    out = dict(_first_inputs(seed))
    spreads = {}
    factors = {}
    for name, (base, spread) in spreads.items():
        noise = np.random.default_rng([zlib.crc32(name.encode()), seed]).standard_normal(out[name].shape)
        drawn = base * np.exp(spread * noise) if base else spread * noise
        out[name] = __import__('jax').numpy.asarray(drawn.astype(out[name].dtype))
    for name, factor in factors.items():
        out[name] = (out[name] * factor).astype(out[name].dtype)
    return out


_narrow_inputs = first_inputs


def first_inputs(seed=0):
    out = dict(_narrow_inputs(seed))
    wider = {'ssm_lambda_re': 12.0,
     'ssm_b_glu': 12.0,
     'mla_q_norm_w': 6.74,
     'mla_kv_norm_w': 4.09,
     'ssm_out_norm_w': 5.84,
     'mla_out_norm_w': 5.93,
     'ffn_norm_w': 5.41,
     'ffn_conv_b': 11.22,
     'final_norm_w': 3.27}
    for name, times in wider.items():
        mean = out[name].mean()
        out[name] = (mean + times * (out[name] - mean)).astype(out[name].dtype)
    return out


CHUNK = 64
HEAD_DIM = 64
D_SSD = D_MODEL
D_RWKV = D_MODEL
D_MIX = D_SSD + D_RWKV
SSD_HEADS = D_SSD // HEAD_DIM
SSD_GROUPS = 4
SSD_HPG = SSD_HEADS // SSD_GROUPS
SSD_STATE = 128
CONV_WIDTH_2 = 4
D_XBC = D_SSD + 2 * SSD_GROUPS * SSD_STATE
RWKV_HEADS = D_RWKV // HEAD_DIM
DECAY_LORA = 96
AAA_LORA = 96
GATE_LORA = 256
D_RWKV_IN = 3 * D_RWKV + DECAY_LORA + AAA_LORA + GATE_LORA
D_IN = D_SSD + D_XBC + SSD_HEADS + D_RWKV_IN
D_FF_2 = -(-8 * D_MODEL // (3 * 256)) * 256
GATED_NORM_EPS = 1e-5
GN_EPS = 64e-5


def rms_norm(x, g, eps=RMS_EPS):
    xf = x.astype(jnp.float32)
    y = xf * lax.rsqrt(jnp.mean(xf * xf, axis=-1, keepdims=True) + eps)
    return (y * g.astype(jnp.float32)).astype(x.dtype)

def causal_depthwise_conv(u, w, b):
    c = u.shape[-1]
    y = lax.conv_general_dilated(u, w[:, None, :].astype(u.dtype), window_strides=(1,),
                                 padding=((w.shape[0] - 1, 0),),
                                 dimension_numbers=('NWC', 'WIO', 'NWC'),
                                 feature_group_count=c)
    return y + b.astype(u.dtype)

def segsum(a):
    t = a.shape[-1]
    rep = jnp.broadcast_to(a[..., None], a.shape + (t,))
    rep = jnp.where(jnp.tril(jnp.ones((t, t), bool), -1), rep, 0.0)
    cs = jnp.cumsum(rep, axis=-2)
    return jnp.where(jnp.tril(jnp.ones((t, t), bool)), cs, -jnp.inf)

def ssd_chunked(xh, dt, A, Bm, Cm):
    b, s, g, e, p = xh.shape
    n = Bm.shape[-1]
    c = s // CHUNK
    X = (xh * dt[..., None]).reshape(b, c, CHUNK, g, e, p)
    Adt = (dt * A).reshape(b, c, CHUNK, g, e).transpose(0, 3, 4, 1, 2)
    Bc = Bm.reshape(b, c, CHUNK, g, n)
    Cc = Cm.reshape(b, c, CHUNK, g, n)
    A_cs = jnp.cumsum(Adt, axis=-1)
    L = jnp.exp(segsum(Adt))
    CB = jnp.einsum('bclgn,bcsgn->bcgls', Cc, Bc)
    y_diag = jnp.einsum('bcgls,bgecls,bcsgep->bclgep', CB, L, X)
    decay_states = jnp.exp(A_cs[..., -1:] - A_cs)
    states = jnp.einsum('bclgn,bgecl,bclgep->bcgepn', Bc, decay_states, X)
    chunk_decay = jnp.exp(A_cs[..., -1])

    def step(h, inp):
        st, dec = inp
        return h * dec[..., None, None] + st, h

    h0 = jnp.zeros((b, g, e, p, n), X.dtype)
    _, h_in = lax.scan(step, h0, (states.transpose(1, 0, 2, 3, 4, 5), chunk_decay.transpose(3, 0, 1, 2)))
    h_in = h_in.transpose(1, 0, 2, 3, 4, 5)
    y_off = jnp.einsum('bclgn,bcgepn,bgecl->bclgep', Cc, h_in, jnp.exp(A_cs))
    return (y_diag + y_off).reshape(b, s, g, e, p)

def ssd_mixer(z, xbc, dt_raw, conv_w, conv_b, dt_bias, A_log, D_skip, norm_g):
    b, s, _ = z.shape
    f32 = jnp.float32
    xbc = jax.nn.silu(causal_depthwise_conv(xbc, conv_w, conv_b)).astype(f32)
    xs = xbc[..., :D_SSD]
    Bm = xbc[..., D_SSD:D_SSD + SSD_GROUPS * SSD_STATE].reshape(b, s, SSD_GROUPS, SSD_STATE)
    Cm = xbc[..., D_SSD + SSD_GROUPS * SSD_STATE:].reshape(b, s, SSD_GROUPS, SSD_STATE)
    xh = xs.reshape(b, s, SSD_GROUPS, SSD_HPG, HEAD_DIM)
    dt = jax.nn.softplus(dt_raw.astype(f32) + dt_bias.astype(f32)).reshape(b, s, SSD_GROUPS, SSD_HPG)
    A = -jnp.exp(A_log.astype(f32)).reshape(SSD_GROUPS, SSD_HPG)
    y = ssd_chunked(xh, dt, A, Bm, Cm)
    y = y + D_skip.astype(f32).reshape(SSD_GROUPS, SSD_HPG)[..., None] * xh
    y = y.reshape(b, s, D_SSD) * jax.nn.silu(z.astype(f32))
    yg = y.reshape(b, s, SSD_GROUPS, D_SSD // SSD_GROUPS)
    yg = yg * lax.rsqrt(jnp.mean(yg * yg, axis=-1, keepdims=True) + GATED_NORM_EPS)
    return (yg.reshape(b, s, D_SSD) * norm_g.astype(f32)).astype(z.dtype)

def wkv7_scan(r, w, k, v, a, bb):
    bsz, _, h, n = r.shape

    def step(S, inp):
        r_t, w_t, k_t, v_t, a_t, b_t = inp
        sa = jnp.einsum('bhvk,bhk->bhv', S, a_t)
        S = S * w_t[:, :, None, :] + sa[..., None] * b_t[:, :, None, :] + v_t[..., None] * k_t[:, :, None, :]
        return S, jnp.einsum('bhvk,bhk->bhv', S, r_t)

    seq = (r.swapaxes(0, 1), w.swapaxes(0, 1), k.swapaxes(0, 1), v.swapaxes(0, 1),
           a.swapaxes(0, 1), bb.swapaxes(0, 1))
    S0 = jnp.zeros((bsz, h, n, n), jnp.float32)
    _, y = lax.scan(step, S0, seq)
    return y.swapaxes(0, 1)

def rwkv7_mixer(r, k, v, wd, ad, gd, w0, w2, a0, a2, g2, k_k, k_a, r_k, gn_w, gn_b):
    f32 = jnp.float32
    b, s, _ = r.shape
    H, N = RWKV_HEADS, HEAD_DIM
    r, k, v, wd, ad, gd = (t.astype(f32) for t in (r, k, v, wd, ad, gd))
    logw = -jax.nn.softplus(-(w0.astype(f32) + jnp.tanh(wd) @ w2.astype(f32))) - 0.5
    decay = jnp.exp(-jnp.exp(logw))
    a = jax.nn.sigmoid(a0.astype(f32) + ad @ a2.astype(f32))
    g = jax.nn.sigmoid(gd) @ g2.astype(f32)
    kk = (k * k_k.astype(f32)).reshape(b, s, H, N)
    kk = kk / jnp.maximum(jnp.sqrt(jnp.sum(kk * kk, axis=-1, keepdims=True)), 1e-12)
    k = k * (1.0 + (a - 1.0) * k_a.astype(f32))
    rh = r.reshape(b, s, H, N)
    kh = k.reshape(b, s, H, N)
    vh = v.reshape(b, s, H, N)
    ah = a.reshape(b, s, H, N)
    y = wkv7_scan(rh, decay.reshape(b, s, H, N), kh, vh, -kk, kk * ah)
    mu = jnp.mean(y, axis=-1, keepdims=True)
    var = jnp.mean(jnp.square(y - mu), axis=-1, keepdims=True)
    y = ((y - mu) * lax.rsqrt(var + GN_EPS)).reshape(b, s, D_RWKV) * gn_w.astype(f32) + gn_b.astype(f32)
    bonus = jnp.sum(rh * kh * r_k.astype(f32).reshape(H, N), axis=-1, keepdims=True) * vh
    y = y + bonus.reshape(b, s, D_RWKV)
    return y * g

def second_inputs(seed: int = 0) -> dict:
    key = jax.random.key(seed)
    ks = jax.random.split(key, 32)
    f32 = jnp.float32
    L = DEPTH

    def nrm(k, shape, scale):
        return jax.random.normal(k, shape, f32) * scale

    dt0 = jnp.exp(jax.random.uniform(ks[5], (L, SSD_HEADS), f32, np.log(1e-3), np.log(1e-1)))
    w0_base = jnp.linspace(-6.0, -1.0, D_RWKV, dtype=f32) + 0.5
    return {
        "x": jax.random.normal(ks[0], (BATCH, SEQ, D_MODEL), f32),
        "norm1_g": 1.0 + nrm(ks[1], (L, D_MODEL), 0.02),
        "w_in": nrm(ks[2], (L, D_MODEL, D_IN), D_MODEL ** -0.5),
        "ssd_conv_w": nrm(ks[3], (L, CONV_WIDTH_2, D_XBC), CONV_WIDTH_2 ** -0.5),
        "ssd_conv_b": nrm(ks[4], (L, D_XBC), 0.02),
        "ssd_dt_bias": dt0 + jnp.log(-jnp.expm1(-dt0)),
        "ssd_A_log": jnp.log(jax.random.uniform(ks[6], (L, SSD_HEADS), f32, 1.0, 16.0)),
        "ssd_D": 1.0 + nrm(ks[7], (L, SSD_HEADS), 0.1),
        "ssd_norm_g": 1.0 + nrm(ks[8], (L, D_SSD), 0.02),
        "rwkv_mu": jax.random.uniform(ks[9], (L, D_RWKV_IN), f32),
        "rwkv_w0": w0_base + nrm(ks[10], (L, D_RWKV), 0.1),
        "rwkv_w2": nrm(ks[11], (L, DECAY_LORA, D_RWKV), 0.1 * DECAY_LORA ** -0.5),
        "rwkv_a0": nrm(ks[12], (L, D_RWKV), 0.1),
        "rwkv_a2": nrm(ks[13], (L, AAA_LORA, D_RWKV), 0.1 * AAA_LORA ** -0.5),
        "rwkv_g2": nrm(ks[14], (L, GATE_LORA, D_RWKV), GATE_LORA ** -0.5),
        "rwkv_k_k": 0.85 + nrm(ks[15], (L, D_RWKV), 0.05),
        "rwkv_k_a": 1.0 + nrm(ks[16], (L, D_RWKV), 0.05),
        "rwkv_r_k": nrm(ks[17], (L, D_RWKV), 0.1),
        "rwkv_gn_w": 1.0 + nrm(ks[18], (L, D_RWKV), 0.02),
        "rwkv_gn_b": nrm(ks[19], (L, D_RWKV), 0.02),
        "w_out": nrm(ks[20], (L, D_MIX, D_MODEL), D_MIX ** -0.5),
        "norm2_g": 1.0 + nrm(ks[21], (L, D_MODEL), 0.02),
        "w_gate": nrm(ks[22], (L, D_MODEL, D_FF_2), D_MODEL ** -0.5),
        "w_up": nrm(ks[23], (L, D_MODEL, D_FF_2), D_MODEL ** -0.5),
        "w_down": nrm(ks[24], (L, D_FF_2, D_MODEL), D_FF_2 ** -0.5),
        "norm_f_g": 1.0 + nrm(ks[25], (D_MODEL,), 0.02),
    }

def second_block(x, norm1_g, w_in, ssd_conv_w, ssd_conv_b, ssd_dt_bias, ssd_A_log, ssd_D, ssd_norm_g,
              rwkv_mu, rwkv_w0, rwkv_w2, rwkv_a0, rwkv_a2, rwkv_g2, rwkv_k_k, rwkv_k_a, rwkv_r_k,
              rwkv_gn_w, rwkv_gn_b, w_out, norm2_g, w_gate, w_up, w_down, norm_f_g):
    h = x
    for l in range(DEPTH):
        u = rms_norm(h, norm1_g[l])
        P = u @ w_in[l]
        o1 = D_SSD
        o2 = o1 + D_XBC
        o3 = o2 + SSD_HEADS
        z = P[..., :o1]
        xbc = P[..., o1:o2]
        dt_raw = P[..., o2:o3]
        pr = P[..., o3:]
        prev = jnp.pad(pr, ((0, 0), (1, 0), (0, 0)))[:, :-1]
        pr = pr + (prev - pr) * rwkv_mu[l]
        c1 = D_RWKV
        c2 = 2 * D_RWKV
        c3 = 3 * D_RWKV
        c4 = c3 + DECAY_LORA
        c5 = c4 + AAA_LORA
        y_ssd = ssd_mixer(z, xbc, dt_raw, ssd_conv_w[l], ssd_conv_b[l], ssd_dt_bias[l],
                          ssd_A_log[l], ssd_D[l], ssd_norm_g[l])
        y_rwkv = rwkv7_mixer(pr[..., :c1], pr[..., c1:c2], pr[..., c2:c3], pr[..., c3:c4],
                             pr[..., c4:c5], pr[..., c5:], rwkv_w0[l], rwkv_w2[l], rwkv_a0[l],
                             rwkv_a2[l], rwkv_g2[l], rwkv_k_k[l], rwkv_k_a[l], rwkv_r_k[l],
                             rwkv_gn_w[l], rwkv_gn_b[l]).astype(h.dtype)
        h = h + jnp.concatenate([y_ssd, y_rwkv], axis=-1) @ w_out[l]
        v = rms_norm(h, norm2_g[l])
        h = h + (jax.nn.silu(v @ w_gate[l]) * (v @ w_up[l])) @ w_down[l]
    return rms_norm(h, norm_f_g)


_first_inputs_2 = second_inputs


def second_inputs(seed=0):
    import zlib

    import numpy as np

    out = dict(_first_inputs_2(seed))
    spreads = {}
    factors = {'ssd_conv_b': 3.4,
     'ssd_norm_g': 4.842,
     'rwkv_w2': 8.0,
     'rwkv_a0': 3.673,
     'rwkv_a2': 4.096,
     'rwkv_k_k': 5.784,
     'rwkv_k_a': 3.221,
     'rwkv_gn_w': 8.0,
     'rwkv_gn_b': 8.0,
     'norm2_g': 4.541,
     'norm_f_g': 2.729}
    for name, (base, spread) in spreads.items():
        noise = np.random.default_rng([zlib.crc32(name.encode()), seed]).standard_normal(out[name].shape)
        drawn = base * np.exp(spread * noise) if base else spread * noise
        out[name] = __import__('jax').numpy.asarray(drawn.astype(out[name].dtype))
    for name, factor in factors.items():
        out[name] = (out[name] * factor).astype(out[name].dtype)
    return out


_narrow_inputs_2 = second_inputs


def second_inputs(seed=0):

    out = dict(_narrow_inputs_2(seed))
    wider = {'ssd_norm_g': 3.22, 'rwkv_gn_w': 3.55, 'rwkv_gn_b': 3.63, 'norm_f_g': 3.07}
    for name, times in wider.items():
        mean = out[name].mean()
        out[name] = (mean + times * (out[name] - mean)).astype(out[name].dtype)
    return out


def setup_inputs(seed=0):
    out = dict(first_inputs(seed))
    for name, value in second_inputs(seed + 1).items():
        if name != "x":
            out[name + "_2"] = value
    return out


def reference(
    x, positions, attn_norm_w, w_in, ssm_lambda_re, ssm_lambda_im, ssm_log_dt, ssm_b_re,
    ssm_b_im, ssm_c_re, ssm_c_im, ssm_d, ssm_w_glu, ssm_b_glu, mla_q_norm_w, mla_w_uq,
    mla_kv_norm_w, mla_w_ukv, ssm_out_norm_w, mla_out_norm_w, w_out, ffn_norm_w, ffn_w_up,
    ffn_conv_w, ffn_conv_b, ffn_w_down, final_norm_w, norm1_g_2, w_in_2, ssd_conv_w_2,
    ssd_conv_b_2, ssd_dt_bias_2, ssd_A_log_2, ssd_D_2, ssd_norm_g_2, rwkv_mu_2, rwkv_w0_2,
    rwkv_w2_2, rwkv_a0_2, rwkv_a2_2, rwkv_g2_2, rwkv_k_k_2, rwkv_k_a_2, rwkv_r_k_2, rwkv_gn_w_2,
    rwkv_gn_b_2, w_out_2, norm2_g_2, w_gate_2, w_up_2, w_down_2, norm_f_g_2,
):
    x = first_block(
        x, positions, attn_norm_w, w_in, ssm_lambda_re, ssm_lambda_im, ssm_log_dt, ssm_b_re,
        ssm_b_im, ssm_c_re, ssm_c_im, ssm_d, ssm_w_glu, ssm_b_glu, mla_q_norm_w, mla_w_uq,
        mla_kv_norm_w, mla_w_ukv, ssm_out_norm_w, mla_out_norm_w, w_out, ffn_norm_w, ffn_w_up,
        ffn_conv_w, ffn_conv_b, ffn_w_down, final_norm_w,
    )
    return second_block(
        x, norm1_g_2, w_in_2, ssd_conv_w_2, ssd_conv_b_2, ssd_dt_bias_2, ssd_A_log_2, ssd_D_2,
        ssd_norm_g_2, rwkv_mu_2, rwkv_w0_2, rwkv_w2_2, rwkv_a0_2, rwkv_a2_2, rwkv_g2_2,
        rwkv_k_k_2, rwkv_k_a_2, rwkv_r_k_2, rwkv_gn_w_2, rwkv_gn_b_2, w_out_2, norm2_g_2,
        w_gate_2, w_up_2, w_down_2, norm_f_g_2,
    )


_drawn_inputs = setup_inputs


def setup_inputs(seed=0):
    import zlib

    import numpy as np

    out = dict(_drawn_inputs(seed))
    spreads = {}
    factors = {}
    for name, (base, spread) in spreads.items():
        noise = np.random.default_rng([zlib.crc32(name.encode()), seed]).standard_normal(out[name].shape)
        drawn = base * np.exp(spread * noise) if base else spread * noise
        out[name] = __import__('jax').numpy.asarray(drawn.astype(out[name].dtype))
    for name, factor in factors.items():
        out[name] = (out[name] * factor).astype(out[name].dtype)
    return out
```

```python
import math
from collections import deque
from contextlib import ExitStack

import numpy as np

import concourse.bass as bass
from concourse import mybir

F32 = mybir.dt.float32
I32 = mybir.dt.int32
ALU = mybir.AluOpType
ACT = mybir.ActivationFunctionType
X = mybir.AxisListType.X
MUL, ADD, SUB, MAX, MIN = ALU.mult, ALU.add, ALU.subtract, ALU.max, ALU.min

T = 256
D = 2048
FF = 5632
NH = 32
RING = 7
SLOT = 2048
NARENA = 38500

CST_COLS = [("ident", 128), ("ones", 128), ("blk", 128), ("perm", 128), ("m3", 384), ("s32", 32),
            ("bm", 128), ("bm4", 4), ("zc", 256), ("cm", 256), ("kp", 2), ("ifr", 1), ("rm", 256)]
VEC_COLS = [("attn_norm_w", 16), ("mla_q_norm_w", 4), ("mla_kv_norm_w", 2), ("ssm_out_norm_w", 8),
            ("mla_out_norm_w", 8), ("ffn_norm_w", 16), ("cw0", 88), ("cw1", 88), ("cw2", 88),
            ("ffn_conv_b", 88), ("final_norm_w", 16), ("ssm_d", 8), ("ssm_b_glu", 8),
            ("norm1_g_2", 16), ("dw0", 24), ("dw1", 24), ("dw2", 24), ("dw3", 24),
            ("ssd_conv_b_2", 24), ("ssd_norm_g_2", 16), ("mu_r", 16), ("mu_k", 16), ("mu_v", 16),
            ("mu_wd", 1), ("mu_ad", 1), ("mu_gd", 2), ("rwkv_w0_2", 16), ("rwkv_a0_2", 16),
            ("rwkv_k_k_2", 16), ("rwkv_k_a_2", 16), ("rwkv_r_k_2", 16), ("rwkv_gn_w_2", 16),
            ("rwkv_gn_b_2", 16), ("norm2_g_2", 16), ("norm_f_g_2", 16), ("dskip", 16),
            ("dtb", 1), ("alog", 1), ("lr", 32), ("li", 32), ("ldt", 32)]


def columns(cols):
    at, out = 0, {}
    for name, n in cols:
        out[name] = (at, n)
        at += n
    return out, at


CST_AT, NCST = columns(CST_COLS)
VEC_AT, NVEC = columns(VEC_COLS)


class Queue:

    def __init__(self, sem):
        self.sem, self.n, self.items, self.seen = sem, 0, [], {}

    def wait(self, *needs):
        for tok in needs:
            if tok is None:
                continue
            if isinstance(tok, list):
                self.wait(*tok)
                continue
            sem, v = tok
            if v > self.seen.get(sem.name, 0):
                self.seen[sem.name] = v
                self.items.append(lambda e, sem=sem, v=v: e.wait_ge(sem, v))

    def put(self, fn, needs, sig=True):
        self.wait(*needs)
        if sig:
            self.n += 1
            sem = self.sem
            self.items.append(lambda e: fn(e).then_inc(sem, 1))
            return (sem, self.n)
        self.items.append(fn)
        return None

    def now(self):
        return (self.sem, self.n)

    def replay(self, e):
        for f in self.items:
            f(e)

    def tt(self, out, a, b, op, *needs):
        return self.put(lambda e: e.tensor_tensor(out, a, b, op), needs)

    def ts(self, out, a, s1, s2, op0, op1, *needs):
        if op1 is None:
            return self.put(lambda e: e.tensor_scalar(out, a, s1, None, op0), needs)
        return self.put(lambda e: e.tensor_scalar(out, a, s1, s2, op0, op1), needs)

    def stt(self, out, a, s, b, op0, op1, *needs):
        return self.put(lambda e: e.scalar_tensor_tensor(out=out, in0=a, scalar=s, in1=b, op0=op0,
                                                         op1=op1), needs)

    def copy(self, out, a, *needs):
        return self.put(lambda e: e.tensor_copy(out, a), needs)

    def recip(self, out, a, *needs):
        return self.put(lambda e: e.reciprocal(out, a), needs)

    def red(self, out, a, op, *needs):
        return self.put(lambda e: e.tensor_reduce(out, a, X, op), needs)

    def scan(self, out, d0, d1, *needs):
        return self.put(lambda e: e.tensor_tensor_scan(out, d0, d1, 0.0, MUL, ADD), needs)

    def tr(self, out, a, *needs):
        return self.put(lambda e: e.transpose(out, a), needs)

    def mset(self, out, v, *needs):
        return self.put(lambda e: e.memset(out, v), needs)

    def act(self, out, a, f, *needs, bias=0.0, scale=1.0, acc=None):
        if acc is not None:
            return self.put(lambda e: e.activation(out, a, f, bias=bias, scale=scale, accum_out=acc), needs)
        return self.put(lambda e: e.activation(out, a, f, bias=bias, scale=scale), needs)

    def mm(self, out, lhsT, rhs, start, stop, *needs, sig=False):
        return self.put(lambda e: e.matmul(out, lhsT, rhs, start=start, stop=stop), needs, sig)

    def tp(self, out, a, ident, *needs, sig=False):
        return self.put(lambda e: e.transpose(out, a, ident), needs, sig)


class Pool:

    def __init__(self, items):
        self.free = deque((x, []) for x in items)

    def take(self):
        return self.free.popleft()

    def give(self, x, *toks):
        self.free.append((x, list(toks)))


def run(*gens):
    live = list(gens)
    while live:
        for g in list(live):
            try:
                next(g)
            except StopIteration:
                live.remove(g)


def flight(make, n, depth):
    live, i = [], 0
    while live or i < n:
        while len(live) < depth and i < n:
            live.append(make(i))
            i += 1
        for g in list(live):
            try:
                next(g)
            except StopIteration:
                live.remove(g)
        yield


def program(nc, d, out):
    with ExitStack() as ctx:
        def sem(name):
            return ctx.enter_context(nc.semaphore(name))

        arena = ctx.enter_context(nc.sbuf_tensor("arena", [128, NARENA], F32))
        ring = ctx.enter_context(nc.sbuf_tensor("ring", [128, RING * SLOT], F32))
        banks = [ctx.enter_context(nc.psum_tensor(f"bank{i}", [128, 512], F32)) for i in range(8)]
        P, V, A, G, S = (Queue(sem(f"s_{n}")) for n in ("pe", "dve", "act", "pool", "sp"))
        ENG = (P, V, A, G)
        ring_sem = [sem(f"s_ring{i}") for i in range(RING)]
        st_sem = sem("s_st")
        nload, nstore = [0], [0]

        top = [0]

        def alloc(*shape):
            n = int(np.prod(shape))
            o = top[0]
            top[0] += n
            assert top[0] <= NARENA, top[0]
            v = arena[:, o:o + n]
            if len(shape) == 2:
                v = v.rearrange("p (a b) -> p a b", b=shape[1])
            elif len(shape) == 3:
                v = v.rearrange("p (a b c) -> p a b c", b=shape[1], c=shape[2])
            elif len(shape) == 4:
                v = v.rearrange("p (a b c d) -> p a b c d", b=shape[1], c=shape[2], d=shape[3])
            return v

        def barrier():
            toks = [q.now() for q in ENG]
            for q in ENG:
                q.wait(*[t for t in toks if t[1]])
            return toks

        def load(dst, src, *needs, q=S):
            q.wait(*needs)
            nload[0] += 1
            sm = sem(f"s_ld{nload[0]}")
            q.items.append(lambda e: e.dma_start(dst, src).then_inc(sm, 16))
            return (sm, 16)

        slot_free = [[] for _ in range(RING)]
        nslot = [0]

        def unit(src, n):
            u = nslot[0]
            nslot[0] += 1
            s = u % RING
            S.wait(*slot_free[s])
            dst = ring[:, s * SLOT:s * SLOT + n]
            sm = ring_sem[s]
            if len(src.shape) == 3:
                d3 = dst.rearrange("p (m x) -> p m x", m=src.shape[1])
                S.items.append(lambda e: e.dma_start(d3, src).then_inc(sm, 16))
            else:
                S.items.append(lambda e: e.dma_start(dst, src).then_inc(sm, 16))
            return dst, s, (sm, 16 * (u // RING + 1))

        PS = Pool(range(8))

        def linear(w, nt, KC, rhs, ktok, evac, t0=0, M=128, N=T):
            kper = max(k for k in range(1, KC + 1) if KC % k == 0 and k * 128 <= SLOT)
            tper = max(1, SLOT // (KC * M)) if KC == kper else 1
            t = t0
            while t < t0 + nt:
                m = min(tper, t0 + nt - t)
                if KC == kper:
                    src = w[t:t + m].rearrange("m p x -> p m x")
                    buf, s, tok = unit(src, m * KC * M)
                    units = [(buf, s, tok)]
                else:
                    units = []
                    for k0 in range(0, KC, kper):
                        units.append(unit(w[t, :, k0 * 128:(k0 + kper) * 128], kper * 128))
                for j in range(m):
                    b, free = PS.take()
                    ps = banks[b][0:M, 0:N]
                    last = None
                    for ui, (buf, s, tok) in enumerate(units):
                        kn = KC if KC == kper else kper
                        wv = buf.rearrange("p (m k c) -> p m k c", k=kn, c=M)
                        for kk in range(kn):
                            kc = ui * kper + kk
                            need = [tok] + (free if kc == 0 else []) + [ktok(kc)]
                            last = P.mm(ps, wv[:, j, kk, :], rhs(kc), kc == 0, kc == KC - 1,
                                        *need, sig=(kk == kn - 1))
                        slot_free[s] = [last]
                    PS.give(b, *evac(t + j, banks[b], last))
                    yield
                t += m

        cst = alloc(NCST)
        vec = alloc(NVEC)
        tc0 = [load(cst, d["cst"]), load(vec, d["vec"])]

        def C(name, a=0, b=None):
            o, n = CST_AT[name]
            return cst[:, o + a:o + (n if b is None else b)]

        def W(name, i=0):
            o, n = VEC_AT[name]
            return vec[:, o + i:o + i + 1]

        def WR(name):
            o, n = VEC_AT[name]
            return vec[:, o:o + n]

        ident, ones, blk = C("ident"), C("ones"), C("blk")
        h = alloc(16, T)
        hl = [load(h[:, i * 4:(i + 1) * 4, :], d["xT"][:, i * 4:(i + 1) * 4, :]) for i in range(4)]
        htok = [hl[i // 4] for i in range(16)]
        scr = Pool([alloc(T) for _ in range(6)])
        ms, rr = alloc(T), alloc(T)
        base = top[0]
        for q in ENG:
            q.wait(tc0)
        norm_free = [[]]

        def rms(chunks, toks, wname, outs, n, eps):
            b, free = PS.take()
            nk = len(chunks)
            for i in range(nk):
                s, sf = scr.take()
                ta = A.act(s, chunks[i], ACT.Square, toks[i], *sf)
                tm = P.mm(banks[b][:, 0:T], ones, s, i == 0, i == nk - 1, ta, *free, sig=True)
                scr.give(s, tm)
            t = V.ts(ms, banks[b][:, 0:T], 1.0 / n, eps, MUL, ADD, tm, *norm_free[0])
            PS.give(b, t)
            t = V.recip(rr, ms, t)
            t = A.act(rr, rr, ACT.Sqrt, t)
            res = []
            for i in range(nk):
                res.append(V.stt(outs[i], chunks[i], W(wname[0], wname[1] + i), rr, MUL, MUL, t, toks[i]))
            norm_free[0] = [res[-1]]
            return res

        hn = alloc(16, T)
        hchunks = [h[:, i, :] for i in range(16)]
        tn = rms(hchunks, htok, ("attn_norm_w", 0), [hn[:, i, :] for i in range(16)], D, 1e-6)
        ntok = lambda kc: tn[kc]
        nrhs = lambda kc: hn[:, kc, :]

        u = alloc(8, T)
        cq = alloc(4, T)
        ckv = alloc(2, T)
        kpe = alloc(T)
        utok, cqtok, ckvtok, kpetok = {}, {}, {}, {}

        def ev_in(t, b, tok):
            ps = b[:, 0:T]
            if t < 8:
                r = utok[t] = A.act(u[:, t, :], ps, ACT.Copy, tok)
            elif t < 12:
                r = cqtok[t - 8] = A.act(cq[:, t - 8, :], ps, ACT.Copy, tok)
            else:
                r = ckvtok[t - 12] = A.act(ckv[:, t - 12, :], ps, ACT.Copy, tok)
            return [r]

        def ev_kpe(t, b, tok):
            r = kpetok[0] = A.act(kpe, b[:, 0:T], ACT.Copy, tok)
            return [r]

        s5 = {n: alloc(32) for n in ("dt", "mag", "phi", "kf", "r", "sn", "cs", "sh", "ar", "ai", "den",
                                     "zr", "zi", "t1", "t2")}
        Cw = [alloc(32, 32) for _ in range(2)]
        Bw = [alloc(8, 128) for _ in range(2)]
        tl = [load(Cw[0], d["cre"]), load(Cw[1], d["cim"]), load(Bw[0], d["bre"]), load(Bw[1], d["bim"])]
        for q in ENG:
            q.wait(tl)
        NB = 8
        Cz = Cw
        tab = [alloc(NB, T) for _ in range(2)]
        ec, es, e1, e2, e3 = (alloc(NB) for _ in range(5))
        tmpA = alloc(NB, 128)

        MAGIC = 12582912.0
        PC = []
        rest = 2 * math.pi
        for bits in (8, 8, 10):
            e = math.floor(math.log2(rest))
            q_ = math.floor(rest / 2.0 ** (e - bits + 1)) * 2.0 ** (e - bits + 1)
            PC.append(q_)
            rest -= q_
        PC.append(float(np.float32(rest)))

        def sincos(ang, kf, r, sn, cs, sh, tok, *needs):
            t = V.ts(kf, ang, 1.0 / (2 * math.pi), MAGIC, MUL, ADD, tok, *needs)
            t = V.ts(kf, kf, MAGIC, None, SUB, None, t)
            t = V.stt(r, kf, -PC[0], ang, MUL, ADD, t)
            for c in PC[1:]:
                t = V.stt(r, kf, -c, r, MUL, ADD, t)
            t = V.ts(r, r, 3.1415925, -3.1415925, MIN, MAX, t)
            ta = A.act(sn, r, ACT.Sin, t)
            tb = A.act(sh, r, ACT.Sin, t, scale=0.5)
            t = V.tt(sh, sh, sh, MUL, tb)
            t = V.ts(cs, sh, -2.0, 1.0, MUL, ADD, t)
            return [ta, t]

        def s5_params():
            k = s5
            t = A.act(k["dt"], WR("ldt"), ACT.Exp)
            t1 = V.tt(k["t1"], WR("lr"), k["dt"], MUL, t)
            t2 = V.tt(k["phi"], WR("li"), k["dt"], MUL, t)
            tm = A.act(k["mag"], k["t1"], ACT.Exp, t1)
            tk = sincos(k["phi"], k["kf"], k["r"], k["sn"], k["cs"], k["sh"], t2)
            yield
            t = V.tt(k["ar"], k["mag"], k["cs"], MUL, tm, *tk)
            t = V.ts(k["ar"], k["ar"], -1.0, None, ADD, None, t)
            ta = V.tt(k["ai"], k["mag"], k["sn"], MUL)
            t = V.tt(k["den"], WR("lr"), WR("lr"), MUL)
            t = V.tt(k["t1"], WR("li"), WR("li"), MUL, tm)
            t = V.tt(k["den"], k["den"], k["t1"], ADD, t)
            t = V.recip(k["den"], k["den"], t)
            t = V.tt(k["t1"], k["ar"], WR("lr"), MUL, t)
            t = V.tt(k["t2"], k["ai"], WR("li"), MUL, ta, t)
            t = V.tt(k["t1"], k["t1"], k["t2"], ADD, t)
            t = V.tt(k["zr"], k["t1"], k["den"], MUL, t)
            t = V.tt(k["t1"], k["ai"], WR("lr"), MUL, t)
            t = V.tt(k["t2"], k["ar"], WR("li"), MUL, t)
            t = V.tt(k["t1"], k["t1"], k["t2"], SUB, t)
            t = V.tt(k["zi"], k["t1"], k["den"], MUL, t)
            yield
            zr = k["zr"].unsqueeze(2).broadcast_to([128, 32, 32])
            zi = k["zi"].unsqueeze(2).broadcast_to([128, 32, 32])
            tmp = tmpA.rearrange("p a b -> p (a b)").rearrange("p (a b) -> p a b", b=32)
            tmp2 = tab[0].rearrange("p a b -> p (a b)")[:, 0:1024].rearrange("p (a b) -> p a b", b=32)
            t = V.tt(tmp, Cw[1], zi, MUL, t)
            t = V.tt(tmp2, Cw[0], zi, MUL, t)
            t = V.tt(Cw[0], Cw[0], zr, MUL, t)
            t = V.tt(Cw[0], Cw[0], tmp, SUB, t)
            t = V.tt(Cw[1], Cw[1], zr, MUL, t)
            t = V.stt(Cw[1], Cw[1], -1.0, tmp2, MUL, SUB, t)
            s5["done"] = t
            yield

        def tables(hf, *needs):
            tc, tsn = tab
            c0 = s5["cs"][:, hf * NB:hf * NB + NB]
            s0 = s5["sn"][:, hf * NB:hf * NB + NB]
            t = V.mset(tc[:, :, 0:1], 1.0, s5["done"], *needs)
            t = V.mset(tsn[:, :, 0:1], 0.0, t)
            t = V.copy(ec, c0, t)
            t = V.copy(es, s0, t)
            n = 1
            while n < T:
                ecb = ec.unsqueeze(2).broadcast_to([128, NB, n])
                esb = es.unsqueeze(2).broadcast_to([128, NB, n])
                a, b = tc[:, :, 0:n], tsn[:, :, 0:n]
                c, s = tc[:, :, n:2 * n], tsn[:, :, n:2 * n]
                tmp = tmpA[:, :, 0:n]
                t = V.tt(c, a, ecb, MUL, t)
                t = V.tt(tmp, b, esb, MUL, t)
                t = V.tt(c, c, tmp, SUB, t)
                yield
                t = V.tt(s, b, ecb, MUL, t)
                t = V.tt(tmp, a, esb, MUL, t)
                t = V.tt(s, s, tmp, ADD, t)
                yield
                n *= 2
                if n < T:
                    t = V.tt(e1, ec, ec, MUL, t)
                    t = V.tt(e2, es, es, MUL, t)
                    t = V.tt(e3, ec, es, MUL, t)
                    t = V.tt(ec, e1, e2, SUB, t)
                    t = V.ts(es, e3, 2.0, None, MUL, None, t)
            s5["tab"] = t

        def chain(*gens):
            for g in gens:
                yield from g

        run(chain(linear(d["w_in"], 14, 16, nrhs, ntok, ev_in),
                  linear(d["w_kpe"], 1, 16, nrhs, ntok, ev_kpe)),
            chain(s5_params(), tables(0)))

        barrier()
        def seq(dct, n):
            return [dct[i] for i in range(n)]

        y = alloc(8, T)
        ytok = {}
        wz = Pool([(alloc(2, T), alloc(2, T), alloc(2, T)) for _ in range(2)])

        def ssm_tile(hf, c, q, yb, yfree, state):
            j = 4 * c + q
            jj = j - NB * hf
            b, free = PS.take()
            bk = banks[b][:, :].rearrange("p (r t) -> p r t", r=2)
            for r in range(2):
                tm = P.mm(bk[:, r, :], Bw[r][32 * q:32 * q + 32, c, :], u[32 * q:32 * q + 32, c, :],
                          True, True, utok[c], *free, sig=True)
            (wa, wb, wc), wf = wz.take()
            cb = tab[0][:, jj, :].unsqueeze(1).broadcast_to([128, 2, T])
            sb_ = tab[1][:, jj, :].unsqueeze(1).broadcast_to([128, 2, T])
            yield
            ta = V.tt(wa, bk, cb, MUL, tm, s5["tab"], *wf)
            tb = V.tt(wb, bk, sb_, MUL)
            PS.give(b, tb)
            t1 = V.tt(wc[:, 0, :], wa[:, 0, :], wb[:, 1, :], ADD, tb)
            t2 = G.tt(wc[:, 1, :], wa[:, 1, :], wb[:, 0, :], SUB, tb, *wf)
            yield
            mg = s5["mag"][:, j:j + 1].broadcast_to([128, T])
            t1 = V.scan(wa[:, 0, :], mg, wc[:, 0, :], t1, t2)
            t2 = V.scan(wa[:, 1, :], mg, wc[:, 1, :], t2)
            yield
            t3 = V.tt(wb, wa, cb, MUL, t2)
            t4 = G.tt(wc, wa, sb_, MUL, t2, s5["tab"])
            t5 = V.tt(wa[:, 0, :], wb[:, 0, :], wc[:, 1, :], SUB, t3, t4)
            t6 = V.tt(wa[:, 1, :], wb[:, 1, :], wc[:, 0, :], ADD, t3, t4)
            yield
            yp = banks[yb][32 * q:32 * q + 32, 0:T]
            P.mm(yp, Cz[0][:, j, :], wa[:, 0, :], True, False, t5, s5["done"], *yfree)
            tm = P.mm(yp, Cz[1][:, j, :], wa[:, 1, :], False, True, t6, sig=True)
            wz.give((wa, wb, wc), tm)
            state.append(t6)
            state.append(tm)

        def ssm_chunk(hf, c):
            yb, yfree = PS.take()
            st = []
            yield from flight(lambda q: ssm_tile(hf, c, q, yb, yfree, st), 4, 2)
            s, sf = scr.take()
            t = V.stt(s, u[:, c, :], W("ssm_d", c), banks[yb][:, 0:T], MUL, ADD, *st, *sf)
            PS.give(yb, t)
            t = A.act(y[:, c, :], s, ACT.Gelu_apprx_tanh, t)
            scr.give(s, t)
            ytok[c] = t
            s5["last"] = st

        def ssm_half(hf):
            for c in range(2 * hf, 2 * hf + 2):
                yield from ssm_chunk(hf, c)

        def ssm_all():
            for hf in range(4):
                if hf:
                    yield from tables(hf, s5["last"])
                yield from ssm_half(hf)

        cqn = cq
        ckn = ckv
        qn = hn[:, 0:8, :]
        kn = hn[:, 8:16, :]
        qp = alloc(4, T)
        o = h[:, 0:8, :]
        vt = h[:, 8:16, :].rearrange("p (a b) c -> p a (b c)", a=2)
        kz = alloc(2, T)
        pos = alloc(T)
        posi = arena[:, top[0]:top[0] + 2 * T].bitcast(I32)
        top[0] += 2 * T
        pf_ = posi.bitcast(F32)
        ak, ar_ = pf_[:, 0:T], pf_[:, T:2 * T]
        csn, ssn, ash = (alloc(T) for _ in range(3))
        pt2 = Pool([(alloc(T), alloc(T)) for _ in range(2)])
        sm = alloc(16, 4)
        qtok, qptok, ktok_, vtok, otok = {}, {}, {}, {}, {}

        def mla():
            cqt = rms([cq[:, i, :] for i in range(4)], seq(cqtok, 4), ("mla_q_norm_w", 0),
                      [cqn[:, i, :] for i in range(4)], 512, 1e-6)
            ckt = rms([ckv[:, i, :] for i in range(2)], seq(ckvtok, 2), ("mla_kv_norm_w", 0),
                      [ckn[:, i, :] for i in range(2)], 256, 1e-6)
            yield
            tl = load(posi, d["pos"].partition_broadcast(128), q=A)
            t = V.copy(pos, posi[:, 0:2 * T:2], tl)
            t = V.ts(pos, pos, C("ifr"), None, MUL, None, t)
            tcs = sincos(pos, ak, ar_, ssn, csn, ash, t)
            yield

            def rope(dst, src, tok):
                b, free = PS.take()
                tm = P.mm(banks[b][:, 0:T], C("perm"), src, True, True, tok, *free, sig=True)
                s, sf = scr.take()
                t1 = V.tt(s, banks[b][:, 0:T], ssn, MUL, tm, *tcs, *sf)
                PS.give(b, t1)
                t2 = V.tt(dst, src, csn, MUL, tm, *tcs)
                t = V.tt(dst, dst, s, ADD, t1, t2)
                scr.give(s, t)
                return t

            tk = rope(kpe, kpe, kpetok[0])
            for z in range(2):
                tkz = V.ts(kz[:, z, :], kpe, C("kp", z, z + 1), None, MUL, None, tk)
            yield

            def ev_q(t, b, tok):
                if t < 8:
                    r = qtok[t] = A.act(qn[:, t, :], b[:, 0:T], ACT.Copy, tok)
                    return [r]
                r = A.act(qp[:, t - 8, :], b[:, 0:T], ACT.Copy, tok)
                qptok[t - 8] = rope(qp[:, t - 8, :], qp[:, t - 8, :], r)
                return [r]

            yield from linear(d["w_uq"], 12, 4, lambda kc: cqn[:, kc, :], lambda kc: cqt[kc], ev_q)

            def ev_k(t, b, tok):
                r = ktok_[t] = A.act(kn[:, t, :], b[:, 0:T], ACT.Copy, tok)
                return [r]

            yield from linear(d["w_uk"], 8, 2, lambda kc: ckn[:, kc, :], lambda kc: ckt[kc], ev_k)
            buf, s, tok = unit(d["w_uv"], 2048)
            wv = buf.rearrange("p (k n) -> p k n", k=2)
            for hf in range(2):
                for n in range(2):
                    b, free = PS.take()
                    for k in range(2):
                        tm = P.mm(banks[b][:, :], ckn[:, k, hf * 128:(hf + 1) * 128],
                                  wv[:, k, n * 512:(n + 1) * 512], k == 0, k == 1, tok, ckt[k], *free,
                                  sig=(k == 1))
                    slot_free[s] = [tm]
                    r = A.act(vt[:, hf, n * 512:(n + 1) * 512], banks[b][:, :], ACT.Copy, tm)
                    PS.give(b, r)
                    vtok[(hf, n)] = r
                yield

            scale = float((128 + 64) ** -0.5)

            def head(i):
                hd, hf = i // 2, i % 2
                n = 128 * (hf + 1)
                b, free = PS.take()
                sp_ = banks[b][:, 0:n]
                P.mm(sp_, qn[:, hd, hf * 128:(hf + 1) * 128], kn[:, hd, 0:n], True, False,
                     qtok[hd], ktok_[hd], *free)
                tm = P.mm(sp_, qp[:, hd // 2, hf * 128:(hf + 1) * 128], kz[:, hd % 2, 0:n], False, True,
                          qptok[hd // 2], tkz, sig=True)
                (sa, sb_), sf = pt2.take()
                yield
                zc = C("zc", 128 - 128 * hf, 256)
                s4 = sm[:, i, :]
                t = V.stt(sa[:, 0:n], sp_, scale, zc, MUL, ADD, tm, *sf)
                PS.give(b, t)
                t = V.red(s4[:, 0:1], sa[:, 0:n], MAX, t)
                t = V.ts(s4[:, 1:2], s4[:, 0:1], -1.0, None, MUL, None, t)
                t = A.act(sa[:, 0:n], sa[:, 0:n], ACT.Exp, t, bias=s4[:, 1:2], acc=s4[:, 2:3])
                yield
                t = V.recip(s4[:, 3:4], s4[:, 2:3], t)
                t = V.ts(sa[:, 0:n], sa[:, 0:n], s4[:, 3:4], None, MUL, None, t)
                b, free = PS.take()
                for k in range(hf + 1):
                    tm = P.tp(banks[b][:, k * 128:(k + 1) * 128], sa[:, k * 128:(k + 1) * 128], ident,
                              t, *free, sig=True)
                yield
                t = A.act(sb_[:, 0:n], banks[b][:, 0:n], ACT.Copy, tm)
                PS.give(b, t)
                b, free = PS.take()
                for k in range(hf + 1):
                    tm = P.mm(banks[b][:, 0:128], vt[:, k, hd * 128:(hd + 1) * 128],
                              sb_[:, k * 128:(k + 1) * 128], k == 0, k == hf, t, vtok[(k, hd // 4)],
                              *free, sig=True)
                pt2.give((sa, sb_), tm)
                yield
                t = A.act(o[:, hd, hf * 128:(hf + 1) * 128], banks[b][:, 0:128], ACT.Copy, tm)
                PS.give(b, t)
                otok[i] = t

            yield from flight(head, 16, 2)

        run(ssm_all(), mla())

        y2tok = {}
        y2 = u
        tb = barrier()

        def ev_glu(t, b, tok):
            s, sf = scr.take()
            r = A.act(s, b[:, 0:T], ACT.Sigmoid, tok, *sf, bias=W("ssm_b_glu", t))
            y2tok[t] = V.tt(y2[:, t, :], y[:, t, :], s, MUL, r)
            scr.give(s, y2tok[t])
            return [r]

        run(linear(d["w_glu"], 8, 8, lambda kc: y[:, kc, :], lambda kc: ytok[kc], ev_glu))
        cat = hn
        t1 = rms([y2[:, i, :] for i in range(8)], seq(y2tok, 8), ("ssm_out_norm_w", 0),
                 [cat[:, i, :] for i in range(8)], 1024, 1e-6)
        t2 = rms([o[:, i, :] for i in range(8)], [otok[2 * i + 1] for i in range(8)], ("mla_out_norm_w", 0),
                 [cat[:, 8 + i, :] for i in range(8)], 1024, 1e-6)
        ct = t1 + t2
        tl = load(h, d["xT"], t2, V.now(), P.now(), A.now(), q=A)
        htok = [tl] * 16

        def ev_res(t, b, tok):
            htok[t] = V.tt(h[:, t, :], h[:, t, :], b[:, 0:T], ADD, tok, htok[t])
            return [htok[t]]

        run(linear(d["w_out"], 16, 16, lambda kc: cat[:, kc, :], lambda kc: ct[kc], ev_res))
        barrier()

        top[0] = base
        hn = alloc(16, T)
        fa = alloc(44, T)
        cvs = Pool([alloc(2, T) for _ in range(4)])
        tn = rms(hchunks, htok, ("ffn_norm_w", 0), [hn[:, i, :] for i in range(16)], D, 1e-6)
        nrhs = lambda kc: hn[:, kc, :]
        ntok = lambda kc: tn[kc]
        ftok, gbuf = {}, {}

        def ev_conv(t, b, tok):
            j, val = t // 2, t % 2
            i = j + 44 * val
            if not val:
                gbuf[j] = cvs.take()
            cb, cf = gbuf[j]
            s = cb[:, val, :]
            ps = b[:, 0:T]
            t0 = A.act(s, ps, ACT.Identity, tok, *cf, bias=W("ffn_conv_b", i), scale=W("cw2", i))
            t1 = V.stt(s[:, 1:T], ps[:, 0:T - 1], W("cw1", i), s[:, 1:T], MUL, ADD, t0)
            t1 = V.stt(s[:, 2:T], ps[:, 0:T - 2], W("cw0", i), s[:, 2:T], MUL, ADD, t1)
            if not val:
                gbuf[(j, "t")] = A.act(s, s, ACT.Silu, t1)
            else:
                ftok[j] = G.tt(fa[:, j, :], cb[:, 0, :], s, MUL, t1, gbuf[(j, "t")])
                cvs.give(cb, ftok[j])
            return [t1]

        run(linear(d["w_up"], 88, 16, nrhs, ntok, ev_conv))
        run(linear(d["w_down"], 16, 44, lambda kc: fa[:, kc, :], lambda kc: ftok[kc], ev_res))
        tf = rms(hchunks, htok, ("final_norm_w", 0), hchunks, D, 1e-6)
        htok = list(tf)

        barrier()
        top[0] = base
        hn = alloc(16, T)
        tn = rms(hchunks, htok, ("norm1_g_2", 0), [hn[:, i, :] for i in range(16)], D, 1e-6)
        ntok = lambda kc: tn[kc]
        nrhs = lambda kc: hn[:, kc, :]
        yss = alloc(16, T)
        mark = top[0]
        z = yss
        bc = alloc(8, T)
        xs = alloc(2, T)
        xd = alloc(2, 2048)
        dt_, da_, cs_ = alloc(T), alloc(T), alloc(T)
        dtmp = [alloc(T) for _ in range(4)]
        dtT = alloc(2, 32)
        csT = alloc(2, 32)
        cbm = alloc(4, 384)
        sw = Pool([alloc(384) for _ in range(4)])
        cvs = Pool([alloc(T) for _ in range(4)])
        ztok, xtok, bctok, xdtok = {}, {}, {}, {}
        st = {}

        def ev_z(t, b, tok):
            r = ztok[t] = A.act(z[:, t, :], b[:, 0:T], ACT.Silu, tok)
            return [r]

        def ev_dt(t, b, tok):
            R = slice(0, 32)
            a, e, w, p = (q[R, :] for q in dtmp)
            bi = W("dtb")[R, :]
            t0 = V.ts(a, b[R, 0:T], bi, None, ADD, None, tok)
            t = V.ts(w, a, -1.0, None, MUL, None, t0)
            t = V.tt(w, w, a, MIN, t)
            t = A.act(e, w, ACT.Exp, t)
            t = V.ts(w, e, 2.0, None, ADD, None, t)
            t = V.recip(w, w, t)
            t = V.tt(e, e, w, MUL, t)
            t = V.tt(w, e, e, MUL, t)
            cf = [1.0 / (2 * k + 1) for k in range(10)]
            t = V.ts(p, w, cf[9], cf[8], MUL, ADD, t)
            for k in range(7, -1, -1):
                t = V.tt(p, p, w, MUL, t)
                t = V.ts(p, p, cf[k], None, ADD, None, t)
            t = V.stt(p, e, 2.0, p, MUL, MUL, t)
            t = V.stt(dt_[R, :], a, 0.0, p, MAX, ADD, t)
            ta = A.act(sm2[R, :], W("alog")[R, :], ACT.Exp)
            t = V.ts(sm2[R, :], sm2[R, :], -1.0, None, MUL, None, ta, t)
            t = V.ts(da_[R, :], dt_[R, :], sm2[R, :], None, MUL, None, t)
            tcs = V.scan(cs_[R, :], C("ones", 0, 1)[R, :].broadcast_to([32, T]), da_[R, :], t)
            st["cs"] = tcs
            b2, free = PS.take()
            bk = banks[b2]
            for hf in range(2):
                P.tp(bk[:, hf * 32:hf * 32 + 32], dt_[R, hf * 128:(hf + 1) * 128], ident[R, 0:32], tcs, *free)
                tm = P.tp(bk[:, 64 + hf * 32:96 + hf * 32], cs_[R, hf * 128:(hf + 1) * 128], ident[R, 0:32],
                          tcs, sig=True)
            r = V.copy(dtT, bk[:, 0:64].rearrange("p (a b) -> p a b", a=2), tm)
            st["csT"] = V.copy(csT, bk[:, 64:128].rearrange("p (a b) -> p a b", a=2), tm)
            st["dtT"] = r
            PS.give(b2, r, st["csT"])
            return [t0]

        sm2 = alloc(1)

        def conv4(dst, ps, i, tok, *needs):
            s, cf = cvs.take()
            t = A.act(s, ps, ACT.Identity, tok, *cf, bias=W("ssd_conv_b_2", i), scale=W("dw3", i))
            for sh, nm in ((1, "dw2"), (2, "dw1"), (3, "dw0")):
                t = V.stt(s[:, sh:T], ps[:, 0:T - sh], W(nm, i), s[:, sh:T], MUL, ADD, t)
            r = A.act(dst, s, ACT.Silu, t, *needs)
            cvs.give(s, r)
            return t, r

        xfree = [[], []]
        xT = alloc(16, T)

        def ev_bc(t, b, tok):
            t1, bctok[t - 16] = conv4(bc[:, t - 16, :], b[:, 0:T], t, tok)
            return [t1]

        def ev_x(t, b, tok):
            t1, r = conv4(xT[:, t, :], b[:, 0:T], t, tok)
            xtok[t] = r
            b2, free = PS.take()
            for hf in range(2):
                tm = P.tp(banks[b2][:, hf * 128:(hf + 1) * 128], xT[:, t, hf * 128:(hf + 1) * 128], ident, r,
                          *free, sig=True)
            for hf in range(2):
                dtb = dtT[:, hf, 2 * t:2 * t + 2].unsqueeze(2).broadcast_to([128, 2, 64])
                xdtok[t] = V.tt(xd[:, hf, t * 128:(t + 1) * 128].rearrange("p (a b) -> p a b", a=2),
                                banks[b2][:, hf * 128:(hf + 1) * 128].rearrange("p (a b) -> p a b", a=2),
                                dtb, MUL, tm, st["dtT"])
            PS.give(b2, xdtok[t])
            return [t1]

        run(chain(linear(d["w_dt"], 1, 16, nrhs, ntok, ev_dt, M=32),
                  linear(d["w_xbc"], 8, 16, nrhs, ntok, ev_bc, t0=16),
                  linear(d["w_xbc"], 16, 16, nrhs, ntok, ev_x),
                  linear(d["w_z"], 16, 16, nrhs, ntok, ev_z)))

        cbt = {}
        for g in range(4):
            b, free = PS.take()
            P.mm(banks[b][:, 0:256], bc[:, g, 0:128], bc[:, 4 + g, :], True, True, bctok[g], bctok[4 + g],
                 *free)
            tm = P.mm(banks[b][:, 256:384], bc[:, g, 128:256], bc[:, 4 + g, 128:256], True, True, sig=True)
            V.tt(cbm[:, g, 0:256], banks[b][:, 0:256], C("cm"), MUL, tm)
            cbt[g] = V.tt(cbm[:, g, 256:384], banks[b][:, 256:384], C("cm", 0, 128), MUL)
            PS.give(b, cbt[g])
        ysst = {}

        def ssd_pair(i):
            yb, yfree = PS.take()
            last = []
            for e in range(2):
                hd = 2 * i + e
                g = hd // 8
                b, free = PS.take()
                sel = ident[0:32, hd:hd + 1].broadcast_to([32, 128])
                tm = P.mm(banks[b][:, 0:T], sel, cs_[0:32, :], True, True, st["cs"], *free, sig=True)
                w, wf = sw.take()
                yield
                V.ts(w[:, 0:256], banks[b][:, 0:T], csT[:, 0, hd:hd + 1], 0.0, SUB, MIN, tm, st["csT"], *wf)
                t = V.ts(w[:, 256:384], banks[b][:, 128:T], csT[:, 1, hd:hd + 1], 0.0, SUB, MIN)
                PS.give(b, t)
                t = A.act(w, w, ACT.Exp, t)
                yield
                t = V.tt(w, w, cbm[:, g, :], MUL, t, cbt[g])
                yield
                R = slice(64 * e, 64 * e + 64)
                P.mm(banks[yb][R, 0:256], xd[:, 0, hd * 64:hd * 64 + 64], w[:, 0:256], True, False, t,
                     xdtok[i], *yfree)
                tm = P.mm(banks[yb][R, 128:256], xd[:, 1, hd * 64:hd * 64 + 64], w[:, 256:384], False, True,
                          sig=True)
                sw.give(w, tm)
            yield
            s, sf = scr.take()
            t = V.stt(s, xT[:, i, :], W("dskip", i), banks[yb][:, 0:T], MUL, ADD, tm, *sf)
            PS.give(yb, t)
            ysst[i] = V.tt(z[:, i, :], s, z[:, i, :], MUL, t, ztok[i])
            scr.give(s, ysst[i])

        run(flight(ssd_pair, 16, 2))
        for g in range(4):
            rms([z[:, 4 * g + i, :] for i in range(4)], [ysst[4 * g + i] for i in range(4)],
                ("ssd_norm_g_2", 4 * g), [yss[:, 4 * g + i, :] for i in range(4)], 512, 1e-5)
        barrier()

        A.wait(V.now(), A.now(), G.now(), P.now())
        sv = [sem("s_hsave"), sem("s_ysave")]
        A.items.append(lambda e: e.dma_start(d["hsave"], h).then_inc(sv[0], 16))
        A.items.append(lambda e: e.dma_start(d["ysave"], yss).then_inc(sv[1], 16))
        hst = [(sv[0], 16), (sv[1], 16)]
        top[0] = mark
        kk_, vv = alloc(16, T), alloc(16, T)
        AR = alloc(16, 2, 2, 128)
        bb = h
        gd = alloc(2, T)
        wd, ad = alloc(T), alloc(T)
        PL = alloc(16, 8)
        p33 = Pool([alloc(8, 33) for _ in range(2)])
        shp = Pool([alloc(T) for _ in range(3)])
        w2s = hn[:, 0:8, :].rearrange("p a b -> p (a b)")
        a2s = hn[:, 8:16, :].rearrange("p a b -> p (a b)")
        ktk, vtk, rtk = {}, {}, {}

        def shift(dst, b, mu, R, tok, *needs):
            n = R.stop
            s, sf = shp.take()
            v = b[R, 0:T]
            s, ss = s[R, :], s
            t0 = A.act(ss[R, :], v, ACT.Copy, tok, *sf)
            dd, df = scr.take()
            t1 = V.tt(dd[R, 1:T], s[:, 0:T - 1], v[:, 1:T], SUB, t0, *df)
            t2 = V.ts(dd[R, 0:1], s[:, 0:1], -1.0, None, MUL, None, t0)
            if len(dst.shape) == 3:
                t = V.stt(dst, dd[R, :].rearrange("p (a b) -> p a b", a=2), mu,
                          s.rearrange("p (a b) -> p a b", a=2), MUL, ADD, t1, t2, *needs)
            else:
                t = V.stt(dst, dd[R, :], mu, s, MUL, ADD, t1, t2, *needs)
            scr.give(dd, t)
            shp.give(ss, t)
            return t

        FULL = slice(0, 128)

        def ev_r(t, b, tok):
            rtk[t] = shift(AR[:, t, :, 1, :], b, W("mu_r", t), FULL, tok)
            return [rtk[t]]

        def ev_kk(t, b, tok):
            ktk[t] = shift(kk_[:, t, :], b, W("mu_k", t), FULL, tok)
            return [ktk[t]]

        def ev_vv(t, b, tok):
            vtk[t] = shift(vv[:, t, :], b, W("mu_v", t), FULL, tok)
            return [vtk[t]]

        small = {}

        def ev_wd(t, b, tok):
            R = slice(0, 96)
            r = shift(wd[R, :], b, W("mu_wd")[R, :], R, tok)
            small["wd"] = A.act(wd[R, :], wd[R, :], ACT.Tanh, r)
            return [r]

        def ev_ad(t, b, tok):
            R = slice(0, 96)
            small["ad"] = shift(ad[R, :], b, W("mu_ad")[R, :], R, tok)
            return [small["ad"]]

        def ev_gd(t, b, tok):
            r = shift(gd[:, t, :], b, W("mu_gd", t), FULL, tok)
            small["gd"] = A.act(gd[:, t, :], gd[:, t, :], ACT.Sigmoid, r)
            return [r]

        def prep(i):
            b, free = PS.take()
            P.mm(banks[b][:, 0:T], w2s[0:96, i * 128:(i + 1) * 128], wd[0:96, :], True, True, small["wd"],
                 *free)
            tm = P.mm(banks[b][:, T:2 * T], a2s[0:96, i * 128:(i + 1) * 128], ad[0:96, :], True, True,
                      small["ad"], sig=True)
            s1, f1 = scr.take()
            s2, f2 = scr.take()
            s3, f3 = scr.take()
            yield
            tsg = A.act(s1, banks[b][:, 0:T], ACT.Sigmoid, tm, *f1, bias=W("rwkv_w0_2", i))
            ta = A.act(s2, banks[b][:, T:2 * T], ACT.Sigmoid, tm, *f2, bias=W("rwkv_a0_2", i))
            PS.give(b, tsg, ta)
            t = V.ts(s1, s1, -math.exp(-0.5), None, MUL, None, tsg)
            tcm = V.scan(s3, C("rm"), s1, t, *f3)
            pb, pf = p33.take()
            c3 = s3.rearrange("p (a b) -> p a b", b=32)
            t = V.mset(pb[:, :, 0:1], 1.0, *pf)
            tp_ = A.act(pb[:, :, 1:33], c3, ACT.Exp, tcm, *pf)
            tip = A.act(s3, s3, ACT.Exp, tp_, scale=-1.0)
            yield
            tpl = V.copy(PL[:, i, :].unsqueeze(2), pb[:, :, 32:33], tp_)
            kk = s1
            t = V.ts(kk, kk_[:, i, :], W("rwkv_k_k_2", i), None, MUL, None, ktk[i], tcm)
            s4, f4 = scr.take()
            t4 = A.act(s4, kk, ACT.Square, t, *f4)
            b, free = PS.take()
            tm = P.mm(banks[b][:, 0:T], blk, s4, True, True, t4, *free, sig=True)
            t5 = V.ts(s4, s2, -1.0, W("rwkv_k_a_2", i), ADD, MUL, ta, tm)
            t5 = V.stt(s4, s4, 1.0, kk_[:, i, :], ADD, MUL, t5)
            tkf = V.tt(kk_[:, i, :], s4, s3, MUL, t5, tip)
            yield
            t = V.ts(s4, banks[b][:, 0:T], 1e-24, None, MAX, None, tm, tkf)
            PS.give(b, t)
            t = V.recip(s4, s4, t)
            t = A.act(s4, s4, ACT.Sqrt, t)
            yield
            t = V.tt(kk, kk, s4, MUL, t)
            pp = pb[:, :, 0:32].rearrange("p (s a) b -> p s a b", s=2)
            k4 = kk.rearrange("p (s a b) -> p s a b", s=2, b=32)
            ta2 = V.stt(AR[:, i, :, 0, :].rearrange("p s (a b) -> p s a b", b=32), k4, -1.0, pp, MUL, MUL, t)
            tb1 = V.tt(kk, kk, s2, MUL, ta2)
            tb2 = V.tt(bb[:, i, :], kk, s3, MUL, tb1)
            r4 = AR[:, i, :, 1, :].rearrange("p s (a b) -> p s a b", b=32)
            tr2 = V.tt(r4, r4, pb[:, :, 1:33].rearrange("p (s a) b -> p s a b", s=2), MUL, rtk[i], tp_)
            p33.give(pb, tr2)
            for x in (s1, s2, s3, s4):
                scr.give(x, tr2, tb2)
            ptk[i] = tr2

        ptk = {}
        run(chain(linear(d["w_wd"], 1, 16, nrhs, ntok, ev_wd, M=96),
                  linear(d["w_ad"], 1, 16, nrhs, ntok, ev_ad, M=96),
                  linear(d["w_gd"], 2, 16, nrhs, ntok, ev_gd),
                  linear(d["w_k"], 16, 16, nrhs, ntok, ev_kk),
                  linear(d["w_r"], 16, 16, nrhs, ntok, ev_r),
                  linear(d["w_v"], 16, 16, nrhs, ntok, ev_vv)))
        tl = [load(w2s[0:96, :], d["w2"], *[q.now() for q in ENG], hst, q=A),
              load(a2s[0:96, :], d["a2"], q=A)]
        for q in ENG:
            q.wait(tl)
            q.wait(hst)
        run(flight(prep, 16, 1))
        barrier()

        XA = yss[:, 0:8, :].rearrange("p (s t) b -> p s (t b)", s=2).rearrange(
            "p s (t g) -> p s t g", g=32)
        XB = yss[:, 8:16, :].rearrange("p (s t) b -> p s (t b)", s=2).rearrange(
            "p s (t g) -> p s t g", g=32)
        XX = hn[:, 0:8, :].rearrange("p (s t) b -> p s (t b)", s=2).rearrange(
            "p s (t g) -> p s t g", g=32)
        XT = hn[:, 8:16, :].rearrange("p (s t) b -> p s (t b)", s=2).rearrange(
            "p s (t g) -> p s t g", g=32)
        s32 = C("s32")
        ta_ = None
        for hf in range(2):
            for i in range(0, 16, 4):
                bks = [PS.take() for _ in range(2)]
                for j in range(4):
                    for e in range(2):
                        R = slice(64 * e, 64 * e + 64)
                        tm = P.mm(banks[bks[e][0]][:, j * 128:(j + 1) * 128],
                                  bb[R, i + j, hf * 128:(hf + 1) * 128], AR[R, i + j, hf, 0, :], True, True,
                                  ptk[i + j], *bks[e][1], sig=True)
                for e in range(2):
                    bk = banks[bks[e][0]][:, :].rearrange("p (j t) -> p t j", j=4)
                    for c in range(4):
                        Q = slice(32 * c, 32 * c + 32)
                        ta_ = V.tt(XA[Q, hf, :, 2 * i + e:2 * i + 8:2], bk[Q, 32 * c:32 * c + 32, :],
                                   s32[Q, :].unsqueeze(2).broadcast_to([32, 32, 4]), MUL, tm)
                    PS.give(bks[e][0], ta_)
        t = ta_
        for hf in range(2):
            t = V.tr(XB[:, hf, :, :].rearrange("p t g -> p (t g)"),
                     XA[:, hf, :, :].rearrange("p t g -> p (t g)"), t)
        t = V.mset(XX, 0.0, t)
        t = V.mset(XX[:, :, :, :].rearrange("p s t g -> p s (t g)")[:, :, 0:1024:33], 1.0, t)
        for r in range(1, 32):
            prod = XA.rearrange("p s t g -> p (s t g)")[:, 0:2 * r * r].rearrange(
                "p (s j k) -> p s j k", s=2, j=r)
            a4 = XB[:, :, r, 0:r].unsqueeze(2).broadcast_to([128, 2, r, r])
            x4 = XX[:, :, 0:r, 0:r].rearrange("p s k j -> p s j k")
            t = V.tt(prod, a4, x4, MUL, t)
            t = V.red(XX[:, :, r, 0:r], prod, ADD, t)
        for hf in range(2):
            t = V.tr(XT[:, hf, :, :].rearrange("p t g -> p (t g)"),
                     XX[:, hf, :, :].rearrange("p t g -> p (t g)"), t)
        xtt = t
        barrier()

        def alloc_h(*shape):
            n = int(np.prod(shape))
            for blk_, size, at in pools_:
                if at[0] + n <= size:
                    v = blk_[:, at[0]:at[0] + n]
                    at[0] += n
                    if len(shape) == 2:
                        v = v.rearrange("p (a b) -> p a b", b=shape[1])
                    return v
            raise AssertionError("no room")

        pools_ = [(yss.rearrange("p a b -> p (a b)"), 4096, [0]),
                  (hn[:, 0:8, :].rearrange("p a b -> p (a b)"), 2048, [0]),
                  (arena[:, top[0]:NARENA], NARENA - top[0], [0])]
        DEP = 2
        tokb = Pool([alloc_h(4, 128) for _ in range(DEP)])
        mskb = Pool([alloc_h(3, 128) for _ in range(2 * DEP)])
        bx = Pool([alloc_h(4, 128) for _ in range(DEP)])
        kx = Pool([alloc_h(4, 128) for _ in range(DEP)])
        gt = Pool([alloc_h(4, 128) for _ in range(DEP)])
        wu = Pool([alloc_h(256) for _ in range(DEP)])
        az = Pool([alloc_h(128) for _ in range(DEP)])
        qt = Pool([alloc_h(128) for _ in range(DEP)])
        xbd = Pool([w_ for w_ in (alloc_h(128), alloc_h(128))])
        sbd = Pool([alloc_h(128) for _ in range(2 * DEP)])
        yb_ = Pool([alloc_h(256) for _ in range(DEP)])
        tz = []
        for p_ in (gt, sbd):
            for v, _ in list(p_.free):
                tz.append(G.mset(v, 0.0))
        tzz = tz[-1]
        for q in ENG:
            q.wait(tzz)
        m3 = C("m3")
        bm = C("bm")
        vtk2 = {}

        def block(i, hf, state):
            TS = slice(hf * 128, (hf + 1) * 128)
            b, free = PS.take()
            bk = banks[b]
            P.tp(bk[:, 0:128], AR[:, i, hf, 0, :], ident, *free)
            P.tp(bk[:, 128:256], bb[:, i, TS], ident)
            P.tp(bk[:, 256:384], kk_[:, i, TS], ident)
            tm = P.tp(bk[:, 384:512], vv[:, i, TS], ident, sig=True)
            tk, tf_ = tokb.take()
            tt_ = A.act(tk.rearrange("p a b -> p (a b)"), bk[:, :], ACT.Copy, tm, *tf_)
            PS.give(b, tt_)
            yield
            mks = []
            for e in range(2):
                R = slice(64 * e, 64 * e + 64)
                b, free = PS.take()
                P.mm(banks[b][:, 0:128], bb[R, i, TS], AR[R, i, hf, 1, :], True, True, *free)
                tm = P.mm(banks[b][:, 128:384], kk_[R, i, TS], AR[R, i, hf, :, :].rearrange(
                    "p a b -> p (a b)"), True, True, sig=True)
                mk, mf = mskb.take()
                t = V.tt(mk.rearrange("p a b -> p (a b)"), banks[b][:, 0:384], m3, MUL, tm, *mf)
                PS.give(b, t)
                mks.append((mk, t))
                yield
            bxb, bf = bx.take()
            kxb, kf_ = kx.take()
            m4 = C("bm4").unsqueeze(2).broadcast_to([128, 4, 128])
            tbx = G.tt(bxb, tk[:, 1, :].unsqueeze(1).broadcast_to([128, 4, 128]), m4, MUL, tt_, *bf)
            tkx = G.tt(kxb, tk[:, 2, :].unsqueeze(1).broadcast_to([128, 4, 128]), m4, MUL, tt_, *kf_)
            b, free = PS.take()
            for e in range(2):
                tm = P.mm(banks[b][:, 64 * e:64 * e + 64], mks[e][0][:, 1, :], tk[:, 3, 64 * e:64 * e + 64],
                          True, True, mks[e][1], tt_, *free, sig=True)
            azb, af = az.take()
            taz = V.copy(azb, banks[b][:, 0:128], tm, *af)
            PS.give(b, taz)
            yield
            b, free = PS.take()
            for e in range(2):
                hd = 2 * i + e
                xb, xf = xbd.take()
                tx = V.tt(xb.rearrange("p (c t) -> p c t", c=4),
                          XT[:, hf, :, hd].unsqueeze(1).broadcast_to([128, 4, 32]),
                          bm.rearrange("p (c t) -> p c t", c=4), MUL, *xf)
                P.mm(banks[b][:, 64 * e:64 * e + 64], xb, tk[:, 0, 64 * e:64 * e + 64], True, True, tx, *free)
                tm = P.mm(banks[b][:, 128 + 64 * e:192 + 64 * e], xb, azb[:, 64 * e:64 * e + 64], True, True,
                          taz, sig=True)
                xbd.give(xb, tm)
            az.give(azb, tm)
            wub, wf = wu.take()
            twu = V.copy(wub, banks[b][:, 0:256], tm, *wf)
            PS.give(b, twu)
            yield
            b, free = PS.take()
            for e in range(2):
                R = slice(64 * e, 64 * e + 64)
                tm = P.mm(banks[b][R, 0:128], wub[:, 64 * e:64 * e + 64], mks[e][0][:, 0, :], True, True, twu,
                          *free, sig=True)
            qb, qf = qt.take()
            tq = V.tt(qb, banks[b][:, 0:128], AR[:, i, hf, 1, :], ADD, tm, *qf)
            PS.give(b, tq)
            yb, yfree = PS.take()
            for e in range(2):
                R = slice(64 * e, 64 * e + 64)
                P.mm(banks[yb][R, 0:128], wub[:, 128 + 64 * e:192 + 64 * e], mks[e][0][:, 0, :], True, False,
                     twu, *yfree)
                tm = P.mm(banks[yb][R, 0:128], tk[:, 3, 64 * e:64 * e + 64], mks[e][0][:, 2, :], False, True,
                          sig=True)
            for e in range(2):
                mskb.give(mks[e][0], tm)
            ybuf, ybf = state["y"]
            ty0 = A.act(ybuf[:, TS], banks[yb][:, 0:128], ACT.Copy, tm, *ybf)
            PS.give(yb, ty0)
            yield
            b, free = PS.take()
            tm = P.mm(banks[b][:, :], wub[:, 0:128], bxb.rearrange("p c k -> p (c k)"), True, True, tbx, twu,
                      *free, sig=True)
            gb, gf = gt.take()
            for e in range(2):
                R = slice(64 * e, 64 * e + 64)
                ii = ident[R, 64 * e:64 * e + 64].unsqueeze(1).broadcast_to([64, 4, 64])
                tg = V.tt(gb[R, :, 64 * e:64 * e + 64],
                          banks[b][R, :].rearrange("p (c k) -> p c k", c=4)[:, :, 64 * e:64 * e + 64], ii,
                          ADD, tm, *gf)
            PS.give(b, tg)
            yield
            yb, yfree = PS.take()
            for c in range(4):
                sb_, stok = state["s"]
                ty = P.mm(banks[yb][:, 32 * c:32 * c + 32], sb_, qb[:, 32 * c:32 * c + 32], True, True, stok,
                          tq, *(yfree if c == 0 else []), sig=True)
                b, free = PS.take()
                P.mm(banks[b][:, 0:128], bxb[:, c, :], wub[:, 128:256], True, False, tbx, twu, *free)
                P.mm(banks[b][:, 0:128], kxb[:, c, :], tk[:, 3, :], False, False, tkx)
                tm = P.mm(banks[b][:, 0:128], gb[:, c, :], sb_, False, True, tg, stok, sig=True)
                sbd.give(sb_, tm)
                sn, sf = sbd.take()
                ch = hf * 4 + c
                for e in range(2):
                    R = slice(64 * e, 64 * e + 64)
                    CS = slice(64 * e, 64 * e + 64)
                    if e == 0:
                        ts_a = V.ts(sn[R, CS], banks[b][R, CS], PL[R, i, ch:ch + 1], None, MUL, None, tm, *sf)
                    else:
                        ts_b = A.act(sn[R, CS], banks[b][R, CS], ACT.Copy, tm, *sf,
                                     scale=PL[R, i, ch:ch + 1])
                PS.give(b, ts_a, ts_b)
                state["s"] = (sn, [ts_a, ts_b])
                yield
            tokb.give(tk, tm)
            bx.give(bxb, tm)
            kx.give(kxb, tm)
            gt.give(gb, tm)
            wu.give(wub, tm)
            qt.give(qb, ty)
            ty2 = V.tt(ybuf[:, TS], ybuf[:, TS], banks[yb][:, 0:128], ADD, ty, ty0)
            PS.give(yb, ty2)
            state["yt"].append(ty2)
            yield

        def pair(i):
            state = {"y": yb_.take(), "yt": []}
            sb0, sf0 = sbd.take()
            tz_ = V.mset(sb0, 0.0, *sf0)
            state["s"] = (sb0, [tz_])
            for hf in range(2):
                yield from block(i, hf, state)
            sb_, stok = state["s"]
            sbd.give(sb_, *stok)
            yb = state["y"][0]
            b, free = PS.take()
            tm = P.mm(banks[b][:, 0:T], blk, yb, True, True, *state["yt"], *free, sig=True)
            s1, f1 = scr.take()
            t = V.stt(s1, banks[b][:, 0:T], -1.0 / 64, yb, MUL, ADD, tm, *f1)
            PS.give(b, t)
            s2, f2 = scr.take()
            t2 = A.act(s2, s1, ACT.Square, t, *f2)
            b, free = PS.take()
            tm = P.mm(banks[b][:, 0:T], blk, s2, True, True, t2, *free, sig=True)
            yield
            rk = yb.rearrange("p (a b) -> p a b", a=2)
            t = V.stt(rk, AR[:, i, :, 1, :], W("rwkv_r_k_2", i),
                      kk_[:, i, :].rearrange("p (a b) -> p a b", a=2), MUL, MUL, t)
            t = V.ts(s2, banks[b][:, 0:T], 1.0 / 64, 64e-5, MUL, ADD, tm)
            PS.give(b, t)
            b, free = PS.take()
            tb = P.mm(banks[b][:, 0:T], blk, yb, True, True, t, *free, sig=True)
            t = V.recip(s2, s2, t)
            t = A.act(s2, s2, ACT.Sqrt, t)
            yield
            t = V.tt(s1, s1, s2, MUL, t)
            t = V.ts(s1, s1, W("rwkv_gn_w_2", i), W("rwkv_gn_b_2", i), MUL, ADD, t)
            t3 = V.tt(s2, banks[b][:, 0:T], vv[:, i, :], MUL, tb, t)
            PS.give(b, t3)
            vtk2[i] = V.tt(vv[:, i, :], s1, s2, ADD, t3)
            yb_.give(yb, vtk2[i])
            scr.give(s1, vtk2[i])
            scr.give(s2, vtk2[i])

        run(flight(pair, 16, DEP))

        def ev_g(t, b, tok):
            vtk2[t] = V.tt(vv[:, t, :], vv[:, t, :], b[:, 0:T], MUL, tok, vtk2[t])
            return [vtk2[t]]

        run(linear(d["w_g2"], 16, 2, lambda kc: gd[:, kc, :], lambda kc: small["gd"], ev_g))
        barrier()
        tl = load(h, d["hsave"], *[q.now() for q in ENG], q=A)
        tl2 = load(yss, d["ysave"], q=A)
        htok = [tl] * 16

        def ev_res2(t, b, tok):
            htok[t] = V.tt(h[:, t, :], h[:, t, :], b[:, 0:T], ADD, tok, htok[t])
            return [htok[t]]

        run(linear(d["w_out2"], 16, 32, lambda kc: yss[:, kc, :] if kc < 16 else vv[:, kc - 16, :],
                   lambda kc: tl2, ev_res2))
        barrier()
        top[0] = base
        hn = alloc(16, T)
        fa = alloc(44, T)
        cvs = Pool([alloc(T) for _ in range(4)])
        tn = rms(hchunks, htok, ("norm2_g_2", 0), [hn[:, i, :] for i in range(16)], D, 1e-6)
        nrhs = lambda kc: hn[:, kc, :]
        ntok = lambda kc: tn[kc]

        def ev_gu(t, b, tok):
            j, up = t // 2, t % 2
            if not up:
                s, sf = cvs.take()
                r = A.act(s, b[:, 0:T], ACT.Silu, tok, *sf)
                gbuf[j] = (s, r)
                return [r]
            s, r = gbuf[j]
            ftok[j] = V.tt(fa[:, j, :], s, b[:, 0:T], MUL, tok, r)
            cvs.give(s, ftok[j])
            return [ftok[j]]

        run(linear(d["w_gu"], 88, 16, nrhs, ntok, ev_gu))
        run(linear(d["w_down2"], 16, 44, lambda kc: fa[:, kc, :], lambda kc: ftok[kc], ev_res))
        tf = rms(hchunks, htok, ("norm_f_g_2", 0), hchunks, D, 1e-6)
        for i in range(0, 16, 4):
            S.wait(*tf[i:i + 4])
            S.items.append(lambda e, i=i: e.dma_start(out[:, i:i + 4, :], h[:, i:i + 4, :])
                           .then_inc(st_sem, 16))
            nstore[0] += 1
        S.wait((st_sem, 16 * nstore[0]))

        blockx = ctx.enter_context(nc.Block())

        @blockx.tensor
        def _(e):
            P.replay(e)

        @blockx.vector
        def _(e):
            V.replay(e)

        @blockx.scalar
        def _(e):
            A.replay(e)

        @blockx.gpsimd
        def _(e):
            G.replay(e)

        @blockx.sync
        def _(e):
            S.replay(e)


def constants():
    c = np.zeros((128, NCST), np.float32)

    def put(name, v):
        o, n = CST_AT[name]
        c[:, o:o + n] = v

    p = np.arange(128)
    put("ident", np.eye(128))
    put("ones", 1.0)
    put("blk", p[:, None] // 64 == p[None] // 64)
    perm = np.zeros((128, 128))
    for m in range(128):
        if m % 64 < 32:
            perm[m + 32, m] = -1.0
        else:
            perm[m - 32, m] = 1.0
    put("perm", perm)
    same = p[:, None] // 32 == p[None] // 32
    incl = same & (p[:, None] <= p[None])
    strict = same & (p[:, None] < p[None])
    put("m3", np.concatenate([incl, strict, incl], 1))
    put("s32", (p[:, None] % 32) < np.arange(32)[None])
    put("bm", same)
    put("bm4", p[:, None] // 32 == np.arange(4)[None])
    zc = np.zeros((128, 256), np.float32)
    zc[:, 128:] = np.where(p[None] <= p[:, None], 0.0, np.finfo(np.float32).min)
    put("zc", zc)
    cm = np.ones((128, 256))
    cm[:, 0:128] = p[:, None] <= p[None]
    put("cm", cm)
    put("kp", np.stack([p < 64, p >= 64], 1))
    fr = np.float32(10000.0) ** (-np.arange(0, 64, 2, dtype=np.float32) / np.float32(64))
    put("ifr", fr.astype(np.float32)[p % 32][:, None])
    put("rm", (np.arange(256) % 32 != 0)[None])
    return c


def tiles(w, M=128):
    K, N = w.shape
    return np.ascontiguousarray(w.reshape(K // 128, 128, N // M, M).transpose(2, 1, 0, 3)).reshape(
        N // M, 128, K // 128 * M)


def layout(x):
    f = {}
    cols = lambda a: np.ascontiguousarray(a.reshape(-1, 128).T)

    def padded(a):
        v = np.zeros((128, 1), a.dtype)
        v[:a.size, 0] = a.reshape(-1)
        return v

    vec = np.zeros((128, NVEC), np.float32)

    def put(name, v):
        o, n = VEC_AT[name]
        vec[:, o:o + n] = v

    for n in ("attn_norm_w", "mla_q_norm_w", "mla_kv_norm_w", "ssm_out_norm_w", "mla_out_norm_w",
              "ffn_norm_w", "ffn_conv_b", "final_norm_w", "ssm_d", "ssm_b_glu", "norm1_g_2",
              "ssd_conv_b_2", "ssd_norm_g_2", "rwkv_w0_2", "rwkv_a0_2", "rwkv_k_k_2", "rwkv_k_a_2",
              "rwkv_r_k_2", "rwkv_gn_w_2", "rwkv_gn_b_2", "norm2_g_2", "norm_f_g_2"):
        put(n, cols(x[n]))
    for k in range(3):
        put(f"cw{k}", cols(x["ffn_conv_w"][0, k]))
    for k in range(4):
        put(f"dw{k}", cols(x["ssd_conv_w_2"][0, k]))
    mu = x["rwkv_mu_2"][0]
    put("mu_r", cols(mu[0:2048]))
    put("mu_k", cols(mu[2048:4096]))
    put("mu_v", cols(mu[4096:6144]))
    put("mu_wd", padded(mu[6144:6240]))
    put("mu_ad", padded(mu[6240:6336]))
    put("mu_gd", cols(mu[6336:6592]))
    put("dskip", cols(np.repeat(x["ssd_D_2"][0], 64)))
    put("dtb", padded(x["ssd_dt_bias_2"][0]))
    put("alog", padded(x["ssd_A_log_2"][0]))
    put("lr", x["ssm_lambda_re"][0].reshape(32, 128).T)
    put("li", x["ssm_lambda_im"][0].reshape(32, 128).T)
    put("ldt", np.repeat(x["ssm_log_dt"][0], 64).reshape(32, 128).T)
    f["vec"] = vec
    f["cst"] = constants()
    f["xT"] = np.ascontiguousarray(x["x"][0].T.reshape(16, 128, T).transpose(1, 0, 2))
    f["pos"] = np.ascontiguousarray(x["positions"]).astype(np.int64).view(np.int32).reshape(512)
    for nm, key in (("bre", "ssm_b_re"), ("bim", "ssm_b_im")):
        b = x[key][0].reshape(8, 4, 2, 64, 16)
        v = np.zeros((4, 2, 16, 8, 2, 64), np.float32)
        for g in range(2):
            v[:, g, :, :, g, :] = b[:, :, g].transpose(1, 3, 0, 2)
        f[nm] = v.reshape(128, 8, 128)
    for nm, key in (("cre", "ssm_c_re"), ("cim", "ssm_c_im")):
        c = x[key][0].reshape(32, 2, 16, 64)
        v = np.zeros((2, 64, 32, 2, 16), np.float32)
        for g in range(2):
            v[g, :, :, g, :] = c[:, g].transpose(2, 0, 1)
        f[nm] = v.reshape(128, 32, 32)
    w = x["w_in"][0]
    f["w_in"] = tiles(w[:, 0:1792])
    f["w_kpe"] = tiles(np.concatenate([w[:, 1792:1856], w[:, 1792:1856]], 1))
    uq = x["mla_w_uq"][0].reshape(512, 8, 192)
    f["w_uq"] = tiles(np.concatenate([uq[:, :, 0:128].reshape(512, 1024),
                                      uq[:, :, 128:192].reshape(512, 512)], 1))
    ukv = x["mla_w_ukv"][0].reshape(256, 8, 256)
    f["w_uk"] = tiles(ukv[:, :, 0:128].reshape(256, 1024))
    f["w_uv"] = np.ascontiguousarray(ukv[:, :, 128:256].reshape(2, 128, 1024).transpose(1, 0, 2)).reshape(128, 2048)
    f["w_glu"] = tiles(x["ssm_w_glu"][0])
    f["w_out"] = tiles(x["w_out"][0])
    up = x["ffn_w_up"][0].reshape(2048, 2, 44, 128).transpose(0, 2, 1, 3).reshape(2048, 2 * FF)
    f["w_up"] = tiles(up)
    f["w_down"] = tiles(x["ffn_w_down"][0])
    w = x["w_in_2"][0]
    f["w_z"] = tiles(w[:, 0:2048])
    f["w_xbc"] = tiles(w[:, 2048:5120])
    f["w_dt"] = tiles(w[:, 5120:5152], 32)
    f["w_r"] = tiles(w[:, 5152:7200])
    f["w_k"] = tiles(w[:, 7200:9248])
    f["w_v"] = tiles(w[:, 9248:11296])
    f["w_wd"] = tiles(w[:, 11296:11392], 96)
    f["w_ad"] = tiles(w[:, 11392:11488], 96)
    f["w_gd"] = tiles(w[:, 11488:11744])
    f["w2"] = np.ascontiguousarray(x["rwkv_w2_2"][0])
    f["a2"] = np.ascontiguousarray(x["rwkv_a2_2"][0])
    f["w_g2"] = tiles(x["rwkv_g2_2"][0])
    f["w_out2"] = tiles(x["w_out_2"][0])
    gu = np.stack([x["w_gate_2"][0].reshape(2048, 44, 128), x["w_up_2"][0].reshape(2048, 44, 128)], 2)
    f["w_gu"] = tiles(gu.reshape(2048, 2 * FF))
    f["w_down2"] = tiles(x["w_down_2"][0])
    return f


def kernel(**inputs):
    import concourse.bacc as _bacc
    from concourse import mybir as _mybir
    from concourse.bass_utils import run_bass_kernel_spmd as _run

    nc = _bacc.Bacc("TRN2", target_bir_lowering=False, num_devices=1)
    x = {k: np.asarray(v) for k, v in inputs.items()}
    arrays, d = {}, {}
    for name, a in layout(x).items():
        a = np.ascontiguousarray(a)
        arrays[f"in_{name}"] = a
        d[name] = nc.dram_tensor(f"in_{name}", a.shape, _mybir.dt.from_np(a.dtype), kind="ExternalInput").ap()
    for n in ("hsave", "ysave"):
        d[n] = nc.dram_tensor(n, (128, 16, T), _mybir.dt.float32, kind="Internal").ap()
    out = nc.dram_tensor("out_0", (128, 16, T), _mybir.dt.float32, kind="ExternalOutput").ap()
    program(nc, d, out)
    r = _run(nc, [arrays], core_ids=[0])
    got = r.results[0]["out_0"]
    return np.ascontiguousarray(got.transpose(1, 0, 2).reshape(2048, T).T)[None]
```

```python
import math
from collections import deque
from contextlib import ExitStack

import numpy as np

import concourse.bass as bass
from concourse import mybir

F32 = mybir.dt.float32
F32R = mybir.dt.float32r
I32 = mybir.dt.int32
ALU = mybir.AluOpType
ACT = mybir.ActivationFunctionType
X = mybir.AxisListType.X
MUL, ADD, SUB, MAX, MIN = ALU.mult, ALU.add, ALU.subtract, ALU.max, ALU.min

T = 256
D = 2048
FF = 5632
NH = 32
RAW = 3
CUT = 4
SLOT = 2048
PIECE = 1024
BASE = 16512
NTOT = 53200
NARENA = NTOT - RAW * SLOT - 2 * CUT * PIECE

CST_COLS = [("ident", 128), ("ones", 128), ("blk", 128), ("perm", 128), ("m3", 384), ("s32", 32),
            ("bm", 128), ("bm4", 4), ("zc", 256), ("cm", 256), ("kp", 2), ("ifr", 1), ("rm", 256)]
VEC_COLS = [("attn_norm_w", 16), ("mla_q_norm_w", 4), ("mla_kv_norm_w", 2), ("ssm_out_norm_w", 8),
            ("mla_out_norm_w", 8), ("ffn_norm_w", 16), ("cw0", 88), ("cw1", 88), ("cw2", 88),
            ("ffn_conv_b", 88), ("final_norm_w", 16), ("ssm_d", 8), ("ssm_b_glu", 8),
            ("norm1_g_2", 16), ("dw0", 24), ("dw1", 24), ("dw2", 24), ("dw3", 24),
            ("ssd_conv_b_2", 24), ("ssd_norm_g_2", 16), ("mu_r", 16), ("mu_k", 16), ("mu_v", 16),
            ("mu_wd", 1), ("mu_ad", 1), ("mu_gd", 2), ("rwkv_w0_2", 16), ("rwkv_a0_2", 16),
            ("rwkv_k_k_2", 16), ("rwkv_k_a_2", 16), ("rwkv_r_k_2", 16), ("rwkv_gn_w_2", 16),
            ("rwkv_gn_b_2", 16), ("norm2_g_2", 16), ("norm_f_g_2", 16), ("dskip", 16),
            ("dtb", 1), ("alog", 1), ("lr", 32), ("li", 32), ("ldt", 32)]


def columns(cols):
    at, out = 0, {}
    for name, n in cols:
        out[name] = (at, n)
        at += n
    return out, at


CST_AT, NCST = columns(CST_COLS)
VEC_AT, NVEC = columns(VEC_COLS)


class Queue:

    def __init__(self, sem):
        self.sem, self.n, self.items, self.seen = sem, 0, [], {}

    def wait(self, *needs):
        for tok in needs:
            if tok is None:
                continue
            if isinstance(tok, list):
                self.wait(*tok)
                continue
            sem, v = tok
            if v > self.seen.get(sem.name, 0):
                self.seen[sem.name] = v
                self.items.append(lambda e, sem=sem, v=v: e.wait_ge(sem, v))

    def put(self, fn, needs, sig=True):
        self.wait(*needs)
        if sig:
            self.n += 1
            sem = self.sem
            self.items.append(lambda e: fn(e).then_inc(sem, 1))
            return (sem, self.n)
        self.items.append(fn)
        return None

    def now(self):
        return (self.sem, self.n)

    def replay(self, e):
        for f in self.items:
            f(e)

    def tt(self, out, a, b, op, *needs):
        return self.put(lambda e: e.tensor_tensor(out, a, b, op), needs)

    def ts(self, out, a, s1, s2, op0, op1, *needs):
        if op1 is None:
            return self.put(lambda e: e.tensor_scalar(out, a, s1, None, op0), needs)
        return self.put(lambda e: e.tensor_scalar(out, a, s1, s2, op0, op1), needs)

    def stt(self, out, a, s, b, op0, op1, *needs):
        return self.put(lambda e: e.scalar_tensor_tensor(out=out, in0=a, scalar=s, in1=b, op0=op0,
                                                         op1=op1), needs)

    def copy(self, out, a, *needs):
        return self.put(lambda e: e.tensor_copy(out, a), needs)

    def recip(self, out, a, *needs):
        return self.put(lambda e: e.reciprocal(out, a), needs)

    def red(self, out, a, op, *needs):
        return self.put(lambda e: e.tensor_reduce(out, a, X, op), needs)

    def scan(self, out, d0, d1, *needs):
        return self.put(lambda e: e.tensor_tensor_scan(out, d0, d1, 0.0, MUL, ADD), needs)

    def tr(self, out, a, *needs):
        return self.put(lambda e: e.transpose(out, a), needs)

    def mset(self, out, v, *needs):
        return self.put(lambda e: e.memset(out, v), needs)

    def act(self, out, a, f, *needs, bias=0.0, scale=1.0, acc=None):
        if acc is not None:
            return self.put(lambda e: e.activation(out, a, f, bias=bias, scale=scale, accum_out=acc), needs)
        return self.put(lambda e: e.activation(out, a, f, bias=bias, scale=scale), needs)

    def mm(self, out, lhsT, rhs, start, stop, *needs, sig=False):
        return self.put(lambda e: e.matmul(out, lhsT, rhs, start=start, stop=stop), needs, sig)

    def tp(self, out, a, ident, *needs, sig=False):
        return self.put(lambda e: e.transpose(out, a, ident), needs, sig)


class Pool:

    def __init__(self, items):
        self.free = deque((x, []) for x in items)

    def take(self):
        return self.free.popleft()

    def give(self, x, *toks):
        self.free.append((x, list(toks)))


def run(*gens):
    live = list(gens)
    while live:
        for g in list(live):
            try:
                next(g)
            except StopIteration:
                live.remove(g)


def flight(make, n, depth):
    live, i = [], 0
    while live or i < n:
        while len(live) < depth and i < n:
            live.append(make(i))
            i += 1
        for g in list(live):
            try:
                next(g)
            except StopIteration:
                live.remove(g)
        yield


def program(nc, d, out):
    with ExitStack() as ctx:
        def sem(name):
            return ctx.enter_context(nc.semaphore(name))

        names = [0]

        def at(o, n, dt=F32):
            names[0] += 1
            assert o % 8 == 0
            return nc.alloc_sbuf_tensor_at(f"m{names[0]}", [128, n], dt, offset=BASE + 4 * o)[:, :]

        raw = at(NARENA, RAW * SLOT)
        cut = [at(NARENA + RAW * SLOT + 2 * c * PIECE, 2 * PIECE, F32R) for c in range(CUT)]
        banks = [ctx.enter_context(nc.psum_tensor(f"bank{i}", [128, 512], F32)) for i in range(8)]
        P, V, A, G, S = (Queue(sem(f"s_{n}")) for n in ("pe", "dve", "act", "pool", "sp"))
        ENG = (P, V, A, G)
        raw_sem = [sem(f"s_raw{i}") for i in range(RAW)]
        st_sem = sem("s_st")
        nload, nstore = [0], [0]

        top = [0]

        def shaped(v, shape):
            if len(shape) == 2:
                v = v.rearrange("p (a b) -> p a b", b=shape[1])
            elif len(shape) == 3:
                v = v.rearrange("p (a b c) -> p a b c", b=shape[1], c=shape[2])
            elif len(shape) == 4:
                v = v.rearrange("p (a b c d) -> p a b c d", b=shape[1], c=shape[2], d=shape[3])
            return v

        def alloc(*shape, dt=F32):
            n = int(np.prod(shape))
            o = top[0]
            top[0] += (n + 7) // 8 * 8
            assert top[0] <= NARENA, top[0]
            return shaped(at(o, n, dt), shape)

        def within(o, *shape, dt=F32):
            return shaped(at(o, int(np.prod(shape)), dt), shape)

        def barrier():
            toks = [q.now() for q in ENG]
            for q in ENG:
                q.wait(*[t for t in toks if t[1]])
            return toks

        def load(dst, src, *needs, q=S):
            q.wait(*needs)
            nload[0] += 1
            sm = sem(f"s_ld{nload[0]}")
            q.items.append(lambda e: e.dma_start(dst, src).then_inc(sm, 16))
            return (sm, 16)

        stream, fetched, used = [], [0], [0]
        raw_free = [[] for _ in range(RAW)]
        cut_free = [[] for _ in range(CUT)]
        cut_tok = {}

        def kpart(KC):
            return max(k for k in range(1, KC + 1) if KC % k == 0 and k * 128 <= SLOT)

        def plan(name, nt, KC, t0=0, k0=0, k1=None):
            w = d[name]
            k1 = KC if k1 is None else k1
            kn = k1 - k0
            kper = kpart(kn)
            if kper == kn:
                tper = SLOT // (kn * 128)
                t = t0
                while t < t0 + nt:
                    m = min(tper, t0 + nt - t)
                    stream.append((name, t, k0, w[t:t + m, :, k0 * 128:k1 * 128].rearrange("m p x -> p m x"),
                                   m * kn * 128))
                    t += m
            else:
                for t in range(t0, t0 + nt):
                    for k in range(k0, k1, kper):
                        stream.append((name, t, k, w[t, :, k * 128:(k + kper) * 128], kper * 128))

        pieces, loaded = [], [0]

        def load_next():
            i = loaded[0]
            loaded[0] += 1
            src, n = stream[i][3:5]
            r = i % RAW
            S.wait(*raw_free[r])
            raw_free[r] = []
            dst = raw[:, r * SLOT:r * SLOT + n]
            sm = raw_sem[r]
            d3 = dst.rearrange("p (m x) -> p m x", m=src.shape[1]) if len(src.shape) == 3 else dst
            S.items.append(lambda e: e.dma_start(d3, src).then_inc(sm, 16))

        def fetch():
            j = fetched[0]
            fetched[0] += 1
            i, o, n = pieces[j]
            while loaded[0] < min(i + RAW, len(stream)):
                load_next()
            r, c = i % RAW, j % CUT
            tok = (raw_sem[r], 16 * (i // RAW + 1))
            src = raw[:, r * SLOT + o:r * SLOT + o + n]
            hi, lo = cut[c][:, 0:n], cut[c][:, PIECE:PIECE + n]
            ta = A.act(hi, src, ACT.Copy, tok, *cut_free[c])
            tv = V.tt(lo, src, hi.bitcast(F32), SUB, ta, tok, *cut_free[c])
            raw_free[r] = [ta, tv]
            cut_tok[j] = [ta, tv]

        def piece(name, t, k, o, ahead=CUT):
            j = used[0]
            used[0] += 1
            i, o_, n = pieces[j]
            assert stream[i][0:3] == (name, t, k) and o == o_, (stream[i][0:3], o_, name, t, k, o)
            while fetched[0] < min(j + ahead, len(pieces)):
                fetch()
            c = j % CUT
            return cut[c][:, 0:n], cut[c][:, PIECE:PIECE + n], c, cut_tok[j]

        plan("w_in", 14, 16)
        plan("w_kpe", 1, 16)
        plan("w_uq", 12, 4)
        plan("w_uk", 8, 2)
        plan("w_uv", 1, 16)
        plan("w_glu", 8, 8)
        plan("w_out", 16, 16)
        for q in range(2):
            plan("w_up", 44, 16, t0=44 * q)
            plan("w_down", 16, 44, k0=22 * q, k1=22 * q + 22)
        plan("w_sm", 4, 16)
        plan("w_xbc", 8, 16, t0=16)
        plan("w_xbc", 16, 16)
        plan("w_z", 16, 16)
        for n in ("w_k", "w_r", "w_v"):
            plan(n, 16, 16)
        plan("w_g2", 16, 2)
        plan("w_out2", 16, 32)
        for q in range(2):
            plan("w_gu", 44, 16, t0=44 * q)
            plan("w_down2", 16, 44, k0=22 * q, k1=22 * q + 22)
        for i, u_ in enumerate(stream):
            for o in range(0, u_[4], PIECE):
                pieces.append((i, o, min(PIECE, u_[4] - o)))
        PS = Pool(range(8))

        def linear(name, nt, KC, rhs, ktok, evac, t0=0, k0=0, k1=None):
            k1 = KC if k1 is None else k1
            kn = k1 - k0
            kper = kpart(kn)
            tper = SLOT // (kn * 128) if kper == kn else 1
            for t in range(t0, t0 + nt):
                j = (t - t0) % tper
                b, free = PS.take()
                ps = banks[b][:, 0:T]
                for kc in range(k0, k1):
                    kk = (kc - k0) % kper
                    w = (j * kper + kk) * 128
                    o = w % PIECE
                    if o == 0:
                        hi, lo, c, tok = piece(name, t - j, kc - kk, w)
                        cur[0] = (hi, lo, c, tok)
                    hi, lo, c, tok = cur[0]
                    xh, xl = rhs(kc)
                    P.mm(ps, hi[:, o:o + 128], xh, kc == k0, False, tok, ktok(kc),
                         *(free if kc == k0 else []))
                    P.mm(ps, hi[:, o:o + 128], xl, False, False)
                    end = o + 128 == hi.shape[1]
                    last = P.mm(ps, lo[:, o:o + 128], xh, False, kc == k1 - 1, sig=end or kc == k1 - 1)
                    if end:
                        cut_free[c] = [last]
                PS.give(b, *evac(t, banks[b], last))
                yield

        cur = [None]

        cst = alloc(NCST)
        vec = alloc(NVEC)
        tc0 = [load(cst, d["cst"]), load(vec, d["vec"])]

        def C(name, a=0, b=None):
            o, n = CST_AT[name]
            return cst[:, o + a:o + (n if b is None else b)]

        def W(name, i=0):
            o, n = VEC_AT[name]
            return vec[:, o + i:o + i + 1]

        def WR(name):
            o, n = VEC_AT[name]
            return vec[:, o:o + n]

        ident, ones, blk = C("ident"), C("ones"), C("blk")
        h = alloc(16, T)
        hl = [load(h[:, i * 4:(i + 1) * 4, :], d["xT"][:, i * 4:(i + 1) * 4, :]) for i in range(4)]
        htok = [hl[i // 4] for i in range(16)]
        scr = Pool([alloc(T) for _ in range(6)])
        ms, rr = alloc(T), alloc(T)
        base = top[0]
        for q in ENG:
            q.wait(tc0)
        norm_free = [[]]

        def cutup(hi, lo, src, q, *needs):
            ta = A.act(hi, src, ACT.Copy, *needs)
            tl = q.tt(lo, src, hi.bitcast(F32), SUB, ta, *needs)
            return [ta, tl]

        def rms(chunks, toks, wname, outs, n, eps):
            b, free = PS.take()
            nk = len(chunks)
            for i in range(nk):
                s, sf = scr.take()
                ta = A.act(s, chunks[i], ACT.Square, toks[i], *sf)
                tm = P.mm(banks[b][:, 0:T], ones, s, i == 0, i == nk - 1, ta, *free, sig=True)
                scr.give(s, tm)
            t = V.ts(ms, banks[b][:, 0:T], 1.0 / n, eps, MUL, ADD, tm, *norm_free[0])
            PS.give(b, t)
            t = V.recip(rr, ms, t)
            t = A.act(rr, rr, ACT.Sqrt, t)
            res = []
            for i in range(nk):
                w = W(wname[0], wname[1] + i)
                if isinstance(outs[i], tuple):
                    s, sf = scr.take()
                    tv = V.stt(s, chunks[i], w, rr, MUL, MUL, t, toks[i], *sf)
                    r = cutup(*outs[i], s, (G, V)[i % 2], tv)
                    scr.give(s, r)
                    res.append(r)
                else:
                    tv = V.stt(outs[i], chunks[i], w, rr, MUL, MUL, t, toks[i])
                    res.append(tv)
            norm_free[0] = [tv]
            return res

        hno = top[0]
        hnr = alloc(2, 16, T, dt=F32R)
        hn_out = [(hnr[:, 0, i, :], hnr[:, 1, i, :]) for i in range(16)]
        hchunks = [h[:, i, :] for i in range(16)]
        tn = rms(hchunks, htok, ("attn_norm_w", 0), hn_out, D, 1e-6)
        ntok = lambda kc: tn[kc]
        nrhs = lambda kc: hn_out[kc]

        u = alloc(8, T)
        cq = alloc(4, T)
        ckv = alloc(2, T)
        kpe = alloc(T)
        utok, cqtok, ckvtok, kpetok = {}, {}, {}, {}

        def ev_in(t, b, tok):
            ps = b[:, 0:T]
            if t < 8:
                r = utok[t] = A.act(u[:, t, :], ps, ACT.Copy, tok)
            elif t < 12:
                r = cqtok[t - 8] = A.act(cq[:, t - 8, :], ps, ACT.Copy, tok)
            else:
                r = ckvtok[t - 12] = A.act(ckv[:, t - 12, :], ps, ACT.Copy, tok)
            return [r]

        def ev_kpe(t, b, tok):
            r = kpetok[0] = A.act(kpe, b[:, 0:T], ACT.Copy, tok)
            return [r]

        s5 = {n: alloc(32) for n in ("dt", "mag", "phi", "kf", "r", "sn", "cs", "sh", "ar", "ai", "den",
                                     "zr", "zi", "t1", "t2")}
        Cw = [alloc(32, 32) for _ in range(2)]
        Bw = [alloc(8, 128) for _ in range(2)]
        tl = [load(Cw[0], d["cre"]), load(Cw[1], d["cim"]), load(Bw[0], d["bre"]), load(Bw[1], d["bim"])]
        for q in ENG:
            q.wait(tl)
        NB = 8
        Cz = Cw
        tabo = top[0]
        tab = [alloc(NB, T) for _ in range(2)]
        ec, es, e1, e2, e3 = (alloc(NB) for _ in range(5))
        tmpA = alloc(NB, 128)

        MAGIC = 12582912.0
        PC = []
        rest = 2 * math.pi
        for bits in (8, 8, 10):
            e = math.floor(math.log2(rest))
            q_ = math.floor(rest / 2.0 ** (e - bits + 1)) * 2.0 ** (e - bits + 1)
            PC.append(q_)
            rest -= q_
        PC.append(float(np.float32(rest)))

        def sincos(ang, kf, r, sn, cs, sh, tok, *needs):
            t = V.ts(kf, ang, 1.0 / (2 * math.pi), MAGIC, MUL, ADD, tok, *needs)
            t = V.ts(kf, kf, MAGIC, None, SUB, None, t)
            t = V.stt(r, kf, -PC[0], ang, MUL, ADD, t)
            for c in PC[1:]:
                t = V.stt(r, kf, -c, r, MUL, ADD, t)
            t = V.ts(r, r, 3.1415925, -3.1415925, MIN, MAX, t)
            ta = A.act(sn, r, ACT.Sin, t)
            tb = A.act(sh, r, ACT.Sin, t, scale=0.5)
            t = V.tt(sh, sh, sh, MUL, tb)
            t = V.ts(cs, sh, -2.0, 1.0, MUL, ADD, t)
            return [ta, t]

        def s5_params():
            k = s5
            t = A.act(k["dt"], WR("ldt"), ACT.Exp)
            t1 = V.tt(k["t1"], WR("lr"), k["dt"], MUL, t)
            t2 = V.tt(k["phi"], WR("li"), k["dt"], MUL, t)
            tm = A.act(k["mag"], k["t1"], ACT.Exp, t1)
            tk = sincos(k["phi"], k["kf"], k["r"], k["sn"], k["cs"], k["sh"], t2)
            yield
            t = V.tt(k["ar"], k["mag"], k["cs"], MUL, tm, *tk)
            t = V.ts(k["ar"], k["ar"], -1.0, None, ADD, None, t)
            ta = V.tt(k["ai"], k["mag"], k["sn"], MUL)
            t = V.tt(k["den"], WR("lr"), WR("lr"), MUL)
            t = V.tt(k["t1"], WR("li"), WR("li"), MUL, tm)
            t = V.tt(k["den"], k["den"], k["t1"], ADD, t)
            t = V.recip(k["den"], k["den"], t)
            t = V.tt(k["t1"], k["ar"], WR("lr"), MUL, t)
            t = V.tt(k["t2"], k["ai"], WR("li"), MUL, ta, t)
            t = V.tt(k["t1"], k["t1"], k["t2"], ADD, t)
            t = V.tt(k["zr"], k["t1"], k["den"], MUL, t)
            t = V.tt(k["t1"], k["ai"], WR("lr"), MUL, t)
            t = V.tt(k["t2"], k["ar"], WR("li"), MUL, t)
            t = V.tt(k["t1"], k["t1"], k["t2"], SUB, t)
            t = V.tt(k["zi"], k["t1"], k["den"], MUL, t)
            yield
            zr = k["zr"].unsqueeze(2).broadcast_to([128, 32, 32])
            zi = k["zi"].unsqueeze(2).broadcast_to([128, 32, 32])
            tmp = tmpA.rearrange("p a b -> p (a b)").rearrange("p (a b) -> p a b", b=32)
            tmp2 = tab[0].rearrange("p a b -> p (a b)")[:, 0:1024].rearrange("p (a b) -> p a b", b=32)
            t = V.tt(tmp, Cw[1], zi, MUL, t)
            t = V.tt(tmp2, Cw[0], zi, MUL, t)
            t = V.tt(Cw[0], Cw[0], zr, MUL, t)
            t = V.tt(Cw[0], Cw[0], tmp, SUB, t)
            t = V.tt(Cw[1], Cw[1], zr, MUL, t)
            t = V.stt(Cw[1], Cw[1], -1.0, tmp2, MUL, SUB, t)
            s5["done"] = t
            yield

        def tables(hf, *needs):
            tc, tsn = tab
            c0 = s5["cs"][:, hf * NB:hf * NB + NB]
            s0 = s5["sn"][:, hf * NB:hf * NB + NB]
            t = V.mset(tc[:, :, 0:1], 1.0, s5["done"], *needs)
            t = V.mset(tsn[:, :, 0:1], 0.0, t)
            t = V.copy(ec, c0, t)
            t = V.copy(es, s0, t)
            n = 1
            while n < T:
                ecb = ec.unsqueeze(2).broadcast_to([128, NB, n])
                esb = es.unsqueeze(2).broadcast_to([128, NB, n])
                a, b = tc[:, :, 0:n], tsn[:, :, 0:n]
                c, s = tc[:, :, n:2 * n], tsn[:, :, n:2 * n]
                tmp = tmpA[:, :, 0:n]
                t = V.tt(c, a, ecb, MUL, t)
                t = V.tt(tmp, b, esb, MUL, t)
                t = V.tt(c, c, tmp, SUB, t)
                yield
                t = V.tt(s, b, ecb, MUL, t)
                t = V.tt(tmp, a, esb, MUL, t)
                t = V.tt(s, s, tmp, ADD, t)
                yield
                n *= 2
                if n < T:
                    t = V.tt(e1, ec, ec, MUL, t)
                    t = V.tt(e2, es, es, MUL, t)
                    t = V.tt(e3, ec, es, MUL, t)
                    t = V.tt(ec, e1, e2, SUB, t)
                    t = V.ts(es, e3, 2.0, None, MUL, None, t)
            s5["tab"] = t

        def chain(*gens):
            for g in gens:
                yield from g

        run(chain(linear("w_in", 14, 16, nrhs, ntok, ev_in),
                  linear("w_kpe", 1, 16, nrhs, ntok, ev_kpe)),
            chain(s5_params(), tables(0)))

        barrier()
        def seq(dct, n):
            return [dct[i] for i in range(n)]

        hn = within(hno, 16, T)
        hno2 = hno + 4096
        cqr = within(hno2, 2, 4, T, dt=F32R)
        ckr = within(hno2 + 2048, 2, 2, T, dt=F32R)
        kz = within(hno2 + 3072, 2, T)
        pt2s = [(within(hno2 + 3584, T), within(hno2 + 3840, T)), (cq[:, 0, :], cq[:, 1, :])]
        y = alloc(8, T)
        ytok = {}
        wz = Pool([(alloc(2, T), alloc(2, T), alloc(2, T)) for _ in range(2)])

        def ssm_tile(hf, c, q, yb, yfree, state):
            j = 4 * c + q
            jj = j - NB * hf
            b, free = PS.take()
            bk = banks[b][:, :].rearrange("p (r t) -> p r t", r=2)
            for r in range(2):
                tm = P.mm(bk[:, r, :], Bw[r][32 * q:32 * q + 32, c, :], u[32 * q:32 * q + 32, c, :],
                          True, True, utok[c], *free, sig=True)
            (wa, wb, wc), wf = wz.take()
            cb = tab[0][:, jj, :].unsqueeze(1).broadcast_to([128, 2, T])
            sb_ = tab[1][:, jj, :].unsqueeze(1).broadcast_to([128, 2, T])
            yield
            ta = V.tt(wa, bk, cb, MUL, tm, s5["tab"], *wf)
            tb = V.tt(wb, bk, sb_, MUL)
            PS.give(b, tb)
            t1 = V.tt(wc[:, 0, :], wa[:, 0, :], wb[:, 1, :], ADD, tb)
            t2 = G.tt(wc[:, 1, :], wa[:, 1, :], wb[:, 0, :], SUB, tb, *wf)
            yield
            mg = s5["mag"][:, j:j + 1].broadcast_to([128, T])
            t1 = V.scan(wa[:, 0, :], mg, wc[:, 0, :], t1, t2)
            t2 = V.scan(wa[:, 1, :], mg, wc[:, 1, :], t2)
            yield
            t3 = V.tt(wb, wa, cb, MUL, t2)
            t4 = G.tt(wc, wa, sb_, MUL, t2, s5["tab"])
            t5 = V.tt(wa[:, 0, :], wb[:, 0, :], wc[:, 1, :], SUB, t3, t4)
            t6 = V.tt(wa[:, 1, :], wb[:, 1, :], wc[:, 0, :], ADD, t3, t4)
            yield
            yp = banks[yb][32 * q:32 * q + 32, 0:T]
            P.mm(yp, Cz[0][:, j, :], wa[:, 0, :], True, False, t5, s5["done"], *yfree)
            tm = P.mm(yp, Cz[1][:, j, :], wa[:, 1, :], False, True, t6, sig=True)
            wz.give((wa, wb, wc), tm)
            state.append(t6)
            state.append(tm)

        def ssm_chunk(hf, c):
            yb, yfree = PS.take()
            st = []
            yield from flight(lambda q: ssm_tile(hf, c, q, yb, yfree, st), 4, 2)
            s, sf = scr.take()
            t = V.stt(s, u[:, c, :], W("ssm_d", c), banks[yb][:, 0:T], MUL, ADD, *st, *sf)
            PS.give(yb, t)
            t = A.act(y[:, c, :], s, ACT.Gelu_apprx_tanh, t)
            scr.give(s, t)
            ytok[c] = t
            s5["last"] = st

        def ssm_half(hf):
            for c in range(2 * hf, 2 * hf + 2):
                yield from ssm_chunk(hf, c)

        def ssm_all():
            for hf in range(4):
                if hf:
                    yield from tables(hf, s5["last"])
                yield from ssm_half(hf)

        cqn = cq
        ckn = ckv
        qn = hn[:, 0:8, :]
        kn = hn[:, 8:16, :]
        qp = alloc(4, T)
        o = h[:, 0:8, :]
        vt = h[:, 8:16, :].rearrange("p (a b) c -> p a (b c)", a=2)
        pos = alloc(T)
        pf_ = alloc(2 * T)
        posi = pf_.bitcast(I32)
        ak, ar_ = pf_[:, 0:T], pf_[:, T:2 * T]
        csn, ssn, ash = (alloc(T) for _ in range(3))
        pt2 = Pool(pt2s)
        sm = alloc(16, 4)
        qtok, qptok, ktok_, vtok, otok = {}, {}, {}, {}, {}

        def mla():
            cqt = rms([cq[:, i, :] for i in range(4)], seq(cqtok, 4), ("mla_q_norm_w", 0),
                      [(cqr[:, 0, i, :], cqr[:, 1, i, :]) for i in range(4)], 512, 1e-6)
            ckt = rms([ckv[:, i, :] for i in range(2)], seq(ckvtok, 2), ("mla_kv_norm_w", 0),
                      [(ckr[:, 0, i, :], ckr[:, 1, i, :]) for i in range(2)], 256, 1e-6)
            yield
            tl = load(posi, d["pos"].partition_broadcast(128), q=A)
            t = V.copy(pos, posi[:, 0:2 * T:2], tl)
            t = V.ts(pos, pos, C("ifr"), None, MUL, None, t)
            tcs = sincos(pos, ak, ar_, ssn, csn, ash, t)
            yield

            def rope(dst, src, tok):
                b, free = PS.take()
                tm = P.mm(banks[b][:, 0:T], C("perm"), src, True, True, tok, *free, sig=True)
                s, sf = scr.take()
                t1 = V.tt(s, banks[b][:, 0:T], ssn, MUL, tm, *tcs, *sf)
                PS.give(b, t1)
                t2 = V.tt(dst, src, csn, MUL, tm, *tcs)
                t = V.tt(dst, dst, s, ADD, t1, t2)
                scr.give(s, t)
                return t

            tk = rope(kpe, kpe, kpetok[0])
            for z in range(2):
                tkz = V.ts(kz[:, z, :], kpe, C("kp", z, z + 1), None, MUL, None, tk)
            yield

            def ev_q(t, b, tok):
                if t < 8:
                    r = qtok[t] = A.act(qn[:, t, :], b[:, 0:T], ACT.Copy, tok)
                    return [r]
                r = A.act(qp[:, t - 8, :], b[:, 0:T], ACT.Copy, tok)
                qptok[t - 8] = rope(qp[:, t - 8, :], qp[:, t - 8, :], r)
                return [r]

            yield from linear("w_uq", 12, 4, lambda kc: (cqr[:, 0, kc, :], cqr[:, 1, kc, :]), lambda kc: cqt[kc], ev_q)

            def ev_k(t, b, tok):
                r = ktok_[t] = A.act(kn[:, t, :], b[:, 0:T], ACT.Copy, tok)
                return [r]

            yield from linear("w_uk", 8, 2, lambda kc: (ckr[:, 0, kc, :], ckr[:, 1, kc, :]), lambda kc: ckt[kc], ev_k)
            pc = [piece("w_uv", 0, 0, 0), piece("w_uv", 0, 0, PIECE, CUT - 1)]
            for hf in range(2):
                HS = slice(hf * 128, (hf + 1) * 128)
                for n in range(2):
                    NS = slice(n * 512, (n + 1) * 512)
                    b, free = PS.take()
                    for k in range(2):
                        hv, lv, c, tok = pc[k]
                        P.mm(banks[b][:, :], ckr[:, 0, k, HS], hv[:, NS], k == 0, False, tok, ckt[k], *free)
                        P.mm(banks[b][:, :], ckr[:, 0, k, HS], lv[:, NS], False, False)
                        tm = P.mm(banks[b][:, :], ckr[:, 1, k, HS], hv[:, NS], False, k == 1, sig=True)
                        cut_free[c] = [tm]
                    r = A.act(vt[:, hf, NS], banks[b][:, :], ACT.Copy, tm)
                    PS.give(b, r)
                    vtok[(hf, n)] = r
                yield

            scale = float((128 + 64) ** -0.5)

            def head(i):
                hd, hf = i // 2, i % 2
                n = 128 * (hf + 1)
                b, free = PS.take()
                sp_ = banks[b][:, 0:n]
                P.mm(sp_, qn[:, hd, hf * 128:(hf + 1) * 128], kn[:, hd, 0:n], True, False,
                     qtok[hd], ktok_[hd], *free)
                tm = P.mm(sp_, qp[:, hd // 2, hf * 128:(hf + 1) * 128], kz[:, hd % 2, 0:n], False, True,
                          qptok[hd // 2], tkz, sig=True)
                (sa, sb_), sf = pt2.take()
                yield
                zc = C("zc", 128 - 128 * hf, 256)
                s4 = sm[:, i, :]
                t = V.stt(sa[:, 0:n], sp_, scale, zc, MUL, ADD, tm, *sf)
                PS.give(b, t)
                t = V.red(s4[:, 0:1], sa[:, 0:n], MAX, t)
                t = V.ts(s4[:, 1:2], s4[:, 0:1], -1.0, None, MUL, None, t)
                t = A.act(sa[:, 0:n], sa[:, 0:n], ACT.Exp, t, bias=s4[:, 1:2], acc=s4[:, 2:3])
                yield
                t = V.recip(s4[:, 3:4], s4[:, 2:3], t)
                t = V.ts(sa[:, 0:n], sa[:, 0:n], s4[:, 3:4], None, MUL, None, t)
                b, free = PS.take()
                for k in range(hf + 1):
                    tm = P.tp(banks[b][:, k * 128:(k + 1) * 128], sa[:, k * 128:(k + 1) * 128], ident,
                              t, *free, sig=True)
                yield
                t = A.act(sb_[:, 0:n], banks[b][:, 0:n], ACT.Copy, tm)
                PS.give(b, t)
                b, free = PS.take()
                for k in range(hf + 1):
                    tm = P.mm(banks[b][:, 0:128], vt[:, k, hd * 128:(hd + 1) * 128],
                              sb_[:, k * 128:(k + 1) * 128], k == 0, k == hf, t, vtok[(k, hd // 4)],
                              *free, sig=True)
                pt2.give((sa, sb_), tm)
                yield
                t = A.act(o[:, hd, hf * 128:(hf + 1) * 128], banks[b][:, 0:128], ACT.Copy, tm)
                PS.give(b, t)
                otok[i] = t

            yield from flight(head, 16, 2)

        run(ssm_all(), mla())

        y2tok = {}
        y2 = u
        barrier()
        yr = within(tabo, 2, 8, T, dt=F32R)
        yct = [cutup(yr[:, 0, i, :], yr[:, 1, i, :], y[:, i, :], (V, G)[i % 2], ytok[i]) for i in range(8)]

        def ev_glu(t, b, tok):
            s, sf = scr.take()
            r = A.act(s, b[:, 0:T], ACT.Sigmoid, tok, *sf, bias=W("ssm_b_glu", t))
            y2tok[t] = V.tt(y2[:, t, :], y[:, t, :], s, MUL, r)
            scr.give(s, y2tok[t])
            return [r]

        run(linear("w_glu", 8, 8, lambda kc: (yr[:, 0, kc, :], yr[:, 1, kc, :]), lambda kc: yct[kc], ev_glu))
        t1 = rms([y2[:, i, :] for i in range(8)], seq(y2tok, 8), ("ssm_out_norm_w", 0),
                 hn_out[0:8], 1024, 1e-6)
        t2 = rms([o[:, i, :] for i in range(8)], [otok[2 * i + 1] for i in range(8)], ("mla_out_norm_w", 0),
                 hn_out[8:16], 1024, 1e-6)
        ct = t1 + t2
        tl = load(h, d["xT"], t2, V.now(), P.now(), A.now(), q=A)
        htok = [tl] * 16

        def ev_res(t, b, tok):
            htok[t] = V.tt(h[:, t, :], h[:, t, :], b[:, 0:T], ADD, tok, htok[t])
            return [htok[t]]

        run(linear("w_out", 16, 16, nrhs, lambda kc: ct[kc], ev_res))
        barrier()

        ffo = base + 2 * 16 * T
        far = within(ffo, 2, 22, T, dt=F32R)
        top[0] = ffo + 2 * 22 * T
        cvs = Pool([alloc(2, T) for _ in range(4)])
        tn = rms(hchunks, htok, ("ffn_norm_w", 0), hn_out, D, 1e-6)
        ftok, gbuf = {}, {}
        fdone = [[]]

        def frhs(kc):
            return far[:, 0, kc % 22, :], far[:, 1, kc % 22, :]

        def ev_conv(t, b, tok):
            j, val = t // 2, t % 2
            i = j + 44 * val
            if not val:
                gbuf[j] = cvs.take()
            cb, cf = gbuf[j]
            s = cb[:, val, :]
            ps = b[:, 0:T]
            t0 = A.act(s, ps, ACT.Identity, tok, *cf, bias=W("ffn_conv_b", i), scale=W("cw2", i))
            t1 = V.stt(s[:, 1:T], ps[:, 0:T - 1], W("cw1", i), s[:, 1:T], MUL, ADD, t0)
            t1 = V.stt(s[:, 2:T], ps[:, 0:T - 2], W("cw0", i), s[:, 2:T], MUL, ADD, t1)
            if not val:
                gbuf[(j, "t")] = A.act(s, s, ACT.Silu, t1)
            else:
                tg = G.tt(s, cb[:, 0, :], s, MUL, t1, gbuf[(j, "t")])
                ftok[j] = cutup(*frhs(j), s, G, tg, *fdone[0])
                cvs.give(cb, ftok[j])
            return [t1]

        for q in range(2):
            run(linear("w_up", 44, 16, nrhs, ntok, ev_conv, t0=44 * q))
            run(linear("w_down", 16, 44, frhs, lambda kc: ftok[kc], ev_res, k0=22 * q, k1=22 * q + 22))
            fdone[0] = [P.now()]
        tf = rms(hchunks, htok, ("final_norm_w", 0), hchunks, D, 1e-6)
        htok = list(tf)

        barrier()
        top[0] = ffo
        tn = rms(hchunks, htok, ("norm1_g_2", 0), hn_out, D, 1e-6)
        sv = [sem("s_hsave"), sem("s_ysave")]
        A.wait(V.now(), A.now(), G.now())
        A.items.append(lambda e: e.dma_start(d["hsave"], h).then_inc(sv[0], 16))
        hst = [(sv[0], 16)]
        gdr = alloc(2, 2, T, dt=F32R)
        wd, ad = alloc(T), alloc(T)
        mark = top[0]
        yss = alloc(16, T)
        z = yss
        bc = alloc(8, T)
        xs = alloc(2, T)
        xd = alloc(2, 2048)
        dt_, da_, cs_ = alloc(T), alloc(T), alloc(T)
        dtmp = [alloc(T) for _ in range(4)]
        dtT = alloc(2, 32)
        csT = alloc(2, 32)
        cbm = alloc(4, 384)
        sw = Pool([alloc(384) for _ in range(4)])
        cvs = Pool([alloc(T) for _ in range(4)])
        ztok, xtok, bctok, xdtok = {}, {}, {}, {}
        st = {}

        def ev_z(t, b, tok):
            r = ztok[t] = A.act(z[:, t, :], b[:, 0:T], ACT.Silu, tok)
            return [r]

        def ev_dt(t, b, tok):
            R = slice(96, 128)
            a, e, w, p = (q[R, :] for q in dtmp)
            bi = W("dtb")[R, :]
            t0 = V.ts(a, b[R, 0:T], bi, None, ADD, None, tok)
            t = V.ts(w, a, -1.0, None, MUL, None, t0)
            t = V.tt(w, w, a, MIN, t)
            t = A.act(e, w, ACT.Exp, t)
            t = V.ts(w, e, 2.0, None, ADD, None, t)
            t = V.recip(w, w, t)
            t = V.tt(e, e, w, MUL, t)
            t = V.tt(w, e, e, MUL, t)
            cf = [1.0 / (2 * k + 1) for k in range(10)]
            t = V.ts(p, w, cf[9], cf[8], MUL, ADD, t)
            for k in range(7, -1, -1):
                t = V.tt(p, p, w, MUL, t)
                t = V.ts(p, p, cf[k], None, ADD, None, t)
            t = V.stt(p, e, 2.0, p, MUL, MUL, t)
            t = V.stt(dt_[R, :], a, 0.0, p, MAX, ADD, t)
            ta = A.act(sm2[R, :], W("alog")[R, :], ACT.Exp)
            t = V.ts(sm2[R, :], sm2[R, :], -1.0, None, MUL, None, ta, t)
            t = V.ts(da_[R, :], dt_[R, :], sm2[R, :], None, MUL, None, t)
            tcs = V.scan(cs_[R, :], C("ones", 0, 1)[R, :].broadcast_to([32, T]), da_[R, :], t)
            st["cs"] = tcs
            b2, free = PS.take()
            bk = banks[b2]
            for hf in range(2):
                P.tp(bk[:, hf * 32:hf * 32 + 32], dt_[R, hf * 128:(hf + 1) * 128], ident[R, 96:128], tcs, *free)
                tm = P.tp(bk[:, 64 + hf * 32:96 + hf * 32], cs_[R, hf * 128:(hf + 1) * 128], ident[R, 96:128],
                          tcs, sig=True)
            r = V.copy(dtT, bk[:, 0:64].rearrange("p (a b) -> p a b", a=2), tm)
            st["csT"] = V.copy(csT, bk[:, 64:128].rearrange("p (a b) -> p a b", a=2), tm)
            st["dtT"] = r
            PS.give(b2, r, st["csT"])
            return [t0]

        sm2 = alloc(1)
        shp = Pool([alloc(T) for _ in range(2)])
        FULL = slice(0, 128)

        def shift(dst, b, mu, R, tok, *needs):
            n = R.stop
            s, sf = shp.take()
            v = b[R, 0:T]
            s, ss = s[R, :], s
            t0 = A.act(ss[R, :], v, ACT.Copy, tok, *sf)
            dd, df = scr.take()
            t1 = V.tt(dd[R, 1:T], s[:, 0:T - 1], v[:, 1:T], SUB, t0, *df)
            t2 = V.ts(dd[R, 0:1], s[:, 0:1], -1.0, None, MUL, None, t0)
            if len(dst.shape) == 3:
                t = V.stt(dst, dd[R, :].rearrange("p (a b) -> p a b", a=2), mu,
                          s.rearrange("p (a b) -> p a b", a=2), MUL, ADD, t1, t2, *needs)
            else:
                t = V.stt(dst, dd[R, :], mu, s, MUL, ADD, t1, t2, *needs)
            scr.give(dd, t)
            shp.give(ss, t)
            return t

        small = {}

        def ev_wd(t, b, tok):
            R = slice(0, 96)
            r = shift(wd[R, :], b, W("mu_wd")[R, :], R, tok)
            small["wd"] = A.act(wd[R, :], wd[R, :], ACT.Tanh, r)
            return [r]

        def ev_ad(t, b, tok):
            R = slice(0, 96)
            small["ad"] = shift(ad[R, :], b, W("mu_ad")[R, :], R, tok)
            return [small["ad"]]

        def ev_gd(t, b, tok):
            s, sf = scr.take()
            r = shift(s, b, W("mu_gd", t), FULL, tok, *sf)
            ta = A.act(s, s, ACT.Sigmoid, r)
            small[("gd", t)] = cutup(gdr[:, 0, t, :], gdr[:, 1, t, :], s, G, ta)
            scr.give(s, small[("gd", t)])
            return [r]

        def ev_sm(t, b, tok):
            if t == 0:
                r = ev_wd(t, b, tok)
                return ev_dt(t, b, tok) + r
            return ev_ad(t, b, tok) if t == 1 else ev_gd(t - 2, b, tok)


        def conv4(dst, ps, i, tok, *needs):
            s, cf = cvs.take()
            t = A.act(s, ps, ACT.Identity, tok, *cf, bias=W("ssd_conv_b_2", i), scale=W("dw3", i))
            for sh, nm in ((1, "dw2"), (2, "dw1"), (3, "dw0")):
                t = V.stt(s[:, sh:T], ps[:, 0:T - sh], W(nm, i), s[:, sh:T], MUL, ADD, t)
            r = A.act(dst, s, ACT.Silu, t, hst, *needs)
            cvs.give(s, r)
            return t, r

        xfree = [[], []]
        xT = h

        def ev_bc(t, b, tok):
            t1, bctok[t - 16] = conv4(bc[:, t - 16, :], b[:, 0:T], t, tok)
            return [t1]

        def ev_x(t, b, tok):
            t1, r = conv4(xT[:, t, :], b[:, 0:T], t, tok)
            xtok[t] = r
            b2, free = PS.take()
            for hf in range(2):
                tm = P.tp(banks[b2][:, hf * 128:(hf + 1) * 128], xT[:, t, hf * 128:(hf + 1) * 128], ident, r,
                          *free, sig=True)
            for hf in range(2):
                dtb = dtT[:, hf, 2 * t:2 * t + 2].unsqueeze(2).broadcast_to([128, 2, 64])
                xdtok[t] = V.tt(xd[:, hf, t * 128:(t + 1) * 128].rearrange("p (a b) -> p a b", a=2),
                                banks[b2][:, hf * 128:(hf + 1) * 128].rearrange("p (a b) -> p a b", a=2),
                                dtb, MUL, tm, st["dtT"])
            PS.give(b2, xdtok[t])
            return [t1]

        run(chain(linear("w_sm", 4, 16, nrhs, ntok, ev_sm),
                  linear("w_xbc", 8, 16, nrhs, ntok, ev_bc, t0=16),
                  linear("w_xbc", 16, 16, nrhs, ntok, ev_x),
                  linear("w_z", 16, 16, nrhs, ntok, ev_z)))

        cbt = {}
        for g in range(4):
            b, free = PS.take()
            P.mm(banks[b][:, 0:256], bc[:, g, 0:128], bc[:, 4 + g, :], True, True, bctok[g], bctok[4 + g],
                 *free)
            tm = P.mm(banks[b][:, 256:384], bc[:, g, 128:256], bc[:, 4 + g, 128:256], True, True, sig=True)
            V.tt(cbm[:, g, 0:256], banks[b][:, 0:256], C("cm"), MUL, tm)
            cbt[g] = V.tt(cbm[:, g, 256:384], banks[b][:, 256:384], C("cm", 0, 128), MUL)
            PS.give(b, cbt[g])
        ysst = {}

        def ssd_pair(i):
            yb, yfree = PS.take()
            last = []
            for e in range(2):
                hd = 2 * i + e
                g = hd // 8
                b, free = PS.take()
                sel = ident[96:128, 96 + hd:97 + hd].broadcast_to([32, 128])
                tm = P.mm(banks[b][:, 0:T], sel, cs_[96:128, :], True, True, st["cs"], *free, sig=True)
                w, wf = sw.take()
                yield
                V.ts(w[:, 0:256], banks[b][:, 0:T], csT[:, 0, hd:hd + 1], 0.0, SUB, MIN, tm, st["csT"], *wf)
                t = V.ts(w[:, 256:384], banks[b][:, 128:T], csT[:, 1, hd:hd + 1], 0.0, SUB, MIN)
                PS.give(b, t)
                t = A.act(w, w, ACT.Exp, t)
                yield
                t = V.tt(w, w, cbm[:, g, :], MUL, t, cbt[g])
                yield
                R = slice(64 * e, 64 * e + 64)
                P.mm(banks[yb][R, 0:256], xd[:, 0, hd * 64:hd * 64 + 64], w[:, 0:256], True, False, t,
                     xdtok[i], *yfree)
                tm = P.mm(banks[yb][R, 128:256], xd[:, 1, hd * 64:hd * 64 + 64], w[:, 256:384], False, True,
                          sig=True)
                sw.give(w, tm)
            yield
            s, sf = scr.take()
            t = V.stt(s, xT[:, i, :], W("dskip", i), banks[yb][:, 0:T], MUL, ADD, tm, *sf)
            PS.give(yb, t)
            ysst[i] = V.tt(z[:, i, :], s, z[:, i, :], MUL, t, ztok[i])
            scr.give(s, ysst[i])

        run(flight(ssd_pair, 16, 2))
        for g in range(4):
            rms([z[:, 4 * g + i, :] for i in range(4)], [ysst[4 * g + i] for i in range(4)],
                ("ssd_norm_g_2", 4 * g), [yss[:, 4 * g + i, :] for i in range(4)], 512, 1e-5)
        barrier()

        A.wait(V.now(), A.now(), G.now(), P.now())
        A.items.append(lambda e, y_=yss: e.dma_start(d["ysave"], y_).then_inc(sv[1], 16))
        hst = [(sv[1], 16)]
        for q in ENG:
            q.wait(hst)
        top[0] = mark
        kko = top[0]
        kk_, vv = alloc(16, T), alloc(16, T)
        aro = top[0]
        AR = alloc(16, 2, 2, 128)
        bb = h
        PL = alloc(16, 8)
        p33 = Pool([alloc(8, 33) for _ in range(2)])
        shp = Pool([alloc(T) for _ in range(2)])
        w2s = within(hno, 2048)
        a2s = within(hno + 2048, 2048)
        ktk, vtk, rtk = {}, {}, {}


        def ev_r(t, b, tok):
            rtk[t] = shift(AR[:, t, :, 1, :], b, W("mu_r", t), FULL, tok)
            return [rtk[t]]

        def ev_kk(t, b, tok):
            ktk[t] = shift(kk_[:, t, :], b, W("mu_k", t), FULL, tok)
            return [ktk[t]]

        def ev_vv(t, b, tok):
            vtk[t] = shift(vv[:, t, :], b, W("mu_v", t), FULL, tok)
            return [vtk[t]]

        def prep(i):
            b, free = PS.take()
            P.mm(banks[b][:, 0:T], w2s[0:96, i * 128:(i + 1) * 128], wd[0:96, :], True, True, small["wd"],
                 *free)
            tm = P.mm(banks[b][:, T:2 * T], a2s[0:96, i * 128:(i + 1) * 128], ad[0:96, :], True, True,
                      small["ad"], sig=True)
            s1, f1 = scr.take()
            s2, f2 = scr.take()
            s3, f3 = scr.take()
            yield
            tsg = A.act(s1, banks[b][:, 0:T], ACT.Sigmoid, tm, *f1, bias=W("rwkv_w0_2", i))
            ta = A.act(s2, banks[b][:, T:2 * T], ACT.Sigmoid, tm, *f2, bias=W("rwkv_a0_2", i))
            PS.give(b, tsg, ta)
            t = V.ts(s1, s1, -math.exp(-0.5), None, MUL, None, tsg)
            tcm = V.scan(s3, C("rm"), s1, t, *f3)
            pb, pf = p33.take()
            c3 = s3.rearrange("p (a b) -> p a b", b=32)
            t = V.mset(pb[:, :, 0:1], 1.0, *pf)
            tp_ = A.act(pb[:, :, 1:33], c3, ACT.Exp, tcm, *pf)
            tip = A.act(s3, s3, ACT.Exp, tp_, scale=-1.0)
            yield
            tpl = V.copy(PL[:, i, :].unsqueeze(2), pb[:, :, 32:33], tp_)
            kk = s1
            t = V.ts(kk, kk_[:, i, :], W("rwkv_k_k_2", i), None, MUL, None, ktk[i], tcm)
            s4, f4 = scr.take()
            t4 = A.act(s4, kk, ACT.Square, t, *f4)
            b, free = PS.take()
            tm = P.mm(banks[b][:, 0:T], blk, s4, True, True, t4, *free, sig=True)
            t5 = V.ts(s4, s2, -1.0, W("rwkv_k_a_2", i), ADD, MUL, ta, tm)
            t5 = V.stt(s4, s4, 1.0, kk_[:, i, :], ADD, MUL, t5)
            tkf = V.tt(kk_[:, i, :], s4, s3, MUL, t5, tip)
            yield
            t = V.ts(s4, banks[b][:, 0:T], 1e-24, None, MAX, None, tm, tkf)
            PS.give(b, t)
            t = V.recip(s4, s4, t)
            t = A.act(s4, s4, ACT.Sqrt, t)
            yield
            t = V.tt(kk, kk, s4, MUL, t)
            pp = pb[:, :, 0:32].rearrange("p (s a) b -> p s a b", s=2)
            k4 = kk.rearrange("p (s a b) -> p s a b", s=2, b=32)
            ta2 = V.stt(AR[:, i, :, 0, :].rearrange("p s (a b) -> p s a b", b=32), k4, -1.0, pp, MUL, MUL, t)
            tb1 = V.tt(kk, kk, s2, MUL, ta2)
            tb2 = V.tt(bb[:, i, :], kk, s3, MUL, tb1)
            r4 = AR[:, i, :, 1, :].rearrange("p s (a b) -> p s a b", b=32)
            tr2 = V.tt(r4, r4, pb[:, :, 1:33].rearrange("p (s a) b -> p s a b", s=2), MUL, rtk[i], tp_)
            p33.give(pb, tr2)
            for x in (s1, s2, s3, s4):
                scr.give(x, tr2, tb2)
            ptk[i] = tr2

        ptk = {}
        run(chain(linear("w_k", 16, 16, nrhs, ntok, ev_kk),
                  linear("w_r", 16, 16, nrhs, ntok, ev_r),
                  linear("w_v", 16, 16, nrhs, ntok, ev_vv)))
        tl = [load(w2s[0:96, :], d["w2"], *[q.now() for q in ENG], hst, q=A),
              load(a2s[0:96, :], d["a2"], q=A)]
        for q in ENG:
            q.wait(tl)
            q.wait(hst)
        run(flight(prep, 16, 1))
        barrier()

        XA = within(hno + 0, 2, 32, 32)
        XB = within(hno + 2048, 2, 32, 32)
        XX = within(hno + 4096, 2, 32, 32)
        XT = within(hno + 6144, 2, 32, 32)
        s32 = C("s32")
        ta_ = None
        for hf in range(2):
            for i in range(0, 16, 4):
                bks = [PS.take() for _ in range(2)]
                for j in range(4):
                    for e in range(2):
                        R = slice(64 * e, 64 * e + 64)
                        tm = P.mm(banks[bks[e][0]][:, j * 128:(j + 1) * 128],
                                  bb[R, i + j, hf * 128:(hf + 1) * 128], AR[R, i + j, hf, 0, :], True, True,
                                  ptk[i + j], *bks[e][1], sig=True)
                for e in range(2):
                    bk = banks[bks[e][0]][:, :].rearrange("p (j t) -> p t j", j=4)
                    for c in range(4):
                        Q = slice(32 * c, 32 * c + 32)
                        ta_ = V.tt(XA[Q, hf, :, 2 * i + e:2 * i + 8:2], bk[Q, 32 * c:32 * c + 32, :],
                                   s32[Q, :].unsqueeze(2).broadcast_to([32, 32, 4]), MUL, tm)
                    PS.give(bks[e][0], ta_)
        t = ta_
        for hf in range(2):
            t = V.tr(XB[:, hf, :, :].rearrange("p t g -> p (t g)"),
                     XA[:, hf, :, :].rearrange("p t g -> p (t g)"), t)
        t = V.mset(XX, 0.0, t)
        t = V.mset(XX[:, :, :, :].rearrange("p s t g -> p s (t g)")[:, :, 0:1024:33], 1.0, t)
        for r in range(1, 32):
            prod = XA.rearrange("p s t g -> p (s t g)")[:, 0:2 * r * r].rearrange(
                "p (s j k) -> p s j k", s=2, j=r)
            a4 = XB[:, :, r, 0:r].unsqueeze(2).broadcast_to([128, 2, r, r])
            x4 = XX[:, :, 0:r, 0:r].rearrange("p s k j -> p s j k")
            t = V.tt(prod, a4, x4, MUL, t)
            t = V.red(XX[:, :, r, 0:r], prod, ADD, t)
        for hf in range(2):
            t = V.tr(XT[:, hf, :, :].rearrange("p t g -> p (t g)"),
                     XX[:, hf, :, :].rearrange("p t g -> p (t g)"), t)
        xtt = t
        barrier()

        def alloc_h(*shape):
            n = int(np.prod(shape))
            for blk_, size, at in pools_:
                if at[0] + n <= size:
                    v = blk_[:, at[0]:at[0] + n]
                    at[0] += n
                    if len(shape) == 2:
                        v = v.rearrange("p (a b) -> p a b", b=shape[1])
                    return v
            raise AssertionError("no room")

        pools_ = [(within(hno, 6144), 6144, [0]),
                  (at(top[0], NARENA - top[0]), NARENA - top[0], [0])]
        DEP = 2
        tokb = Pool([alloc_h(2, 128) for _ in range(DEP)])
        mskb = Pool([alloc_h(3, 128) for _ in range(2 * DEP)])
        bx = Pool([alloc_h(4, 128) for _ in range(DEP)])
        kx = Pool([alloc_h(4, 128) for _ in range(DEP)])
        gt = Pool([alloc_h(4, 128) for _ in range(DEP)])
        wu = Pool([alloc_h(256) for _ in range(DEP)])
        az = Pool([alloc_h(128) for _ in range(DEP)])
        qt = Pool([alloc_h(128) for _ in range(DEP)])
        xbd = Pool([w_ for w_ in (alloc_h(128), alloc_h(128))])
        sbd = Pool([alloc_h(128) for _ in range(2 * DEP)])
        yb_ = Pool([alloc_h(256) for _ in range(DEP)])
        tz = []
        for p_ in (gt, sbd):
            for v, _ in list(p_.free):
                tz.append(G.mset(v, 0.0))
        tzz = tz[-1]
        for q in ENG:
            q.wait(tzz)
        m3 = C("m3")
        bm = C("bm")
        vtk2 = {}

        def block(i, hf, state):
            TS = slice(hf * 128, (hf + 1) * 128)
            b, free = PS.take()
            bk = banks[b]
            P.tp(bk[:, 0:128], AR[:, i, hf, 0, :], ident, *free)
            P.tp(bk[:, 128:256], vv[:, i, TS], ident)
            P.tp(bk[:, 256:384], bb[:, i, TS], ident)
            tm = P.tp(bk[:, 384:512], kk_[:, i, TS], ident, sig=True)
            tk, tf_ = tokb.take()
            bxb, bf = bx.take()
            kxb, kf_ = kx.take()
            m4 = C("bm4").unsqueeze(2).broadcast_to([128, 4, 128])
            tt_ = A.act(tk.rearrange("p a b -> p (a b)"), bk[:, 0:256], ACT.Copy, tm, *tf_)
            tbx = V.tt(bxb, bk[:, 256:384].unsqueeze(1).broadcast_to([128, 4, 128]), m4, MUL, tt_, *bf)
            tkx = V.tt(kxb, bk[:, 384:512].unsqueeze(1).broadcast_to([128, 4, 128]), m4, MUL, *kf_)
            PS.give(b, tkx)
            yield
            mks = []
            for e in range(2):
                R = slice(64 * e, 64 * e + 64)
                b, free = PS.take()
                P.mm(banks[b][:, 0:128], bb[R, i, TS], AR[R, i, hf, 1, :], True, True, *free)
                tm = P.mm(banks[b][:, 128:384], kk_[R, i, TS], AR[R, i, hf, :, :].rearrange(
                    "p a b -> p (a b)"), True, True, sig=True)
                mk, mf = mskb.take()
                t = V.tt(mk.rearrange("p a b -> p (a b)"), banks[b][:, 0:384], m3, MUL, tm, *mf)
                PS.give(b, t)
                mks.append((mk, t))
                yield
            b, free = PS.take()
            for e in range(2):
                tm = P.mm(banks[b][:, 64 * e:64 * e + 64], mks[e][0][:, 1, :], tk[:, 1, 64 * e:64 * e + 64],
                          True, True, mks[e][1], tt_, *free, sig=True)
            azb, af = az.take()
            taz = V.copy(azb, banks[b][:, 0:128], tm, *af)
            PS.give(b, taz)
            yield
            b, free = PS.take()
            for e in range(2):
                hd = 2 * i + e
                xb, xf = xbd.take()
                tx = V.tt(xb.rearrange("p (c t) -> p c t", c=4),
                          XT[:, hf, :, hd].unsqueeze(1).broadcast_to([128, 4, 32]),
                          bm.rearrange("p (c t) -> p c t", c=4), MUL, *xf)
                P.mm(banks[b][:, 64 * e:64 * e + 64], xb, tk[:, 0, 64 * e:64 * e + 64], True, True, tx, *free)
                tm = P.mm(banks[b][:, 128 + 64 * e:192 + 64 * e], xb, azb[:, 64 * e:64 * e + 64], True, True,
                          taz, sig=True)
                xbd.give(xb, tm)
            az.give(azb, tm)
            wub, wf = wu.take()
            twu = V.copy(wub, banks[b][:, 0:256], tm, *wf)
            PS.give(b, twu)
            yield
            b, free = PS.take()
            for e in range(2):
                R = slice(64 * e, 64 * e + 64)
                tm = P.mm(banks[b][R, 0:128], wub[:, 64 * e:64 * e + 64], mks[e][0][:, 0, :], True, True, twu,
                          *free, sig=True)
            qb, qf = qt.take()
            tq = V.tt(qb, banks[b][:, 0:128], AR[:, i, hf, 1, :], ADD, tm, *qf)
            PS.give(b, tq)
            yb, yfree = PS.take()
            for e in range(2):
                R = slice(64 * e, 64 * e + 64)
                P.mm(banks[yb][R, 0:128], wub[:, 128 + 64 * e:192 + 64 * e], mks[e][0][:, 0, :], True, False,
                     twu, *yfree)
                tm = P.mm(banks[yb][R, 0:128], tk[:, 1, 64 * e:64 * e + 64], mks[e][0][:, 2, :], False, True,
                          sig=True)
            for e in range(2):
                mskb.give(mks[e][0], tm)
            ybuf, ybf = state["y"]
            ty0 = A.act(ybuf[:, TS], banks[yb][:, 0:128], ACT.Copy, tm, *ybf)
            PS.give(yb, ty0)
            yield
            b, free = PS.take()
            tm = P.mm(banks[b][:, :], wub[:, 0:128], bxb.rearrange("p c k -> p (c k)"), True, True, tbx, twu,
                      *free, sig=True)
            gb, gf = gt.take()
            for e in range(2):
                R = slice(64 * e, 64 * e + 64)
                ii = ident[R, 64 * e:64 * e + 64].unsqueeze(1).broadcast_to([64, 4, 64])
                tg = V.tt(gb[R, :, 64 * e:64 * e + 64],
                          banks[b][R, :].rearrange("p (c k) -> p c k", c=4)[:, :, 64 * e:64 * e + 64], ii,
                          ADD, tm, *gf)
            PS.give(b, tg)
            yield
            yb, yfree = PS.take()
            for c in range(4):
                sb_, stok = state["s"]
                ty = P.mm(banks[yb][:, 32 * c:32 * c + 32], sb_, qb[:, 32 * c:32 * c + 32], True, True, stok,
                          tq, *(yfree if c == 0 else []), sig=True)
                b, free = PS.take()
                P.mm(banks[b][:, 0:128], bxb[:, c, :], wub[:, 128:256], True, False, tbx, twu, *free)
                P.mm(banks[b][:, 0:128], kxb[:, c, :], tk[:, 1, :], False, False, tkx)
                tm = P.mm(banks[b][:, 0:128], gb[:, c, :], sb_, False, True, tg, stok, sig=True)
                sbd.give(sb_, tm)
                sn, sf = sbd.take()
                ch = hf * 4 + c
                for e in range(2):
                    R = slice(64 * e, 64 * e + 64)
                    CS = slice(64 * e, 64 * e + 64)
                    if e == 0:
                        ts_a = V.ts(sn[R, CS], banks[b][R, CS], PL[R, i, ch:ch + 1], None, MUL, None, tm, *sf)
                    else:
                        ts_b = A.act(sn[R, CS], banks[b][R, CS], ACT.Copy, tm, *sf,
                                     scale=PL[R, i, ch:ch + 1])
                PS.give(b, ts_a, ts_b)
                state["s"] = (sn, [ts_a, ts_b])
                yield
            tokb.give(tk, tm)
            bx.give(bxb, tm)
            kx.give(kxb, tm)
            gt.give(gb, tm)
            wu.give(wub, tm)
            qt.give(qb, ty)
            ty2 = V.tt(ybuf[:, TS], ybuf[:, TS], banks[yb][:, 0:128], ADD, ty, ty0)
            PS.give(yb, ty2)
            state["yt"].append(ty2)
            yield

        def pair(i):
            state = {"y": yb_.take(), "yt": []}
            sb0, sf0 = sbd.take()
            tz_ = V.mset(sb0, 0.0, *sf0)
            state["s"] = (sb0, [tz_])
            for hf in range(2):
                yield from block(i, hf, state)
            sb_, stok = state["s"]
            sbd.give(sb_, *stok)
            yb = state["y"][0]
            b, free = PS.take()
            tm = P.mm(banks[b][:, 0:T], blk, yb, True, True, *state["yt"], *free, sig=True)
            s1, f1 = scr.take()
            t = V.stt(s1, banks[b][:, 0:T], -1.0 / 64, yb, MUL, ADD, tm, *f1)
            PS.give(b, t)
            s2, f2 = scr.take()
            t2 = A.act(s2, s1, ACT.Square, t, *f2)
            b, free = PS.take()
            tm = P.mm(banks[b][:, 0:T], blk, s2, True, True, t2, *free, sig=True)
            yield
            rk = yb.rearrange("p (a b) -> p a b", a=2)
            t = V.stt(rk, AR[:, i, :, 1, :], W("rwkv_r_k_2", i),
                      kk_[:, i, :].rearrange("p (a b) -> p a b", a=2), MUL, MUL, t)
            t = V.ts(s2, banks[b][:, 0:T], 1.0 / 64, 64e-5, MUL, ADD, tm)
            PS.give(b, t)
            b, free = PS.take()
            tb = P.mm(banks[b][:, 0:T], blk, yb, True, True, t, *free, sig=True)
            t = V.recip(s2, s2, t)
            t = A.act(s2, s2, ACT.Sqrt, t)
            yield
            t = V.tt(s1, s1, s2, MUL, t)
            t = V.ts(s1, s1, W("rwkv_gn_w_2", i), W("rwkv_gn_b_2", i), MUL, ADD, t)
            t3 = V.tt(s2, banks[b][:, 0:T], vv[:, i, :], MUL, tb, t)
            PS.give(b, t3)
            vtk2[i] = V.tt(vv[:, i, :], s1, s2, ADD, t3)
            yb_.give(yb, vtk2[i])
            scr.give(s1, vtk2[i])
            scr.give(s2, vtk2[i])

        run(flight(pair, 16, DEP))

        def ev_g(t, b, tok):
            vtk2[t] = V.tt(vv[:, t, :], vv[:, t, :], b[:, 0:T], MUL, tok, vtk2[t])
            return [vtk2[t]]

        run(linear("w_g2", 16, 2, lambda kc: (gdr[:, 0, kc, :], gdr[:, 1, kc, :]), lambda kc: small[("gd", kc)], ev_g))
        barrier()
        tl = load(h, d["hsave"], *[q.now() for q in ENG], q=A)
        yss = within(hno, 16, T)
        tl2 = load(yss, d["ysave"], q=A)
        htok = [tl] * 16
        vvr = within(aro, 2, 16, T, dt=F32R)
        vct = [cutup(vvr[:, 0, i, :], vvr[:, 1, i, :], vv[:, i, :], (V, G)[i % 2], vtk2[i]) for i in range(16)]
        ysr = within(kko, 2, 16, T, dt=F32R)
        yct = [cutup(ysr[:, 0, i, :], ysr[:, 1, i, :], yss[:, i, :], (V, G)[i % 2], tl2, *vct) for i in range(16)]
        run(linear("w_out2", 16, 32,
                   lambda kc: (ysr[:, 0, kc, :], ysr[:, 1, kc, :]) if kc < 16 else
                   (vvr[:, 0, kc - 16, :], vvr[:, 1, kc - 16, :]),
                   lambda kc: yct[kc] if kc < 16 else vct[kc - 16], ev_res))
        barrier()
        top[0] = ffo + 2 * 22 * T
        cvs = Pool([alloc(T) for _ in range(4)])
        tn = rms(hchunks, htok, ("norm2_g_2", 0), hn_out, D, 1e-6)
        fdone[0] = []

        def ev_gu(t, b, tok):
            j, up = t // 2, t % 2
            if not up:
                s, sf = cvs.take()
                r = A.act(s, b[:, 0:T], ACT.Silu, tok, *sf)
                gbuf[j] = (s, r)
                return [r]
            s, r = gbuf[j]
            tg = V.tt(s, s, b[:, 0:T], MUL, tok, r)
            ftok[j] = cutup(*frhs(j), s, G, tg, *fdone[0])
            cvs.give(s, ftok[j])
            return [tg]

        for q in range(2):
            run(linear("w_gu", 44, 16, nrhs, ntok, ev_gu, t0=44 * q))
            run(linear("w_down2", 16, 44, frhs, lambda kc: ftok[kc], ev_res, k0=22 * q, k1=22 * q + 22))
            fdone[0] = [P.now()]
        tf = rms(hchunks, htok, ("norm_f_g_2", 0), hchunks, D, 1e-6)
        for i in range(0, 16, 4):
            S.wait(*tf[i:i + 4])
            S.items.append(lambda e, i=i: e.dma_start(out[:, i:i + 4, :], h[:, i:i + 4, :])
                           .then_inc(st_sem, 16))
            nstore[0] += 1
        S.wait((st_sem, 16 * nstore[0]))

        blockx = ctx.enter_context(nc.Block())

        @blockx.tensor
        def _(e):
            P.replay(e)

        @blockx.vector
        def _(e):
            V.replay(e)

        @blockx.scalar
        def _(e):
            A.replay(e)

        @blockx.gpsimd
        def _(e):
            G.replay(e)

        @blockx.sync
        def _(e):
            S.replay(e)


def constants():
    c = np.zeros((128, NCST), np.float32)

    def put(name, v):
        o, n = CST_AT[name]
        c[:, o:o + n] = v

    p = np.arange(128)
    put("ident", np.eye(128))
    put("ones", 1.0)
    put("blk", p[:, None] // 64 == p[None] // 64)
    perm = np.zeros((128, 128))
    for m in range(128):
        if m % 64 < 32:
            perm[m + 32, m] = -1.0
        else:
            perm[m - 32, m] = 1.0
    put("perm", perm)
    same = p[:, None] // 32 == p[None] // 32
    incl = same & (p[:, None] <= p[None])
    strict = same & (p[:, None] < p[None])
    put("m3", np.concatenate([incl, strict, incl], 1))
    put("s32", (p[:, None] % 32) < np.arange(32)[None])
    put("bm", same)
    put("bm4", p[:, None] // 32 == np.arange(4)[None])
    zc = np.zeros((128, 256), np.float32)
    zc[:, 128:] = np.where(p[None] <= p[:, None], 0.0, np.finfo(np.float32).min)
    put("zc", zc)
    cm = np.ones((128, 256))
    cm[:, 0:128] = p[:, None] <= p[None]
    put("cm", cm)
    put("kp", np.stack([p < 64, p >= 64], 1))
    fr = np.float32(10000.0) ** (-np.arange(0, 64, 2, dtype=np.float32) / np.float32(64))
    put("ifr", fr.astype(np.float32)[p % 32][:, None])
    put("rm", (np.arange(256) % 32 != 0)[None])
    return c


def tiles(w, M=128):
    K, N = w.shape
    return np.ascontiguousarray(w.reshape(K // 128, 128, N // M, M).transpose(2, 1, 0, 3)).reshape(
        N // M, 128, K // 128 * M)


def layout(x):
    f = {}
    cols = lambda a: np.ascontiguousarray(a.reshape(-1, 128).T)

    def padded(a, o=0):
        v = np.zeros((128, 1), a.dtype)
        v[o:o + a.size, 0] = a.reshape(-1)
        return v

    vec = np.zeros((128, NVEC), np.float32)

    def put(name, v):
        o, n = VEC_AT[name]
        vec[:, o:o + n] = v

    for n in ("attn_norm_w", "mla_q_norm_w", "mla_kv_norm_w", "ssm_out_norm_w", "mla_out_norm_w",
              "ffn_norm_w", "ffn_conv_b", "final_norm_w", "ssm_d", "ssm_b_glu", "norm1_g_2",
              "ssd_conv_b_2", "ssd_norm_g_2", "rwkv_w0_2", "rwkv_a0_2", "rwkv_k_k_2", "rwkv_k_a_2",
              "rwkv_r_k_2", "rwkv_gn_w_2", "rwkv_gn_b_2", "norm2_g_2", "norm_f_g_2"):
        put(n, cols(x[n]))
    for k in range(3):
        put(f"cw{k}", cols(x["ffn_conv_w"][0, k]))
    for k in range(4):
        put(f"dw{k}", cols(x["ssd_conv_w_2"][0, k]))
    mu = x["rwkv_mu_2"][0]
    put("mu_r", cols(mu[0:2048]))
    put("mu_k", cols(mu[2048:4096]))
    put("mu_v", cols(mu[4096:6144]))
    put("mu_wd", padded(mu[6144:6240]))
    put("mu_ad", padded(mu[6240:6336]))
    put("mu_gd", cols(mu[6336:6592]))
    put("dskip", cols(np.repeat(x["ssd_D_2"][0], 64)))
    put("dtb", padded(x["ssd_dt_bias_2"][0], 96))
    put("alog", padded(x["ssd_A_log_2"][0], 96))
    put("lr", x["ssm_lambda_re"][0].reshape(32, 128).T)
    put("li", x["ssm_lambda_im"][0].reshape(32, 128).T)
    put("ldt", np.repeat(x["ssm_log_dt"][0], 64).reshape(32, 128).T)
    f["vec"] = vec
    f["cst"] = constants()
    f["xT"] = np.ascontiguousarray(x["x"][0].T.reshape(16, 128, T).transpose(1, 0, 2))
    f["pos"] = np.ascontiguousarray(x["positions"]).astype(np.int64).view(np.int32).reshape(512)
    for nm, key in (("bre", "ssm_b_re"), ("bim", "ssm_b_im")):
        b = x[key][0].reshape(8, 4, 2, 64, 16)
        v = np.zeros((4, 2, 16, 8, 2, 64), np.float32)
        for g in range(2):
            v[:, g, :, :, g, :] = b[:, :, g].transpose(1, 3, 0, 2)
        f[nm] = v.reshape(128, 8, 128)
    for nm, key in (("cre", "ssm_c_re"), ("cim", "ssm_c_im")):
        c = x[key][0].reshape(32, 2, 16, 64)
        v = np.zeros((2, 64, 32, 2, 16), np.float32)
        for g in range(2):
            v[g, :, :, g, :] = c[:, g].transpose(2, 0, 1)
        f[nm] = v.reshape(128, 32, 32)
    w = x["w_in"][0]
    f["w_in"] = tiles(w[:, 0:1792])
    f["w_kpe"] = tiles(np.concatenate([w[:, 1792:1856], w[:, 1792:1856]], 1))
    uq = x["mla_w_uq"][0].reshape(512, 8, 192)
    f["w_uq"] = tiles(np.concatenate([uq[:, :, 0:128].reshape(512, 1024),
                                      uq[:, :, 128:192].reshape(512, 512)], 1))
    ukv = x["mla_w_ukv"][0].reshape(256, 8, 256)
    f["w_uk"] = tiles(ukv[:, :, 0:128].reshape(256, 1024))
    f["w_uv"] = np.ascontiguousarray(ukv[:, :, 128:256].reshape(2, 128, 1024).transpose(1, 0, 2)).reshape(1, 128, 2048)
    f["w_glu"] = tiles(x["ssm_w_glu"][0])
    f["w_out"] = tiles(x["w_out"][0])
    up = x["ffn_w_up"][0].reshape(2048, 2, 44, 128).transpose(0, 2, 1, 3).reshape(2048, 2 * FF)
    f["w_up"] = tiles(up)
    f["w_down"] = tiles(x["ffn_w_down"][0])
    w = x["w_in_2"][0]
    f["w_z"] = tiles(w[:, 0:2048])
    f["w_xbc"] = tiles(w[:, 2048:5120])
    f["w_r"] = tiles(w[:, 5152:7200])
    f["w_k"] = tiles(w[:, 7200:9248])
    f["w_v"] = tiles(w[:, 9248:11296])
    f["w_sm"] = tiles(np.concatenate([w[:, 11296:11392], w[:, 5120:5152], w[:, 11392:11488],
                                      np.zeros((2048, 32), w.dtype), w[:, 11488:11744]], 1))
    f["w2"] = np.ascontiguousarray(x["rwkv_w2_2"][0])
    f["a2"] = np.ascontiguousarray(x["rwkv_a2_2"][0])
    f["w_g2"] = tiles(x["rwkv_g2_2"][0])
    f["w_out2"] = tiles(x["w_out_2"][0])
    gu = np.stack([x["w_gate_2"][0].reshape(2048, 44, 128), x["w_up_2"][0].reshape(2048, 44, 128)], 2)
    f["w_gu"] = tiles(gu.reshape(2048, 2 * FF))
    f["w_down2"] = tiles(x["w_down_2"][0])
    return f


def kernel(**inputs):
    import concourse.bacc as _bacc
    from concourse import mybir as _mybir
    from concourse.bass_utils import run_bass_kernel_spmd as _run

    nc = _bacc.Bacc("TRN2", target_bir_lowering=False, num_devices=1)
    x = {k: np.asarray(v) for k, v in inputs.items()}
    arrays, d = {}, {}
    for name, a in layout(x).items():
        a = np.ascontiguousarray(a)
        arrays[f"in_{name}"] = a
        d[name] = nc.dram_tensor(f"in_{name}", a.shape, _mybir.dt.from_np(a.dtype), kind="ExternalInput").ap()
    for n in ("hsave", "ysave"):
        d[n] = nc.dram_tensor(n, (128, 16, T), _mybir.dt.float32, kind="Internal").ap()
    out = nc.dram_tensor("out_0", (128, 16, T), _mybir.dt.float32, kind="ExternalOutput").ap()
    program(nc, d, out)
    r = _run(nc, [arrays], core_ids=[0])
    got = r.results[0]["out_0"]
    return np.ascontiguousarray(got.transpose(1, 0, 2).reshape(2048, T).T)[None]
```

```python
import math
from collections import deque
from contextlib import ExitStack

import numpy as np

import concourse.bass as bass
from concourse import mybir

F32 = mybir.dt.float32
F32R = mybir.dt.float32r
I32 = mybir.dt.int32
ALU = mybir.AluOpType
ACT = mybir.ActivationFunctionType
X = mybir.AxisListType.X
MUL, ADD, SUB, MAX, MIN = ALU.mult, ALU.add, ALU.subtract, ALU.max, ALU.min

T = 256
D = 2048
FF = 5632
NH = 32
RAW = 3
SSM_STEPS = 2
CUT = 4
SLOT = 2048
PIECE = 1024
BASE = 16512
NTOT = 53200
NARENA = NTOT - RAW * SLOT - 2 * CUT * PIECE

CST_COLS = [("ident", 128), ("ones", 128), ("blk", 128), ("perm", 128), ("m3", 384), ("s32", 32),
            ("bm", 128), ("bm4", 4), ("zc", 256), ("cm", 256), ("kp", 2), ("ifr", 1), ("rm", 256)]
VEC_COLS = [("attn_norm_w", 16), ("mla_q_norm_w", 4), ("mla_kv_norm_w", 2), ("ssm_out_norm_w", 8),
            ("mla_out_norm_w", 8), ("ffn_norm_w", 16), ("cw0", 88), ("cw1", 88), ("cw2", 88),
            ("ffn_conv_b", 88), ("final_norm_w", 16), ("ssm_d", 8), ("ssm_b_glu", 8),
            ("norm1_g_2", 16), ("dw0", 24), ("dw1", 24), ("dw2", 24), ("dw3", 24),
            ("ssd_conv_b_2", 24), ("ssd_norm_g_2", 16), ("mu_r", 16), ("mu_k", 16), ("mu_v", 16),
            ("mu_wd", 1), ("mu_ad", 1), ("mu_gd", 2), ("rwkv_w0_2", 16), ("rwkv_a0_2", 16),
            ("rwkv_k_k_2", 16), ("rwkv_k_a_2", 16), ("rwkv_r_k_2", 16), ("rwkv_gn_w_2", 16),
            ("rwkv_gn_b_2", 16), ("norm2_g_2", 16), ("norm_f_g_2", 16), ("dskip", 16),
            ("dtb", 1), ("alog", 1), ("lr", 32), ("li", 32), ("ldt", 32)]


def columns(cols):
    at, out = 0, {}
    for name, n in cols:
        out[name] = (at, n)
        at += n
    return out, at


CST_AT, NCST = columns(CST_COLS)
VEC_AT, NVEC = columns(VEC_COLS)


class Queue:

    def __init__(self, sem):
        self.sem, self.n, self.items, self.seen = sem, 0, [], {}

    def wait(self, *needs):
        for tok in needs:
            if tok is None:
                continue
            if isinstance(tok, list):
                self.wait(*tok)
                continue
            sem, v = tok
            if v > self.seen.get(sem.name, 0):
                self.seen[sem.name] = v
                self.items.append(lambda e, sem=sem, v=v: e.wait_ge(sem, v))

    def put(self, fn, needs, sig=True):
        self.wait(*needs)
        if sig:
            self.n += 1
            sem = self.sem
            self.items.append(lambda e: fn(e).then_inc(sem, 1))
            return (sem, self.n)
        self.items.append(fn)
        return None

    def now(self):
        return (self.sem, self.n)

    def replay(self, e):
        for f in self.items:
            f(e)

    def tt(self, out, a, b, op, *needs):
        return self.put(lambda e: e.tensor_tensor(out, a, b, op), needs)

    def ts(self, out, a, s1, s2, op0, op1, *needs):
        if op1 is None:
            return self.put(lambda e: e.tensor_scalar(out, a, s1, None, op0), needs)
        return self.put(lambda e: e.tensor_scalar(out, a, s1, s2, op0, op1), needs)

    def stt(self, out, a, s, b, op0, op1, *needs):
        return self.put(lambda e: e.scalar_tensor_tensor(out=out, in0=a, scalar=s, in1=b, op0=op0,
                                                         op1=op1), needs)

    def copy(self, out, a, *needs):
        return self.put(lambda e: e.tensor_copy(out, a), needs)

    def recip(self, out, a, *needs):
        return self.put(lambda e: e.reciprocal(out, a), needs)

    def red(self, out, a, op, *needs):
        return self.put(lambda e: e.tensor_reduce(out, a, X, op), needs)

    def scan(self, out, d0, d1, *needs):
        return self.put(lambda e: e.tensor_tensor_scan(out, d0, d1, 0.0, MUL, ADD), needs)

    def tr(self, out, a, *needs):
        return self.put(lambda e: e.transpose(out, a), needs)

    def mset(self, out, v, *needs):
        return self.put(lambda e: e.memset(out, v), needs)

    def act(self, out, a, f, *needs, bias=0.0, scale=1.0, acc=None):
        if acc is not None:
            return self.put(lambda e: e.activation(out, a, f, bias=bias, scale=scale, accum_out=acc), needs)
        return self.put(lambda e: e.activation(out, a, f, bias=bias, scale=scale), needs)

    def mm(self, out, lhsT, rhs, start, stop, *needs, sig=False):
        return self.put(lambda e: e.matmul(out, lhsT, rhs, start=start, stop=stop), needs, sig)

    def tp(self, out, a, ident, *needs, sig=False):
        return self.put(lambda e: e.transpose(out, a, ident), needs, sig)


class Pool:

    def __init__(self, items):
        self.free = deque((x, []) for x in items)

    def take(self):
        return self.free.popleft()

    def give(self, x, *toks):
        self.free.append((x, list(toks)))


def run(*gens):
    live = list(gens)
    while live:
        for g in list(live):
            try:
                next(g)
            except StopIteration:
                live.remove(g)


def mix(*pairs):
    live = list(pairs)
    while live:
        for p in list(live):
            for _ in range(p[1]):
                try:
                    next(p[0])
                except StopIteration:
                    live.remove(p)
                    break
        yield


def flight(make, n, depth):
    live, i = [], 0
    while live or i < n:
        while len(live) < depth and i < n:
            live.append(make(i))
            i += 1
        for g in list(live):
            try:
                next(g)
            except StopIteration:
                live.remove(g)
        yield


def program(nc, d, out):
    with ExitStack() as ctx:
        def sem(name):
            return ctx.enter_context(nc.semaphore(name))

        names = [0]

        def at(o, n, dt=F32):
            names[0] += 1
            assert o % 8 == 0
            return nc.alloc_sbuf_tensor_at(f"m{names[0]}", [128, n], dt, offset=BASE + 4 * o)[:, :]

        raw = at(NARENA, RAW * SLOT)
        cut = [at(NARENA + RAW * SLOT + 2 * c * PIECE, 2 * PIECE, F32R) for c in range(CUT)]
        banks = [ctx.enter_context(nc.psum_tensor(f"bank{i}", [128, 512], F32)) for i in range(8)]
        P, V, A, G, S = (Queue(sem(f"s_{n}")) for n in ("pe", "dve", "act", "pool", "sp"))
        ENG = (P, V, A, G)
        raw_sem = [sem(f"s_raw{i}") for i in range(RAW)]
        st_sem = sem("s_st")
        nload, nstore = [0], [0]

        top = [0]

        def shaped(v, shape):
            if len(shape) == 2:
                v = v.rearrange("p (a b) -> p a b", b=shape[1])
            elif len(shape) == 3:
                v = v.rearrange("p (a b c) -> p a b c", b=shape[1], c=shape[2])
            elif len(shape) == 4:
                v = v.rearrange("p (a b c d) -> p a b c d", b=shape[1], c=shape[2], d=shape[3])
            return v

        def alloc(*shape, dt=F32):
            n = int(np.prod(shape))
            o = top[0]
            top[0] += (n + 7) // 8 * 8
            assert top[0] <= NARENA, top[0]
            return shaped(at(o, n, dt), shape)

        def within(o, *shape, dt=F32):
            return shaped(at(o, int(np.prod(shape)), dt), shape)

        def barrier():
            toks = [q.now() for q in ENG]
            for q in ENG:
                q.wait(*[t for t in toks if t[1]])
            return toks

        def load(dst, src, *needs, q=S):
            q.wait(*needs)
            nload[0] += 1
            sm = sem(f"s_ld{nload[0]}")
            q.items.append(lambda e: e.dma_start(dst, src).then_inc(sm, 16))
            return (sm, 16)

        stream, fetched, used = [], [0], [0]
        raw_free = [[] for _ in range(RAW)]
        cut_free = [[] for _ in range(CUT)]
        cut_tok = {}

        def kpart(KC):
            return max(k for k in range(1, KC + 1) if KC % k == 0 and k * 128 <= SLOT)

        def plan(name, nt, KC, t0=0, k0=0, k1=None):
            w = d[name]
            k1 = KC if k1 is None else k1
            kn = k1 - k0
            kper = kpart(kn)
            if kper == kn:
                tper = SLOT // (kn * 128)
                t = t0
                while t < t0 + nt:
                    m = min(tper, t0 + nt - t)
                    stream.append((name, t, k0, w[t:t + m, :, k0 * 128:k1 * 128].rearrange("m p x -> p m x"),
                                   m * kn * 128))
                    t += m
            else:
                for t in range(t0, t0 + nt):
                    for k in range(k0, k1, kper):
                        stream.append((name, t, k, w[t, :, k * 128:(k + kper) * 128], kper * 128))

        pieces, loaded = [], [0]

        def load_next():
            i = loaded[0]
            loaded[0] += 1
            src, n = stream[i][3:5]
            r = i % RAW
            S.wait(*raw_free[r])
            raw_free[r] = []
            dst = raw[:, r * SLOT:r * SLOT + n]
            sm = raw_sem[r]
            d3 = dst.rearrange("p (m x) -> p m x", m=src.shape[1]) if len(src.shape) == 3 else dst
            S.items.append(lambda e: e.dma_start(d3, src).then_inc(sm, 16))

        def fetch():
            j = fetched[0]
            fetched[0] += 1
            i, o, n = pieces[j]
            while loaded[0] < min(i + RAW, len(stream)):
                load_next()
            r, c = i % RAW, j % CUT
            tok = (raw_sem[r], 16 * (i // RAW + 1))
            src = raw[:, r * SLOT + o:r * SLOT + o + n]
            hi, lo = cut[c][:, 0:n], cut[c][:, PIECE:PIECE + n]
            ta = A.act(hi, src, ACT.Copy, tok, *cut_free[c])
            tv = V.tt(lo, src, hi.bitcast(F32), SUB, ta, tok, *cut_free[c])
            raw_free[r] = [ta, tv]
            cut_tok[j] = [ta, tv]

        def piece(name, t, k, o, ahead=CUT):
            j = used[0]
            used[0] += 1
            i, o_, n = pieces[j]
            assert stream[i][0:3] == (name, t, k) and o == o_, (stream[i][0:3], o_, name, t, k, o)
            while fetched[0] < min(j + ahead, len(pieces)):
                fetch()
            c = j % CUT
            return cut[c][:, 0:n], cut[c][:, PIECE:PIECE + n], c, cut_tok[j]

        plan("w_in", 8, 16)
        plan("w_in", 6, 16, t0=8)
        plan("w_kpe", 1, 16)
        plan("w_uq", 12, 4)
        plan("w_uk", 8, 2)
        plan("w_uv", 1, 16)
        plan("w_out", 16, 16, k0=8)
        plan("w_glu", 8, 8)
        plan("w_out", 16, 16, k1=8)
        for q in range(2):
            plan("w_up", 44, 16, t0=44 * q)
            plan("w_down", 16, 44, k0=22 * q, k1=22 * q + 22)
        plan("w_sm", 4, 16)
        plan("w_krv", 6, 16)
        for b_ in range(10):
            if b_ > 1:
                plan("w_g2", 2, 2, t0=2 * b_ - 4)
            if b_ < 7:
                plan("w_krv", 6, 16, t0=6 * b_ + 6)
            elif b_ == 7:
                plan("w_xbc", 8, 16, t0=16)
            elif b_ == 8:
                plan("w_xbc", 16, 16)
        plan("w_z", 16, 16)
        plan("w_out2", 16, 32, k0=16)
        plan("w_out2", 16, 32, k1=16)
        for q in range(2):
            plan("w_gu", 44, 16, t0=44 * q)
            plan("w_down2", 16, 44, k0=22 * q, k1=22 * q + 22)
        for i, u_ in enumerate(stream):
            for o in range(0, u_[4], PIECE):
                pieces.append((i, o, min(PIECE, u_[4] - o)))
        PS = Pool(range(8))

        def linear(name, nt, KC, rhs, ktok, evac, t0=0, k0=0, k1=None, step=8):
            k1 = KC if k1 is None else k1
            kn = k1 - k0
            kper = kpart(kn)
            tper = SLOT // (kn * 128) if kper == kn else 1
            for t in range(t0, t0 + nt):
                j = (t - t0) % tper
                b, free = PS.take()
                ps = banks[b][:, 0:T]
                for kc in range(k0, k1):
                    kk = (kc - k0) % kper
                    w = (j * kper + kk) * 128
                    o = w % PIECE
                    if o == 0:
                        hi, lo, c, tok = piece(name, t - j, kc - kk, w)
                        cur[0] = (hi, lo, c, tok)
                    hi, lo, c, tok = cur[0]
                    xh, xl = rhs(kc)
                    P.mm(ps, hi[:, o:o + 128], xh, kc == k0, False, tok, ktok(kc),
                         *(free if kc == k0 else []))
                    P.mm(ps, hi[:, o:o + 128], xl, False, False)
                    end = o + 128 == hi.shape[1]
                    last = P.mm(ps, lo[:, o:o + 128], xh, False, kc == k1 - 1, sig=end or kc == k1 - 1)
                    if end:
                        cut_free[c] = [last]
                    if (kc - k0) % step == step - 1 and kc < k1 - 1 or end and step == 8 and kc < k1 - 1:
                        yield
                PS.give(b, *evac(t, banks[b], last))
                yield

        cur = [None]

        cst = alloc(NCST)
        vec = alloc(NVEC)
        tc0 = [load(cst, d["cst"]), load(vec, d["vec"])]

        def C(name, a=0, b=None):
            o, n = CST_AT[name]
            return cst[:, o + a:o + (n if b is None else b)]

        def W(name, i=0):
            o, n = VEC_AT[name]
            return vec[:, o + i:o + i + 1]

        def WR(name):
            o, n = VEC_AT[name]
            return vec[:, o:o + n]

        ident, ones, blk = C("ident"), C("ones"), C("blk")
        h = alloc(16, T)
        hl = [load(h[:, i * 4:(i + 1) * 4, :], d["xT"][:, i * 4:(i + 1) * 4, :]) for i in range(4)]
        htok = [hl[i // 4] for i in range(16)]
        scr = Pool([alloc(T) for _ in range(6)])
        ms, rr = alloc(T), alloc(T)
        base = top[0]
        for q in ENG:
            q.wait(tc0)
        norm_free = [[]]

        def cutup(hi, lo, src, q, *needs):
            ta = A.act(hi, src, ACT.Copy, *needs)
            tl = q.tt(lo, src, hi.bitcast(F32), SUB, ta, *needs)
            return [ta, tl]

        sq = {}

        def squares(n):
            b, free = PS.take()
            sq.update(b=b, free=free, n=n, done=0, pend=deque())

        def square(chunk, tok):
            s, sf = scr.take()
            sq["pend"].append((s, A.act(s, chunk, ACT.Square, tok, *sf)))
            if len(sq["pend"]) > 2:
                add_square()

        def add_square():
            s, ta = sq["pend"].popleft()
            i = sq["done"]
            sq["done"] += 1
            tm = P.mm(banks[sq["b"]][:, 0:T], ones, s, i == 0, i == sq["n"] - 1, ta, *sq["free"], sig=True)
            scr.give(s, tm)
            return tm

        def rms(chunks, toks, wname, outs, n, eps):
            nk = len(chunks)
            if not sq:
                squares(nk)
                for i in range(nk):
                    square(chunks[i], toks[i])
            while sq["pend"]:
                tm = add_square()
            b = sq["b"]
            sq.clear()
            while fetched[0] < min(used[0] + CUT - 1, len(pieces)):
                fetch()
            t = V.ts(ms, banks[b][:, 0:T], 1.0 / n, eps, MUL, ADD, tm, *norm_free[0])
            PS.give(b, t)
            t = V.recip(rr, ms, t)
            t = A.act(rr, rr, ACT.Sqrt, t)
            res = []
            for i in range(nk):
                w = W(wname[0], wname[1] + i)
                if isinstance(outs[i], tuple):
                    s, sf = scr.take()
                    tv = V.stt(s, chunks[i], w, rr, MUL, MUL, t, toks[i], *sf)
                    r = cutup(*outs[i], s, (G, V, G)[i % 3], tv)
                    scr.give(s, r)
                    res.append(r)
                else:
                    tv = V.stt(outs[i], chunks[i], w, rr, MUL, MUL, t, toks[i])
                    res.append(tv)
            norm_free[0] = [tv]
            return res

        hno = top[0]
        hnr = alloc(2, 16, T, dt=F32R)
        hn_out = [(hnr[:, 0, i, :], hnr[:, 1, i, :]) for i in range(16)]
        hchunks = [h[:, i, :] for i in range(16)]
        tn = rms(hchunks, htok, ("attn_norm_w", 0), hn_out, D, 1e-6)
        ntok = lambda kc: tn[kc]
        nrhs = lambda kc: hn_out[kc]

        u = alloc(8, T)
        cq = alloc(4, T)
        ckv = alloc(2, T)
        kpe = alloc(T)
        utok, cqtok, ckvtok, kpetok = {}, {}, {}, {}

        def ev_in(t, b, tok):
            ps = b[:, 0:T]
            if t < 8:
                r = utok[t] = A.act(u[:, t, :], ps, ACT.Copy, tok)
            elif t < 12:
                r = cqtok[t - 8] = A.act(cq[:, t - 8, :], ps, ACT.Copy, tok)
            else:
                r = ckvtok[t - 12] = A.act(ckv[:, t - 12, :], ps, ACT.Copy, tok)
            return [r]

        def ev_kpe(t, b, tok):
            r = kpetok[0] = A.act(kpe, b[:, 0:T], ACT.Copy, tok)
            return [r]

        s5 = {n: alloc(32) for n in ("dt", "mag", "phi", "kf", "r", "sn", "cs", "sh", "ar", "ai", "den",
                                     "zr", "zi", "t1", "t2")}
        Cw = [alloc(32, 32) for _ in range(2)]
        Bw = [alloc(8, 128) for _ in range(2)]
        tl = [load(Cw[0], d["cre"]), load(Cw[1], d["cim"]), load(Bw[0], d["bre"]), load(Bw[1], d["bim"])]
        for q in ENG:
            q.wait(tl)
        NB = 4
        Cz = Cw
        tabo = top[0]
        tabs = [[alloc(NB, T) for _ in range(2)] for _ in range(2)]
        pwc, pws = alloc(8, 32), alloc(8, 32)
        tmpA, tmpB = alloc(NB, 128), alloc(NB, 128)

        MAGIC = 12582912.0
        PC = []
        rest = 2 * math.pi
        for bits in (8, 8, 10):
            e = math.floor(math.log2(rest))
            q_ = math.floor(rest / 2.0 ** (e - bits + 1)) * 2.0 ** (e - bits + 1)
            PC.append(q_)
            rest -= q_
        PC.append(float(np.float32(rest)))

        def sincos(ang, kf, r, sn, cs, sh, tok, *needs):
            t = V.ts(kf, ang, 1.0 / (2 * math.pi), MAGIC, MUL, ADD, tok, *needs)
            t = V.ts(kf, kf, MAGIC, None, SUB, None, t)
            t = V.stt(r, kf, -PC[0], ang, MUL, ADD, t)
            for c in PC[1:]:
                t = V.stt(r, kf, -c, r, MUL, ADD, t)
            t = V.ts(r, r, 3.1415925, -3.1415925, MIN, MAX, t)
            ta = A.act(sn, r, ACT.Sin, t)
            tb = A.act(sh, r, ACT.Sin, t, scale=0.5)
            t = V.tt(sh, sh, sh, MUL, tb)
            t = V.ts(cs, sh, -2.0, 1.0, MUL, ADD, t)
            return [ta, t]

        def s5_params():
            k = s5
            t = A.act(k["dt"], WR("ldt"), ACT.Exp)
            t1 = V.tt(k["t1"], WR("lr"), k["dt"], MUL, t)
            t2 = V.tt(k["phi"], WR("li"), k["dt"], MUL, t)
            tm = A.act(k["mag"], k["t1"], ACT.Exp, t1)
            tk = sincos(k["phi"], k["kf"], k["r"], k["sn"], k["cs"], k["sh"], t2)
            yield
            t = V.tt(k["ar"], k["mag"], k["cs"], MUL, tm, *tk)
            t = V.ts(k["ar"], k["ar"], -1.0, None, ADD, None, t)
            ta = V.tt(k["ai"], k["mag"], k["sn"], MUL)
            t = V.tt(k["den"], WR("lr"), WR("lr"), MUL)
            t = V.tt(k["t1"], WR("li"), WR("li"), MUL, tm)
            t = V.tt(k["den"], k["den"], k["t1"], ADD, t)
            t = V.recip(k["den"], k["den"], t)
            t = V.tt(k["t1"], k["ar"], WR("lr"), MUL, t)
            t = V.tt(k["t2"], k["ai"], WR("li"), MUL, ta, t)
            t = V.tt(k["t1"], k["t1"], k["t2"], ADD, t)
            t = V.tt(k["zr"], k["t1"], k["den"], MUL, t)
            t = V.tt(k["t1"], k["ai"], WR("lr"), MUL, t)
            t = V.tt(k["t2"], k["ar"], WR("li"), MUL, t)
            t = V.tt(k["t1"], k["t1"], k["t2"], SUB, t)
            t = V.tt(k["zi"], k["t1"], k["den"], MUL, t)
            t = V.ts(k["ar"], k["zr"], -1.0, None, MUL, None, t)
            t = V.ts(k["den"], k["zi"], -1.0, None, MUL, None, t)
            yield
            zr, nr, ni = (k[n].unsqueeze(2).broadcast_to([128, 32, 32]) for n in ("zr", "ar", "den"))
            tmp, tmp2 = (v.rearrange("p a b -> p (a b)").rearrange("p (a b) -> p a b", b=32) for v in tabs[1])
            g = G.tt(tmp, Cw[1], ni, MUL, t)
            g = G.tt(tmp2, Cw[0], ni, MUL, g)
            g = G.tt(Cw[0], Cw[0], zr, MUL, g)
            g = G.tt(Cw[0], Cw[0], tmp, ADD, g)
            g = G.tt(Cw[1], Cw[1], nr, MUL, g)
            s5["done"] = G.tt(Cw[1], Cw[1], tmp2, ADD, g)
            t = V.copy(pwc[:, 0, :], k["cs"], t)
            t = V.copy(pws[:, 0, :], k["sn"], t)
            for n in range(7):
                t = V.tt(k["t1"], pwc[:, n, :], pwc[:, n, :], MUL, t)
                t = V.tt(k["t2"], pws[:, n, :], pws[:, n, :], MUL, t)
                t = V.tt(pwc[:, n + 1, :], k["t1"], k["t2"], SUB, t)
                t = V.stt(pws[:, n + 1, :], pwc[:, n, :], 2.0, pws[:, n, :], MUL, MUL, t)
                if n % 2:
                    yield
            s5["pw"] = t
            yield

        tabtok = {}

        def tables(c, *needs):
            tc, tsn = tabs[c % 2]
            tv = V.mset(tc[:, :, 0:1], 1.0, s5["pw"], s5["done"] if c else None, tabtok.get(c - 1), *needs)
            tg = V.mset(tsn[:, :, 0:1], 0.0)
            for lv in range(8):
                n = 1 << lv
                ecb = pwc[:, lv, NB * c:NB * c + NB].unsqueeze(2).broadcast_to([128, NB, n])
                esb = pws[:, lv, NB * c:NB * c + NB].unsqueeze(2).broadcast_to([128, NB, n])
                a, b = tc[:, :, 0:n], tsn[:, :, 0:n]
                co, si = tc[:, :, n:2 * n], tsn[:, :, n:2 * n]
                q = G if lv > 3 else V
                both = [tv, tg]
                t1 = V.tt(co, a, ecb, MUL, both)
                t2 = V.tt(tmpA[:, :, 0:n], b, esb, MUL, both)
                u1 = q.tt(si, b, ecb, MUL, both)
                u2 = q.tt(tmpB[:, :, 0:n], a, esb, MUL, both)
                tv = V.tt(co, co, tmpA[:, :, 0:n], SUB, t1, t2)
                tg = q.tt(si, si, tmpB[:, :, 0:n], ADD, u1, u2)
                yield
            tabtok[c] = [tv, tg]

        def chain(*gens):
            for g in gens:
                yield from g

        run(mix((linear("w_in", 8, 16, nrhs, ntok, ev_in), 1), (chain(s5_params(), tables(0)), 1)))

        def seq(dct, n):
            return [dct[i] for i in range(n)]

        hn = within(hno, 16, T)
        hno2 = hno + 4096
        cqr = within(hno2, 2, 4, T, dt=F32R)
        ckr = within(hno2 + 2048, 2, 2, T, dt=F32R)
        kz = within(hno2 + 3072, 2, T)
        pt2s = [(within(hno2 + 3584, T), within(hno2 + 3840, T)), (cq[:, 0, :], cq[:, 1, :])]
        y = alloc(8, T)
        ytok = {}
        wz = Pool([(alloc(2, T), alloc(2, T), alloc(2, T)) for _ in range(2)])

        def ssm_tile(c, q, yb, yfree, state):
            j = 4 * c + q
            tab = tabs[c % 2]
            b, free = PS.take()
            bk = banks[b][:, :].rearrange("p (r t) -> p r t", r=2)
            for r in range(2):
                tm = P.mm(bk[:, r, :], Bw[r][32 * q:32 * q + 32, c, :], u[32 * q:32 * q + 32, c, :],
                          True, True, utok[c], *free, sig=True)
            (wa, wb, wc), wf = wz.take()
            cb = tab[0][:, q, :].unsqueeze(1).broadcast_to([128, 2, T])
            sb_ = tab[1][:, q, :].unsqueeze(1).broadcast_to([128, 2, T])
            yield
            ta = V.tt(wa, bk, cb, MUL, tm, tabtok[c], *wf)
            tb = V.tt(wb, bk, sb_, MUL)
            PS.give(b, tb)
            t1 = V.tt(wc[:, 0, :], wa[:, 0, :], wb[:, 1, :], ADD, tb)
            t2 = G.tt(wc[:, 1, :], wa[:, 1, :], wb[:, 0, :], SUB, tb, *wf)
            yield
            mg = s5["mag"][:, j:j + 1].broadcast_to([128, T])
            t1 = V.scan(wa[:, 0, :], mg, wc[:, 0, :], t1, t2)
            t2 = V.scan(wa[:, 1, :], mg, wc[:, 1, :], t1, t2)
            yield
            t3 = V.tt(wb, wa, cb, MUL, t2)
            t4 = G.tt(wc, wa, sb_, MUL, t2, tabtok[c])
            yield
            t5 = V.tt(wa[:, 0, :], wb[:, 0, :], wc[:, 1, :], SUB, t3, t4)
            t6 = V.tt(wa[:, 1, :], wb[:, 1, :], wc[:, 0, :], ADD, t3, t4)
            yield
            yp = banks[yb][32 * q:32 * q + 32, 0:T]
            P.mm(yp, Cz[0][:, j, :], wa[:, 0, :], True, False, t5, s5["done"], *yfree)
            tm = P.mm(yp, Cz[1][:, j, :], wa[:, 1, :], False, True, t6, sig=True)
            wz.give((wa, wb, wc), tm)
            state.append(t6)
            state.append(tm)
            state.append(t4)

        def ssm_chunk(c):
            yb, yfree = PS.take()
            st = []
            yield from flight(lambda q: ssm_tile(c, q, yb, yfree, st), 4, 2)
            s, sf = scr.take()
            t = V.stt(s, u[:, c, :], W("ssm_d", c), banks[yb][:, 0:T], MUL, ADD, *st, *sf)
            PS.give(yb, t)
            t = A.act(y[:, c, :], s, ACT.Gelu_apprx_tanh, t)
            scr.give(s, t)
            ytok[c] = t
            s5[("last", c)] = st

        def ssm_all():
            for c in range(8):
                gs = [(ssm_chunk(c), 1)]
                if c < 7:
                    gs.append((tables(c + 1, *s5.get(("last", c - 1), [])), 1))
                yield from mix(*gs)

        cqn = cq
        ckn = ckv
        qn = hn[:, 0:8, :]
        kn = hn[:, 8:16, :]
        qp = alloc(4, T)
        o = h[:, 0:8, :]
        vt = h[:, 8:16, :].rearrange("p (a b) c -> p a (b c)", a=2)
        pos = alloc(T)
        pf_ = alloc(2 * T)
        posi = pf_.bitcast(I32)
        ak, ar_ = pf_[:, 0:T], pf_[:, T:2 * T]
        csn, ssn, ash = (alloc(T) for _ in range(3))
        pt2 = Pool(pt2s)
        sm = alloc(16, 4)
        qtok, qptok, ktok_, vtok, otok = {}, {}, {}, {}, {}

        def angles():
            tl = load(posi, d["pos"].partition_broadcast(128), q=A)
            t = V.copy(pos, posi[:, 0:2 * T:2], tl)
            t = V.ts(pos, pos, C("ifr"), None, MUL, None, t)
            s5["rope"] = sincos(pos, ak, ar_, ssn, csn, ash, t)
            yield

        def mla():
            barrier()
            cqt = rms([cq[:, i, :] for i in range(4)], seq(cqtok, 4), ("mla_q_norm_w", 0),
                      [(cqr[:, 0, i, :], cqr[:, 1, i, :]) for i in range(4)], 512, 1e-6)
            ckt = rms([ckv[:, i, :] for i in range(2)], seq(ckvtok, 2), ("mla_kv_norm_w", 0),
                      [(ckr[:, 0, i, :], ckr[:, 1, i, :]) for i in range(2)], 256, 1e-6)
            yield
            tcs = s5["rope"]

            def rope(dst, src, tok):
                b, free = PS.take()
                tm = P.mm(banks[b][:, 0:T], C("perm"), src, True, True, tok, *free, sig=True)
                s, sf = scr.take()
                t1 = V.tt(s, banks[b][:, 0:T], ssn, MUL, tm, *tcs, *sf)
                PS.give(b, t1)
                t2 = V.tt(dst, src, csn, MUL, tm, *tcs)
                t = V.tt(dst, dst, s, ADD, t1, t2)
                scr.give(s, t)
                return t

            tk = rope(kpe, kpe, kpetok[0])
            for z in range(2):
                tkz = V.ts(kz[:, z, :], kpe, C("kp", z, z + 1), None, MUL, None, tk)
            yield

            ropes = []

            def turn_last():
                if ropes:
                    i, r = ropes.pop()
                    qptok[i] = rope(qp[:, i, :], qp[:, i, :], r)

            def ev_q(t, b, tok):
                if t < 8:
                    r = qtok[t] = A.act(qn[:, t, :], b[:, 0:T], ACT.Copy, tok)
                    return [r]
                r = A.act(qp[:, t - 8, :], b[:, 0:T], ACT.Copy, tok)
                turn_last()
                ropes.append((t - 8, r))
                return [r]

            yield from linear("w_uq", 12, 4, lambda kc: (cqr[:, 0, kc, :], cqr[:, 1, kc, :]), lambda kc: cqt[kc], ev_q)
            turn_last()

            def ev_k(t, b, tok):
                r = ktok_[t] = A.act(kn[:, t, :], b[:, 0:T], ACT.Copy, tok)
                return [r]

            yield from linear("w_uk", 8, 2, lambda kc: (ckr[:, 0, kc, :], ckr[:, 1, kc, :]), lambda kc: ckt[kc], ev_k)
            pc = [piece("w_uv", 0, 0, 0), piece("w_uv", 0, 0, PIECE, CUT - 1)]
            for hf in range(2):
                HS = slice(hf * 128, (hf + 1) * 128)
                for n in range(2):
                    NS = slice(n * 512, (n + 1) * 512)
                    b, free = PS.take()
                    for k in range(2):
                        hv, lv, c, tok = pc[k]
                        P.mm(banks[b][:, :], ckr[:, 0, k, HS], hv[:, NS], k == 0, False, tok, ckt[k], *free)
                        P.mm(banks[b][:, :], ckr[:, 0, k, HS], lv[:, NS], False, False)
                        tm = P.mm(banks[b][:, :], ckr[:, 1, k, HS], hv[:, NS], False, k == 1, sig=True)
                        cut_free[c] = [tm]
                    r = A.act(vt[:, hf, NS], banks[b][:, :], ACT.Copy, tm)
                    PS.give(b, r)
                    vtok[(hf, n)] = r
                yield

            scale = float((128 + 64) ** -0.5)

            def head(i):
                hd, hf = i // 2, i % 2
                n = 128 * (hf + 1)
                b, free = PS.take()
                sp_ = banks[b][:, 0:n]
                P.mm(sp_, qn[:, hd, hf * 128:(hf + 1) * 128], kn[:, hd, 0:n], True, False,
                     qtok[hd], ktok_[hd], *free)
                tm = P.mm(sp_, qp[:, hd // 2, hf * 128:(hf + 1) * 128], kz[:, hd % 2, 0:n], False, True,
                          qptok[hd // 2], tkz, sig=True)
                (sa, sb_), sf = pt2.take()
                yield
                zc = C("zc", 128 - 128 * hf, 256)
                s4 = sm[:, i, :]
                t = V.stt(sa[:, 0:n], sp_, scale, zc, MUL, ADD, tm, *sf)
                PS.give(b, t)
                t = V.red(s4[:, 0:1], sa[:, 0:n], MAX, t)
                t = V.ts(s4[:, 1:2], s4[:, 0:1], -1.0, None, MUL, None, t)
                t = A.act(sa[:, 0:n], sa[:, 0:n], ACT.Exp, t, bias=s4[:, 1:2], acc=s4[:, 2:3])
                yield
                t = V.recip(s4[:, 3:4], s4[:, 2:3], t)
                t = V.ts(sa[:, 0:n], sa[:, 0:n], s4[:, 3:4], None, MUL, None, t)
                yield
                b, free = PS.take()
                for k in range(hf + 1):
                    tm = P.tp(banks[b][:, k * 128:(k + 1) * 128], sa[:, k * 128:(k + 1) * 128], ident,
                              t, *free, sig=True)
                yield
                t = A.act(sb_[:, 0:n], banks[b][:, 0:n], ACT.Copy, tm)
                PS.give(b, t)
                yield
                b, free = PS.take()
                for k in range(hf + 1):
                    tm = P.mm(banks[b][:, 0:128], vt[:, k, hd * 128:(hd + 1) * 128],
                              sb_[:, k * 128:(k + 1) * 128], k == 0, k == hf, t, vtok[(k, hd // 4)],
                              *free, sig=True)
                pt2.give((sa, sb_), tm)
                t = A.act(o[:, hd, hf * 128:(hf + 1) * 128], banks[b][:, 0:128], ACT.Copy, tm)
                PS.give(b, t)
                otok[i] = t

            yield from flight(head, 16, 2)
            t2 = rms([o[:, i, :] for i in range(8)], [otok[2 * i + 1] for i in range(8)],
                     ("mla_out_norm_w", 0), hn_out[8:16], 1024, 1e-6)
            tl = load(h, d["xT"], t2, V.now(), P.now(), q=A)
            for i in range(16):
                htok[i] = tl
            yield
            yield from linear("w_out", 16, 16, nrhs, lambda kc: t2[kc - 8], ev_res, k0=8)

        htok = [None] * 16

        def ev_res(t, b, tok):
            htok[t] = V.tt(h[:, t, :], h[:, t, :], b[:, 0:T], ADD, tok, htok[t])
            if sq:
                square(h[:, t, :], htok[t])
            return [htok[t]]

        run(mix((chain(angles(), linear("w_in", 6, 16, nrhs, ntok, ev_in, t0=8),
                       linear("w_kpe", 1, 16, nrhs, ntok, ev_kpe), mla()), 1),
                (ssm_all(), SSM_STEPS)))

        y2tok = {}
        y2 = u
        barrier()
        yr = within(tabo, 2, 8, T, dt=F32R)
        yct = [cutup(yr[:, 0, i, :], yr[:, 1, i, :], y[:, i, :], (V, G)[i % 2], ytok[i]) for i in range(8)]

        def ev_glu(t, b, tok):
            s, sf = scr.take()
            r = A.act(s, b[:, 0:T], ACT.Sigmoid, tok, *sf, bias=W("ssm_b_glu", t))
            y2tok[t] = V.tt(y2[:, t, :], y[:, t, :], s, MUL, r)
            scr.give(s, y2tok[t])
            return [r]

        run(linear("w_glu", 8, 8, lambda kc: (yr[:, 0, kc, :], yr[:, 1, kc, :]), lambda kc: yct[kc], ev_glu))
        t1 = rms([y2[:, i, :] for i in range(8)], seq(y2tok, 8), ("ssm_out_norm_w", 0),
                 hn_out[0:8], 1024, 1e-6)
        squares(16)
        run(linear("w_out", 16, 16, nrhs, lambda kc: t1[kc], ev_res, k1=8))
        barrier()

        ffo = base + 2 * 16 * T
        far = within(ffo, 2, 22, T, dt=F32R)
        top[0] = ffo + 2 * 22 * T
        cvs = Pool([alloc(2, T) for _ in range(4)])
        tn = rms(hchunks, htok, ("ffn_norm_w", 0), hn_out, D, 1e-6)
        ftok, gbuf = {}, {}
        fdone = [[]]

        def frhs(kc):
            return far[:, 0, kc % 22, :], far[:, 1, kc % 22, :]

        def ev_conv(t, b, tok):
            j, val = t // 2, t % 2
            i = j + 44 * val
            if not val:
                gbuf[j] = cvs.take()
            cb, cf = gbuf[j]
            s = cb[:, val, :]
            ps = b[:, 0:T]
            t0 = A.act(s, ps, ACT.Identity, tok, *cf, bias=W("ffn_conv_b", i), scale=W("cw2", i))
            t1 = V.stt(s[:, 1:T], ps[:, 0:T - 1], W("cw1", i), s[:, 1:T], MUL, ADD, t0)
            t1 = V.stt(s[:, 2:T], ps[:, 0:T - 2], W("cw0", i), s[:, 2:T], MUL, ADD, t1)
            if not val:
                gbuf[(j, "t")] = A.act(s, s, ACT.Silu, t1)
            else:
                tg = G.tt(s, cb[:, 0, :], s, MUL, t1, gbuf[(j, "t")])
                ftok[j] = cutup(*frhs(j), s, G, tg, *fdone[0])
                cvs.give(cb, ftok[j])
            return [t1]

        for q in range(2):
            run(linear("w_up", 44, 16, nrhs, ntok, ev_conv, t0=44 * q))
            if q:
                squares(16)
            run(linear("w_down", 16, 44, frhs, lambda kc: ftok[kc], ev_res, k0=22 * q, k1=22 * q + 22))
            fdone[0] = [P.now()]
        tf = rms(hchunks, htok, ("final_norm_w", 0), hchunks, D, 1e-6)
        htok = list(tf)

        top[0] = ffo
        tn = rms(hchunks, htok, ("norm1_g_2", 0), hn_out, D, 1e-6)
        sv = [sem("s_hsave"), sem("s_ysave")]
        A.wait(V.now(), A.now(), G.now())
        A.items.append(lambda e: e.dma_start(d["hsave"], h).then_inc(sv[0], 16))
        hst = [(sv[0], 16)]
        gdr = alloc(2, 2, T, dt=F32R)
        wd, ad = alloc(T), alloc(T)
        sm2 = alloc(1)
        mark = top[0]
        dt_, cs_ = wd, ad
        ztok, xtok, bctok, xdtok = {}, {}, {}, {}
        st = {}

        def ev_z(t, b, tok):
            r = ztok[t] = A.act(z[:, t, :], b[:, 0:T], ACT.Silu, tok)
            return [r]

        def ev_dt(t, b, tok):
            R = slice(96, 128)
            bufs = [scr.take() for _ in range(4)]
            V.wait(*[q[1] for q in bufs])
            A.wait(*[q[1] for q in bufs])
            t0 = V.ts(bufs[0][0][R, :], b[R, 0:T], W("dtb")[R, :], None, ADD, None, tok)
            st["dt"] = bufs, t0
            return [t0]

        def later():
            while "dt" not in st:
                yield

        def steps_dt():
            R = slice(96, 128)
            bufs, t0 = st["dt"]
            a, e, w, p = (q[0][R, :] for q in bufs)
            t = V.ts(w, a, -1.0, None, MUL, None, t0)
            t = V.tt(w, w, a, MIN, t)
            t = A.act(e, w, ACT.Exp, t)
            yield
            t = V.ts(w, e, 2.0, None, ADD, None, t)
            t = V.recip(w, w, t)
            t = V.tt(e, e, w, MUL, t)
            t = V.tt(w, e, e, MUL, t)
            cf = [1.0 / (2 * k + 1) for k in range(10)]
            t = V.ts(p, w, cf[9], cf[8], MUL, ADD, t)
            yield
            for k in range(7, -1, -1):
                t = V.tt(p, p, w, MUL, t)
                t = V.ts(p, p, cf[k], None, ADD, None, t)
                if k % 2:
                    yield
            t = V.stt(p, e, 2.0, p, MUL, MUL, t)
            t = V.stt(dt_[R, :], a, 0.0, p, MAX, ADD, t)
            ta = A.act(sm2[R, :], W("alog")[R, :], ACT.Exp)
            t = V.ts(sm2[R, :], sm2[R, :], -1.0, None, MUL, None, ta, t)
            t = V.ts(p, dt_[R, :], sm2[R, :], None, MUL, None, t)
            tcs = V.scan(cs_[R, :], C("ones", 0, 1)[R, :].broadcast_to([32, T]), p, t)
            st["cs"] = tcs
            for q in bufs:
                scr.give(q[0], tcs)
            yield

        def turn_dt():
            R = slice(96, 128)
            tcs = st["cs"]
            b2, free = PS.take()
            bk = banks[b2]
            for hf in range(2):
                P.tp(bk[:, hf * 32:hf * 32 + 32], dt_[R, hf * 128:(hf + 1) * 128], ident[R, 96:128], tcs, *free)
                tm = P.tp(bk[:, 64 + hf * 32:96 + hf * 32], cs_[R, hf * 128:(hf + 1) * 128], ident[R, 96:128],
                          tcs, sig=True)
            r = V.copy(dtT, bk[:, 0:64].rearrange("p (a b) -> p a b", a=2), tm)
            st["csT"] = V.copy(csT, bk[:, 64:128].rearrange("p (a b) -> p a b", a=2), tm)
            st["dtT"] = r
            PS.give(b2, r, st["csT"])

        shp = Pool([alloc(T) for _ in range(2)])
        FULL = slice(0, 128)

        def shift(dst, b, mu, R, tok, *needs):
            n = R.stop
            s, sf = shp.take()
            v = b[R, 0:T]
            s, ss = s[R, :], s
            t0 = A.act(ss[R, :], v, ACT.Copy, tok, *sf)
            dd, df = scr.take()
            t1 = V.tt(dd[R, 1:T], s[:, 0:T - 1], v[:, 1:T], SUB, t0, *df)
            t2 = V.ts(dd[R, 0:1], s[:, 0:1], -1.0, None, MUL, None, t0)
            if len(dst.shape) == 3:
                t = V.stt(dst, dd[R, :].rearrange("p (a b) -> p a b", a=2), mu,
                          s.rearrange("p (a b) -> p a b", a=2), MUL, ADD, t1, t2, *needs)
            else:
                t = V.stt(dst, dd[R, :], mu, s, MUL, ADD, t1, t2, *needs)
            scr.give(dd, t)
            shp.give(ss, t)
            return t

        small = {}

        def ev_wd(t, b, tok):
            R = slice(0, 96)
            r = shift(wd[R, :], b, W("mu_wd")[R, :], R, tok)
            small["wd"] = A.act(wd[R, :], wd[R, :], ACT.Tanh, r)
            return [r]

        def ev_ad(t, b, tok):
            R = slice(0, 96)
            small["ad"] = shift(ad[R, :], b, W("mu_ad")[R, :], R, tok)
            return [small["ad"]]

        def ev_gd(t, b, tok):
            s, sf = scr.take()
            r = shift(s, b, W("mu_gd", t), FULL, tok, *sf)
            ta = A.act(s, s, ACT.Sigmoid, r)
            small[("gd", t)] = cutup(gdr[:, 0, t, :], gdr[:, 1, t, :], s, G, ta)
            scr.give(s, small[("gd", t)])
            return [r]

        def ev_sm(t, b, tok):
            if t == 0:
                r = ev_wd(t, b, tok)
                return ev_dt(t, b, tok) + r
            return ev_ad(t, b, tok) if t == 1 else ev_gd(t - 2, b, tok)


        def conv4(dst, ps, i, tok, *needs):
            s, cf = cvs4.take()
            t = A.act(s, ps, ACT.Identity, tok, *cf, bias=W("ssd_conv_b_2", i), scale=W("dw3", i))
            for sh, nm in ((1, "dw2"), (2, "dw1"), (3, "dw0")):
                t = V.stt(s[:, sh:T], ps[:, 0:T - sh], W(nm, i), s[:, sh:T], MUL, ADD, t)
            r = A.act(dst, s, ACT.Silu, t, *needs)
            cvs4.give(s, r)
            return t, r

        xT = h
        cvs4 = Pool([])

        def ev_bc(t, b, tok):
            t1, bctok[t - 16] = conv4(bc[:, t - 16, :], b[:, 0:T], t, tok, stok[5])
            return [t1]

        def ev_x(t, b, tok):
            t1, xtok[t] = conv4(xT[:, t, :], b[:, 0:T], t, tok)
            return [t1]

        def turn_x():
            for t in range(16):
                b2, free = PS.take()
                for hf in range(2):
                    tm = P.tp(banks[b2][:, hf * 128:(hf + 1) * 128], xT[:, t, hf * 128:(hf + 1) * 128], ident,
                              xtok[t], *free, sig=True)
                for hf in range(2):
                    dtb = dtT[:, hf, 2 * t:2 * t + 2].unsqueeze(2).broadcast_to([128, 2, 64])
                    xdtok[t] = V.tt(xd[:, hf, t * 128:(t + 1) * 128].rearrange("p (a b) -> p a b", a=2),
                                    banks[b2][:, hf * 128:(hf + 1) * 128].rearrange("p (a b) -> p a b", a=2),
                                    dtb, MUL, tm, st["dtT"])
                PS.give(b2, xdtok[t])
                yield

        PL = alloc(16, 8)
        scp = Pool([ms, rr, C("zc"), alloc(T)])
        for q in (V, A):
            q.wait(norm_free[0])
        p33 = Pool([alloc(8, 33) for _ in range(2)])
        bufo = top[0]
        BUF = [(alloc(2, 2, 2, 128), alloc(2, T), alloc(2, T), alloc(2, T)) for _ in range(3)]

        def AR(i):
            return BUF[(i // 2) % 3][0][:, i % 2]

        def KK(i):
            return BUF[(i // 2) % 3][1][:, i % 2, :]

        def VV(i):
            return BUF[(i // 2) % 3][2][:, i % 2, :]

        def BB(i):
            return BUF[(i // 2) % 3][3][:, i % 2, :]

        XA, XB, XX = alloc(32, 32), alloc(32, 32), alloc(32, 32)
        XTs = [alloc(32, 8) for _ in range(2)]
        xtmp = alloc(T)
        w2s = h[:, 0:8, :].rearrange("p a b -> p (a b)")
        a2s = h[:, 8:16, :].rearrange("p a b -> p (a b)")
        tl = [load(w2s[0:96, :], d["w2"], hst, q=A), load(a2s[0:96, :], d["a2"], q=A)]
        stok, bfree = {}, {}
        ktk, vtk, rtk = {}, {}, {}


        def ev_r(t, b, tok):
            rtk[t] = shift(AR(t)[:, :, 1, :], b, W("mu_r", t), FULL, tok)
            return [rtk[t]]

        def ev_kk(t, b, tok):
            ktk[t] = shift(KK(t), b, W("mu_k", t), FULL, tok)
            return [ktk[t]]

        def ev_vv(t, b, tok):
            vtk[t] = shift(VV(t), b, W("mu_v", t), FULL, tok, stok.get(t // 2 - 3))
            return [vtk[t]]

        def ev_krv(t, b, tok):
            return (ev_kk, ev_r, ev_vv)[t % 6 // 2](t // 6 * 2 + t % 2, b, tok)

        def proj(b):
            if b >= 3:
                for q in (V, A, G):
                    q.wait(*bfree[b - 3])
            yield from linear("w_krv", 6, 16, nrhs, ntok, ev_krv, t0=6 * b, step=4)

        def prep(i):
            b, free = PS.take()
            P.mm(banks[b][:, 0:T], w2s[0:96, i * 128:(i + 1) * 128], wd[0:96, :], True, True, small["wd"],
                 tl, *free)
            tm = P.mm(banks[b][:, T:2 * T], a2s[0:96, i * 128:(i + 1) * 128], ad[0:96, :], True, True,
                      small["ad"], sig=True)
            s1, f1 = scr.take()
            s2, f2 = scr.take()
            s3, f3 = scp.take()
            yield
            tsg = A.act(s1, banks[b][:, 0:T], ACT.Sigmoid, tm, *f1, bias=W("rwkv_w0_2", i))
            ta = A.act(s2, banks[b][:, T:2 * T], ACT.Sigmoid, tm, *f2, bias=W("rwkv_a0_2", i))
            PS.give(b, tsg, ta)
            t = V.ts(s1, s1, -math.exp(-0.5), None, MUL, None, tsg)
            tcm = V.scan(s3, C("rm"), s1, t, *f3)
            pb, pf = p33.take()
            c3 = s3.rearrange("p (a b) -> p a b", b=32)
            s4, f4 = scp.take()
            kk = s1
            t = V.ts(kk, KK(i), W("rwkv_k_k_2", i), None, MUL, None, ktk[i], tcm)
            t4 = A.act(s4, kk, ACT.Square, t, *f4)
            t = V.mset(pb[:, :, 0:1], 1.0, *pf)
            yield
            b, free = PS.take()
            tm = P.mm(banks[b][:, 0:T], blk, s4, True, True, t4, *free, sig=True)
            tp_ = A.act(pb[:, :, 1:33], c3, ACT.Exp, tcm, *pf)
            tip = A.act(s3, s3, ACT.Exp, tp_, scale=-1.0)
            t5 = V.ts(s4, s2, -1.0, W("rwkv_k_a_2", i), ADD, MUL, ta, tm)
            t5 = V.stt(s4, s4, 1.0, KK(i), ADD, MUL, t5)
            yield
            tpl = V.copy(PL[:, i, :].unsqueeze(2), pb[:, :, 32:33], tp_)
            tkf = V.tt(KK(i), s4, s3, MUL, t5, tip)
            yield
            t = V.ts(s4, banks[b][:, 0:T], 1e-24, None, MAX, None, tm, tkf)
            PS.give(b, t)
            t = V.recip(s4, s4, t)
            t = A.act(s4, s4, ACT.Sqrt, t)
            yield
            t = V.tt(kk, kk, s4, MUL, t)
            pp = pb[:, :, 0:32].rearrange("p (s a) b -> p s a b", s=2)
            k4 = kk.rearrange("p (s a b) -> p s a b", s=2, b=32)
            ta2 = V.stt(AR(i)[:, :, 0, :].rearrange("p s (a b) -> p s a b", b=32), k4, -1.0, pp, MUL, MUL, t)
            tb1 = V.tt(kk, kk, s2, MUL, ta2)
            tb2 = V.tt(BB(i), kk, s3, MUL, tb1)
            r4 = AR(i)[:, :, 1, :].rearrange("p s (a b) -> p s a b", b=32)
            tr2 = V.tt(r4, r4, pb[:, :, 1:33].rearrange("p (s a) b -> p s a b", s=2), MUL, rtk[i], tp_)
            p33.give(pb, tr2)
            for pool, x in ((scr, s1), (scr, s2), (scp, s3), (scp, s4)):
                pool.give(x, tr2, tb2)
            ptk[i] = tr2

        ptk, xtk, done = {}, {}, set()
        s32 = C("s32")

        def solve(b):
            bks = [PS.take() for _ in range(2)]
            for j in range(4):
                hf, i = j // 2, 2 * b + j % 2
                for e in range(2):
                    R = slice(64 * e, 64 * e + 64)
                    tm = P.mm(banks[bks[e][0]][:, j * 128:(j + 1) * 128], BB(i)[R, hf * 128:(hf + 1) * 128],
                              AR(i)[R, hf, 0, :], True, True, ptk[i], *bks[e][1], sig=True)
            yield
            if b > 0:
                finish(b - 1)
            for e in range(2):
                bk = banks[bks[e][0]][:, :].rearrange("p (j t) -> p t j", j=4)
                for c in range(4):
                    Q = slice(32 * c, 32 * c + 32)
                    t = V.tt(XA[Q, :, e:8:2], bk[Q, 32 * c:32 * c + 32, :],
                             s32[Q, :].unsqueeze(2).broadcast_to([32, 32, 4]), MUL, tm, xtk.get(b - 1))
                PS.give(bks[e][0], t)
            t = V.tr(XB.rearrange("p t g -> p (t g)"), XA.rearrange("p t g -> p (t g)"), t, xtk.get(b - 1))
            yield
            g = G.mset(XX, 0.0, t)
            g = G.mset(XX.rearrange("p t g -> p (t g)")[:, 0:1024:33], 1.0, g)
            for r in range(31):
                n = 31 - r
                prod = xtmp[:, 0:n * (r + 1)].rearrange("p (a b) -> p a b", b=r + 1)
                a4 = XB[:, r + 1:32, r:r + 1].broadcast_to([128, n, r + 1])
                x4 = XX[:, r:r + 1, 0:r + 1].broadcast_to([128, n, r + 1])
                g = G.tt(prod, a4, x4, MUL, g)
                x5 = XX[:, r + 1:32, 0:r + 1]
                g = G.tt(x5, x5, prod, ADD, g)
                if r % 8 == 7:
                    yield
            xtk[b] = g

        def finish(b):
            if b in done:
                return
            done.add(b)
            t = V.tr(XA.rearrange("p t g -> p (t g)"), XX.rearrange("p t g -> p (t g)"), xtk[b])
            xtk[b] = V.copy(XTs[b % 2], XA[:, :, 0:8], t)

        DEP = 2
        tokb = Pool([alloc(2, 128) for _ in range(DEP)])
        mskb = Pool([alloc(3, 128) for _ in range(2 * DEP)])
        bx = Pool([alloc(4, 128) for _ in range(DEP)])
        kx = Pool([alloc(4, 128) for _ in range(DEP)])
        gt = Pool([alloc(4, 128) for _ in range(DEP)])
        wu = Pool([alloc(256) for _ in range(DEP)])
        az = Pool([C("perm"), alloc(128)])
        qt = Pool([alloc(128) for _ in range(DEP)])
        o_ = VEC_AT["cw0"][0]
        xbd = Pool([alloc(128), alloc(128), vec[:, o_:o_ + 128], vec[:, o_ + 128:o_ + 256]])
        sbd = Pool([alloc(128) for _ in range(2 * DEP)])
        yb_ = Pool([alloc(256) for _ in range(DEP)])

        m3 = C("m3")
        bm = C("bm")
        vtk2 = {}

        def block(i, hf, state):
            TS = slice(hf * 128, (hf + 1) * 128)
            b, free = PS.take()
            bk = banks[b]
            P.tp(bk[:, 0:128], AR(i)[:, hf, 0, :], ident, ptk[i], vtk[i], *free)
            P.tp(bk[:, 128:256], VV(i)[:, TS], ident)
            P.tp(bk[:, 256:384], BB(i)[:, TS], ident)
            tm = P.tp(bk[:, 384:512], KK(i)[:, TS], ident, sig=True)
            tk, tf_ = tokb.take()
            bxb, bf = bx.take()
            kxb, kf_ = kx.take()
            m4 = C("bm4").unsqueeze(2).broadcast_to([128, 4, 128])
            tt_ = A.act(tk.rearrange("p a b -> p (a b)"), bk[:, 0:256], ACT.Copy, tm, *tf_)
            tbx = V.tt(bxb, bk[:, 256:384].unsqueeze(1).broadcast_to([128, 4, 128]), m4, MUL, tt_, *bf)
            tkx = V.tt(kxb, bk[:, 384:512].unsqueeze(1).broadcast_to([128, 4, 128]), m4, MUL, *kf_)
            PS.give(b, tkx)
            yield
            mks = []
            for e in range(2):
                R = slice(64 * e, 64 * e + 64)
                b, free = PS.take()
                P.mm(banks[b][:, 0:128], BB(i)[R, TS], AR(i)[R, hf, 1, :], True, True, *free)
                tm = P.mm(banks[b][:, 128:384], KK(i)[R, TS], AR(i)[R, hf, :, :].rearrange(
                    "p a b -> p (a b)"), True, True, sig=True)
                mk, mf = mskb.take()
                t = V.tt(mk.rearrange("p a b -> p (a b)"), banks[b][:, 0:384], m3, MUL, tm, *mf)
                PS.give(b, t)
                mks.append((mk, t))
                yield
            b, free = PS.take()
            for e in range(2):
                tm = P.mm(banks[b][:, 64 * e:64 * e + 64], mks[e][0][:, 1, :], tk[:, 1, 64 * e:64 * e + 64],
                          True, True, mks[e][1], tt_, *free, sig=True)
            azb, af = az.take()
            taz = V.copy(azb, banks[b][:, 0:128], tm, *af)
            PS.give(b, taz)
            finish(i // 2)
            xbs = []
            for e in range(2):
                ln = hf * 4 + i % 2 * 2 + e
                xb, xf = xbd.take()
                xbs.append((xb, V.tt(xb.rearrange("p (c t) -> p c t", c=4),
                                     XTs[i // 2 % 2][:, :, ln].unsqueeze(1).broadcast_to([128, 4, 32]),
                                     bm.rearrange("p (c t) -> p c t", c=4), MUL, xtk[i // 2], *xf)))
            yield
            b, free = PS.take()
            for e in range(2):
                xb, tx = xbs[e]
                P.mm(banks[b][:, 64 * e:64 * e + 64], xb, tk[:, 0, 64 * e:64 * e + 64], True, True, tx, *free)
                tm = P.mm(banks[b][:, 128 + 64 * e:192 + 64 * e], xb, azb[:, 64 * e:64 * e + 64], True, True,
                          taz, sig=True)
                xbd.give(xb, tm)
            az.give(azb, tm)
            wub, wf = wu.take()
            twu = V.copy(wub, banks[b][:, 0:256], tm, *wf)
            PS.give(b, twu)
            yield
            b, free = PS.take()
            for e in range(2):
                R = slice(64 * e, 64 * e + 64)
                tm = P.mm(banks[b][R, 0:128], wub[:, 64 * e:64 * e + 64], mks[e][0][:, 0, :], True, True, twu,
                          *free, sig=True)
            qb, qf = qt.take()
            tq = V.tt(qb, banks[b][:, 0:128], AR(i)[:, hf, 1, :], ADD, tm, *qf)
            PS.give(b, tq)
            yb, yfree = PS.take()
            for e in range(2):
                R = slice(64 * e, 64 * e + 64)
                P.mm(banks[yb][R, 0:128], wub[:, 128 + 64 * e:192 + 64 * e], mks[e][0][:, 0, :], True, False,
                     twu, *yfree)
                tm = P.mm(banks[yb][R, 0:128], tk[:, 1, 64 * e:64 * e + 64], mks[e][0][:, 2, :], False, True,
                          sig=True)
            for e in range(2):
                mskb.give(mks[e][0], tm)
            ybuf, ybf = state["y"]
            ty0 = A.act(ybuf[:, TS], banks[yb][:, 0:128], ACT.Copy, tm, *ybf)
            PS.give(yb, ty0)
            yield
            b, free = PS.take()
            tm = P.mm(banks[b][:, :], wub[:, 0:128], bxb.rearrange("p c k -> p (c k)"), True, True, tbx, twu,
                      *free, sig=True)
            gb, gf = gt.take()
            for e in range(2):
                R = slice(64 * e, 64 * e + 64)
                ii = ident[R, 64 * e:64 * e + 64].unsqueeze(1).broadcast_to([64, 4, 64])
                tg = V.tt(gb[R, :, 64 * e:64 * e + 64],
                          banks[b][R, :].rearrange("p (c k) -> p c k", c=4)[:, :, 64 * e:64 * e + 64], ii,
                          ADD, tm, *gf)
            PS.give(b, tg)
            yield
            yb, yfree = PS.take()
            for c in range(4):
                sb_, stok = state["s"]
                ty = P.mm(banks[yb][:, 32 * c:32 * c + 32], sb_, qb[:, 32 * c:32 * c + 32], True, True, stok,
                          tq, *(yfree if c == 0 else []), sig=True)
                b, free = PS.take()
                P.mm(banks[b][:, 0:128], bxb[:, c, :], wub[:, 128:256], True, False, tbx, twu, *free)
                P.mm(banks[b][:, 0:128], kxb[:, c, :], tk[:, 1, :], False, False, tkx)
                tm = P.mm(banks[b][:, 0:128], gb[:, c, :], sb_, False, True, tg, stok, sig=True)
                sbd.give(sb_, tm)
                sn, sf = sbd.take()
                ch = hf * 4 + c
                for e in range(2):
                    R = slice(64 * e, 64 * e + 64)
                    CS = slice(64 * e, 64 * e + 64)
                    if e == 0:
                        ts_a = V.ts(sn[R, CS], banks[b][R, CS], PL[R, i, ch:ch + 1], None, MUL, None, tm, *sf)
                    else:
                        ts_b = A.act(sn[R, CS], banks[b][R, CS], ACT.Copy, tm, *sf,
                                     scale=PL[R, i, ch:ch + 1])
                PS.give(b, ts_a, ts_b)
                state["s"] = (sn, [ts_a, ts_b])
                yield
            tokb.give(tk, tm)
            bx.give(bxb, tm)
            kx.give(kxb, tm)
            gt.give(gb, tm)
            wu.give(wub, tm)
            qt.give(qb, ty)
            ty2 = V.tt(ybuf[:, TS], ybuf[:, TS], banks[yb][:, 0:128], ADD, ty, ty0)
            PS.give(yb, ty2)
            state["yt"].append(ty2)
            yield

        def pair(i):
            state = {"y": yb_.take(), "yt": []}
            sb0, sf0 = sbd.take()
            tz_ = V.mset(sb0, 0.0, *sf0)
            state["s"] = (sb0, [tz_])
            for hf in range(2):
                yield from block(i, hf, state)
            sb_, stok = state["s"]
            sbd.give(sb_, *stok)
            yb = state["y"][0]
            b, free = PS.take()
            tm = P.mm(banks[b][:, 0:T], blk, yb, True, True, *state["yt"], *free, sig=True)
            s1, f1 = scr.take()
            t = V.stt(s1, banks[b][:, 0:T], -1.0 / 64, yb, MUL, ADD, tm, *f1)
            PS.give(b, t)
            s2, f2 = scr.take()
            t2 = A.act(s2, s1, ACT.Square, t, *f2)
            rk = yb.rearrange("p (a b) -> p a b", a=2)
            tr_ = V.stt(rk, AR(i)[:, :, 1, :], W("rwkv_r_k_2", i),
                        KK(i).rearrange("p (a b) -> p a b", a=2), MUL, MUL, t)
            yield
            b, free = PS.take()
            tm = P.mm(banks[b][:, 0:T], blk, s2, True, True, t2, *free, sig=True)
            t = V.ts(s2, banks[b][:, 0:T], 1.0 / 64, 64e-5, MUL, ADD, tm)
            PS.give(b, t)
            t = V.recip(s2, s2, t)
            t = A.act(s2, s2, ACT.Sqrt, t)
            yield
            b, free = PS.take()
            tb = P.mm(banks[b][:, 0:T], blk, yb, True, True, tr_, *free, sig=True)
            t = V.tt(s1, s1, s2, MUL, t)
            t = V.ts(s1, s1, W("rwkv_gn_w_2", i), W("rwkv_gn_b_2", i), MUL, ADD, t)
            t3 = V.tt(s2, banks[b][:, 0:T], VV(i), MUL, tb, t)
            PS.give(b, t3)
            vtk2[i] = V.tt(VV(i), s1, s2, ADD, t3)
            yb_.give(yb, vtk2[i])
            scr.give(s1, vtk2[i])
            scr.give(s2, vtk2[i])

        def ev_g(t, b, tok):
            vtk2[t] = V.tt(VV(t), VV(t), b[:, 0:T], MUL, tok, vtk2[t])
            return [vtk2[t]]

        def store(b):
            A.wait(vtk2[2 * b], vtk2[2 * b + 1])
            sm = sem(f"s_y{b}")
            dst, src = d["ysave"][:, 2 * b:2 * b + 2, :], BUF[b % 3][2]
            A.items.append(lambda e: e.dma_start(dst, src).then_inc(sm, 16))
            stok[b] = (sm, 16)

        run(mix((chain(linear("w_sm", 4, 16, nrhs, ntok, ev_sm), proj(0)), 1), (chain(later(), steps_dt()), 1)))
        zero = [G.mset(v, 0.0) for v in [XA] + [v for p_ in (gt, sbd) for v, _ in p_.free]]
        for q in (P, V, A):
            q.wait(zero)
        bc = within(bufo + 2 * 2560, 8, T)
        cvb = [within(bufo + 2 * 2560 + 2048, T), within(bufo + 2 * 2560 + 2304, T)]

        def gate(b):
            yield from linear("w_g2", 2, 2, lambda kc: (gdr[:, 0, kc, :], gdr[:, 1, kc, :]),
                              lambda kc: small[("gd", kc)], ev_g, t0=2 * b)
            store(b)

        def main(b):
            if b >= 2:
                yield from gate(b - 2)
            if b < 7:
                yield from proj(b + 1)
            elif b == 7:
                for q in (V, A, G):
                    q.wait(bfree[5])
                for x in cvb:
                    cvs4.give(x, stok[5])
                yield from linear("w_xbc", 8, 16, nrhs, ntok, ev_bc, t0=16, step=4)
            else:
                for q in (V, A, G):
                    q.wait(bfree[7])
                yield from linear("w_xbc", 16, 16, nrhs, ntok, ev_x)

        for b in range(9):
            turn = main(b)
            before = [pair(2 * b - 2 + i) if b > 0 else iter(()) for i in range(2)]
            after = chain(flight(lambda i, b=b: prep(2 * b + i), 2, 2), solve(b)) if b < 8 else iter(())
            run(mix((before[0], 1), (turn, 1), (before[1], 1), (after, 1)))
            bfree[b - 1] = [P.now(), V.now(), A.now()]
            if b == 7:
                bfree[7] = bfree[6]
        run(gate(7))
        barrier()

        top[0] = mark
        z = alloc(16, T)
        cbm = alloc(4, 384)
        dtT, csT = alloc(2, 32), alloc(2, 32)
        assert top[0] <= bufo + 2 * 2560
        top[0] = bufo + 3 * 2560
        sdo = top[0]
        xd = alloc(2, 2048)
        sw = Pool([alloc(384) for _ in range(4)])
        yl = alloc(16, T)
        sw2 = Pool([alloc(T) for _ in range(2)])
        for q in (V, A):
            q.wait(stok[7])
        tyl = load(yl, d["ysave"], *[stok[b] for b in range(8)], q=A)
        cbt = {}

        def turn_cb():
            for g in range(4):
                b, free = PS.take()
                P.mm(banks[b][:, 0:256], bc[:, g, 0:128], bc[:, 4 + g, :], True, True, bctok[g], bctok[4 + g],
                     *free)
                tm = P.mm(banks[b][:, 256:384], bc[:, g, 128:256], bc[:, 4 + g, 128:256], True, True, sig=True)
                V.tt(cbm[:, g, 0:256], banks[b][:, 0:256], C("cm"), MUL, tm)
                cbt[g] = V.tt(cbm[:, g, 256:384], banks[b][:, 256:384], C("cm", 0, 128), MUL)
                PS.give(b, cbt[g])
            yield
        ysst = {}

        def ssd_pair(i):
            yb, yfree = PS.take()
            last = []
            for e in range(2):
                hd = 2 * i + e
                g = hd // 8
                b, free = PS.take()
                sel = ident[96:128, 96 + hd:97 + hd].broadcast_to([32, 128])
                tm = P.mm(banks[b][:, 0:T], sel, cs_[96:128, :], True, True, st["cs"], *free, sig=True)
                w, wf = sw.take()
                yield
                V.ts(w[:, 0:256], banks[b][:, 0:T], csT[:, 0, hd:hd + 1], 0.0, SUB, MIN, tm, st["csT"], *wf)
                t = V.ts(w[:, 256:384], banks[b][:, 128:T], csT[:, 1, hd:hd + 1], 0.0, SUB, MIN)
                PS.give(b, t)
                t = A.act(w, w, ACT.Exp, t)
                yield
                t = V.tt(w, w, cbm[:, g, :], MUL, t, cbt[g])
                yield
                R = slice(64 * e, 64 * e + 64)
                P.mm(banks[yb][R, 0:256], xd[:, 0, hd * 64:hd * 64 + 64], w[:, 0:256], True, False, t,
                     xdtok[i], *yfree)
                tm = P.mm(banks[yb][R, 128:256], xd[:, 1, hd * 64:hd * 64 + 64], w[:, 256:384], False, True,
                          sig=True)
                sw.give(w, tm)
            yield
            s, sf = sw2.take()
            t = V.stt(s, xT[:, i, :], W("dskip", i), banks[yb][:, 0:T], MUL, ADD, tm, *sf)
            PS.give(yb, t)
            while i not in ztok:
                yield
            ysst[i] = V.tt(z[:, i, :], s, z[:, i, :], MUL, t, ztok[i])
            sw2.give(s, ysst[i])

        turn_dt()
        run(mix((linear("w_z", 16, 16, nrhs, ntok, ev_z), 1),
                (chain(turn_x(), turn_cb(), flight(ssd_pair, 16, 2)), 3)))
        barrier()
        tl = load(h, d["hsave"], q=A)
        htok = [tl] * 16
        vvr = within(hno, 2, 16, T, dt=F32R)
        vct = [cutup(vvr[:, 0, i, :], vvr[:, 1, i, :], yl[:, i, :], (V, G)[i % 2], tyl) for i in range(16)]
        ysr = within(sdo, 2, 16, T, dt=F32R)
        yct = {}

        def norm_ssd():
            for g in range(4):
                r = rms([z[:, 4 * g + i, :] for i in range(4)], [ysst[4 * g + i] for i in range(4)],
                        ("ssd_norm_g_2", 4 * g),
                        [(ysr[:, 0, 4 * g + i, :], ysr[:, 1, 4 * g + i, :]) for i in range(4)], 512, 1e-5)
                for i in range(4):
                    yct[4 * g + i] = r[i]
                yield

        for q in (V, A, G):
            q.wait(*vct)
        run(mix((linear("w_out2", 16, 32, lambda kc: (vvr[:, 0, kc - 16, :], vvr[:, 1, kc - 16, :]),
                        lambda kc: vct[kc - 16], ev_res, k0=16), 3), (norm_ssd(), 1)))
        squares(16)
        run(linear("w_out2", 16, 32, lambda kc: (ysr[:, 0, kc, :], ysr[:, 1, kc, :]), lambda kc: yct[kc],
                   ev_res, k1=16))
        barrier()
        top[0] = ffo + 2 * 22 * T
        cvs = Pool([alloc(T) for _ in range(4)])
        tn = rms(hchunks, htok, ("norm2_g_2", 0), hn_out, D, 1e-6)
        fdone[0] = []

        def ev_gu(t, b, tok):
            j, up = t // 2, t % 2
            if not up:
                s, sf = cvs.take()
                r = A.act(s, b[:, 0:T], ACT.Silu, tok, *sf)
                gbuf[j] = (s, r)
                return [r]
            s, r = gbuf[j]
            tg = V.tt(s, s, b[:, 0:T], MUL, tok, r)
            ftok[j] = cutup(*frhs(j), s, G, tg, *fdone[0])
            cvs.give(s, ftok[j])
            return [tg]

        for q in range(2):
            run(linear("w_gu", 44, 16, nrhs, ntok, ev_gu, t0=44 * q))
            if q:
                squares(16)
            run(linear("w_down2", 16, 44, frhs, lambda kc: ftok[kc], ev_res, k0=22 * q, k1=22 * q + 22))
            fdone[0] = [P.now()]
        tf = rms(hchunks, htok, ("norm_f_g_2", 0), hchunks, D, 1e-6)
        for i in range(0, 16, 4):
            S.wait(*tf[i:i + 4])
            S.items.append(lambda e, i=i: e.dma_start(out[:, i:i + 4, :], h[:, i:i + 4, :])
                           .then_inc(st_sem, 16))
            nstore[0] += 1
        S.wait((st_sem, 16 * nstore[0]))

        blockx = ctx.enter_context(nc.Block())

        @blockx.tensor
        def _(e):
            P.replay(e)

        @blockx.vector
        def _(e):
            V.replay(e)

        @blockx.scalar
        def _(e):
            A.replay(e)

        @blockx.gpsimd
        def _(e):
            G.replay(e)

        @blockx.sync
        def _(e):
            S.replay(e)


def constants():
    c = np.zeros((128, NCST), np.float32)

    def put(name, v):
        o, n = CST_AT[name]
        c[:, o:o + n] = v

    p = np.arange(128)
    put("ident", np.eye(128))
    put("ones", 1.0)
    put("blk", p[:, None] // 64 == p[None] // 64)
    perm = np.zeros((128, 128))
    for m in range(128):
        if m % 64 < 32:
            perm[m + 32, m] = -1.0
        else:
            perm[m - 32, m] = 1.0
    put("perm", perm)
    same = p[:, None] // 32 == p[None] // 32
    incl = same & (p[:, None] <= p[None])
    strict = same & (p[:, None] < p[None])
    put("m3", np.concatenate([incl, strict, incl], 1))
    put("s32", (p[:, None] % 32) < np.arange(32)[None])
    put("bm", same)
    put("bm4", p[:, None] // 32 == np.arange(4)[None])
    zc = np.zeros((128, 256), np.float32)
    zc[:, 128:] = np.where(p[None] <= p[:, None], 0.0, np.finfo(np.float32).min)
    put("zc", zc)
    cm = np.ones((128, 256))
    cm[:, 0:128] = p[:, None] <= p[None]
    put("cm", cm)
    put("kp", np.stack([p < 64, p >= 64], 1))
    fr = np.float32(10000.0) ** (-np.arange(0, 64, 2, dtype=np.float32) / np.float32(64))
    put("ifr", fr.astype(np.float32)[p % 32][:, None])
    put("rm", (np.arange(256) % 32 != 0)[None])
    return c


def tiles(w, M=128):
    K, N = w.shape
    return np.ascontiguousarray(w.reshape(K // 128, 128, N // M, M).transpose(2, 1, 0, 3)).reshape(
        N // M, 128, K // 128 * M)


def layout(x):
    f = {}
    cols = lambda a: np.ascontiguousarray(a.reshape(-1, 128).T)

    def padded(a, o=0):
        v = np.zeros((128, 1), a.dtype)
        v[o:o + a.size, 0] = a.reshape(-1)
        return v

    vec = np.zeros((128, NVEC), np.float32)

    def put(name, v):
        o, n = VEC_AT[name]
        vec[:, o:o + n] = v

    for n in ("attn_norm_w", "mla_q_norm_w", "mla_kv_norm_w", "ssm_out_norm_w", "mla_out_norm_w",
              "ffn_norm_w", "ffn_conv_b", "final_norm_w", "ssm_d", "ssm_b_glu", "norm1_g_2",
              "ssd_conv_b_2", "ssd_norm_g_2", "rwkv_w0_2", "rwkv_a0_2", "rwkv_k_k_2", "rwkv_k_a_2",
              "rwkv_r_k_2", "rwkv_gn_w_2", "rwkv_gn_b_2", "norm2_g_2", "norm_f_g_2"):
        put(n, cols(x[n]))
    for k in range(3):
        put(f"cw{k}", cols(x["ffn_conv_w"][0, k]))
    for k in range(4):
        put(f"dw{k}", cols(x["ssd_conv_w_2"][0, k]))
    mu = x["rwkv_mu_2"][0]
    put("mu_r", cols(mu[0:2048]))
    put("mu_k", cols(mu[2048:4096]))
    put("mu_v", cols(mu[4096:6144]))
    put("mu_wd", padded(mu[6144:6240]))
    put("mu_ad", padded(mu[6240:6336]))
    put("mu_gd", cols(mu[6336:6592]))
    put("dskip", cols(np.repeat(x["ssd_D_2"][0], 64)))
    put("dtb", padded(x["ssd_dt_bias_2"][0], 96))
    put("alog", padded(x["ssd_A_log_2"][0], 96))
    put("lr", x["ssm_lambda_re"][0].reshape(32, 128).T)
    put("li", x["ssm_lambda_im"][0].reshape(32, 128).T)
    put("ldt", np.repeat(x["ssm_log_dt"][0], 64).reshape(32, 128).T)
    f["vec"] = vec
    f["cst"] = constants()
    f["xT"] = np.ascontiguousarray(x["x"][0].T.reshape(16, 128, T).transpose(1, 0, 2))
    f["pos"] = np.ascontiguousarray(x["positions"]).astype(np.int64).view(np.int32).reshape(512)
    for nm, key in (("bre", "ssm_b_re"), ("bim", "ssm_b_im")):
        b = x[key][0].reshape(8, 4, 2, 64, 16)
        v = np.zeros((4, 2, 16, 8, 2, 64), np.float32)
        for g in range(2):
            v[:, g, :, :, g, :] = b[:, :, g].transpose(1, 3, 0, 2)
        f[nm] = v.reshape(128, 8, 128)
    for nm, key in (("cre", "ssm_c_re"), ("cim", "ssm_c_im")):
        c = x[key][0].reshape(32, 2, 16, 64)
        v = np.zeros((2, 64, 32, 2, 16), np.float32)
        for g in range(2):
            v[g, :, :, g, :] = c[:, g].transpose(2, 0, 1)
        f[nm] = v.reshape(128, 32, 32)
    w = x["w_in"][0]
    f["w_in"] = tiles(w[:, 0:1792])
    f["w_kpe"] = tiles(np.concatenate([w[:, 1792:1856], w[:, 1792:1856]], 1))
    uq = x["mla_w_uq"][0].reshape(512, 8, 192)
    f["w_uq"] = tiles(np.concatenate([uq[:, :, 0:128].reshape(512, 1024),
                                      uq[:, :, 128:192].reshape(512, 512)], 1))
    ukv = x["mla_w_ukv"][0].reshape(256, 8, 256)
    f["w_uk"] = tiles(ukv[:, :, 0:128].reshape(256, 1024))
    f["w_uv"] = np.ascontiguousarray(ukv[:, :, 128:256].reshape(2, 128, 1024).transpose(1, 0, 2)).reshape(1, 128, 2048)
    f["w_glu"] = tiles(x["ssm_w_glu"][0])
    f["w_out"] = tiles(x["w_out"][0])
    up = x["ffn_w_up"][0].reshape(2048, 2, 44, 128).transpose(0, 2, 1, 3).reshape(2048, 2 * FF)
    f["w_up"] = tiles(up)
    f["w_down"] = tiles(x["ffn_w_down"][0])
    w = x["w_in_2"][0]
    f["w_z"] = tiles(w[:, 0:2048])
    f["w_xbc"] = tiles(w[:, 2048:5120])
    rkv = w[:, 5152:11296].reshape(2048, 3, 8, 256)
    f["w_krv"] = tiles(np.stack([rkv[:, 1], rkv[:, 0], rkv[:, 2]], 2).reshape(2048, 6144))
    f["w_sm"] = tiles(np.concatenate([w[:, 11296:11392], w[:, 5120:5152], w[:, 11392:11488],
                                      np.zeros((2048, 32), w.dtype), w[:, 11488:11744]], 1))
    f["w2"] = np.ascontiguousarray(x["rwkv_w2_2"][0])
    f["a2"] = np.ascontiguousarray(x["rwkv_a2_2"][0])
    f["w_g2"] = tiles(x["rwkv_g2_2"][0])
    f["w_out2"] = tiles(x["w_out_2"][0])
    gu = np.stack([x["w_gate_2"][0].reshape(2048, 44, 128), x["w_up_2"][0].reshape(2048, 44, 128)], 2)
    f["w_gu"] = tiles(gu.reshape(2048, 2 * FF))
    f["w_down2"] = tiles(x["w_down_2"][0])
    return f


def kernel(**inputs):
    import concourse.bacc as _bacc
    from concourse import mybir as _mybir
    from concourse.bass_utils import run_bass_kernel_spmd as _run

    nc = _bacc.Bacc("TRN2", target_bir_lowering=False, num_devices=1)
    x = {k: np.asarray(v) for k, v in inputs.items()}
    arrays, d = {}, {}
    for name, a in layout(x).items():
        a = np.ascontiguousarray(a)
        arrays[f"in_{name}"] = a
        d[name] = nc.dram_tensor(f"in_{name}", a.shape, _mybir.dt.from_np(a.dtype), kind="ExternalInput").ap()
    for n in ("hsave", "ysave"):
        d[n] = nc.dram_tensor(n, (128, 16, T), _mybir.dt.float32, kind="Internal").ap()
    out = nc.dram_tensor("out_0", (128, 16, T), _mybir.dt.float32, kind="ExternalOutput").ap()
    program(nc, d, out)
    r = _run(nc, [arrays], core_ids=[0])
    got = r.results[0]["out_0"]
    return np.ascontiguousarray(got.transpose(1, 0, 2).reshape(2048, T).T)[None]
```
